# Optimizing a Trainium2 kernel written in Bass

```python
import jax, jax.numpy as jnp
from jax import lax
import numpy as np
import jax
import jax.numpy as jnp

D_MODEL = 1024
BATCH = 1
SEQ = 256
DEPTH = 2

GRID_W = 64
CTX_LEN = 256
D_MIX = D_MODEL
HEAD_DIM = 64
ATT_W = D_MIX // 2
N_HEADS = ATT_W // HEAD_DIM
N_KV_HEADS = 2
GQA_GROUP = N_HEADS // N_KV_HEADS
KV_W = N_KV_HEADS * HEAD_DIM
CONV_W = D_MIX // 4
FOUR_W = D_MIX - ATT_W - CONV_W
FOUR_HEADS = 4
FOUR_HEAD_DIM = FOUR_W // FOUR_HEADS
CONV_K = 31
WINDOW = 128
BLOCK = 128
ROPE_BASE = 10000.0
EPS = 1e-6
NEG_INF = -1e30
SPLITS = (ATT_W, KV_W, KV_W, ATT_W, CONV_W, CONV_W, CONV_W, FOUR_W, FOUR_W)
IN_W = ATT_W + 2 * KV_W + ATT_W + 3 * CONV_W + 2 * FOUR_W


def rms_norm(x, g):
    xf = x.astype(jnp.float32)
    y = xf * lax.rsqrt(jnp.mean(xf * xf, axis=-1, keepdims=True) + EPS)
    return (y * g.astype(jnp.float32)).astype(x.dtype)

def layer_norm(x, g, b):
    xf = x.astype(jnp.float32)
    mu = jnp.mean(xf, axis=-1, keepdims=True)
    var = jnp.mean(jnp.square(xf - mu), axis=-1, keepdims=True)
    y = (xf - mu) * lax.rsqrt(var + EPS)
    return (y * g.astype(jnp.float32) + b.astype(jnp.float32)).astype(x.dtype)

def split_cols(p):
    outs = []
    off = 0
    for w in SPLITS:
        outs.append(p[..., off:off + w])
        off += w
    return outs

def rope_axis(x, pos):
    half = x.shape[-1] // 2
    freqs = ROPE_BASE ** (-jnp.arange(half, dtype=jnp.float32) / half)
    ang = pos[:, None] * freqs[None, :]
    cos = jnp.cos(ang)[:, None, :].astype(x.dtype)
    sin = jnp.sin(ang)[:, None, :].astype(x.dtype)
    x1, x2 = x[..., :half], x[..., half:]
    return jnp.concatenate([x1 * cos - x2 * sin, x1 * sin + x2 * cos], axis=-1)

def rope_2d(x, row, col):
    h = x.shape[-1] // 2
    return jnp.concatenate([rope_axis(x[..., :h], row), rope_axis(x[..., h:], col)], axis=-1)

def windowed_attention(q, k, v, kc, vc, sink):
    bn, s = q.shape[0], q.shape[1]
    nb = s // BLOCK
    n_ctx = kc.shape[1]
    scale = HEAD_DIM ** -0.5
    qb = q.reshape(bn, nb, BLOCK, N_KV_HEADS, GQA_GROUP, HEAD_DIM)
    pad = ((0, 0), (BLOCK, BLOCK), (0, 0), (0, 0))
    kp = jnp.pad(k, pad).reshape(bn, nb + 2, BLOCK, N_KV_HEADS, HEAD_DIM)
    vp = jnp.pad(v, pad).reshape(bn, nb + 2, BLOCK, N_KV_HEADS, HEAD_DIM)
    kw = jnp.concatenate([kp[:, :-2], kp[:, 1:-1], kp[:, 2:]], axis=2)
    vw = jnp.concatenate([vp[:, :-2], vp[:, 1:-1], vp[:, 2:]], axis=2)
    s_loc = jnp.einsum('bnqhgd,bnkhd->bnhgqk', qb, kw).astype(jnp.float32) * scale
    q_rel = jnp.arange(BLOCK) + BLOCK
    k_rel = jnp.arange(3 * BLOCK)
    band = jnp.abs(q_rel[:, None] - k_rel[None, :]) <= WINDOW
    k_abs = jnp.arange(nb)[:, None] * BLOCK - BLOCK + k_rel[None, :]
    valid = (k_abs >= 0) & (k_abs < s)
    mask = band[None, :, :] & valid[:, None, :]
    s_loc = jnp.where(mask[None, :, None, None], s_loc, NEG_INF)
    s_ctx = jnp.einsum('bnqhgd,blhd->bnhgql', qb, kc).astype(jnp.float32) * scale
    s_sink = jnp.broadcast_to(
        sink.astype(jnp.float32).reshape(1, 1, N_KV_HEADS, GQA_GROUP, 1, 1),
        s_loc.shape[:-1] + (1,))
    p = jax.nn.softmax(jnp.concatenate([s_loc, s_ctx, s_sink], axis=-1), axis=-1)
    p_loc = p[..., :3 * BLOCK].astype(v.dtype)
    p_ctx = p[..., 3 * BLOCK:3 * BLOCK + n_ctx].astype(v.dtype)
    o = (jnp.einsum('bnhgqk,bnkhd->bnqhgd', p_loc, vw)
         + jnp.einsum('bnhgql,blhd->bnqhgd', p_ctx, vc))
    return o.reshape(bn, s, ATT_W)

def context_attention(q, k, v, sink):
    bn, n_ctx = q.shape[0], q.shape[1]
    scale = HEAD_DIM ** -0.5
    qh = q.reshape(bn, n_ctx, N_KV_HEADS, GQA_GROUP, HEAD_DIM)
    sc = jnp.einsum('blhgd,bmhd->bhglm', qh, k).astype(jnp.float32) * scale
    s_sink = jnp.broadcast_to(
        sink.astype(jnp.float32).reshape(1, N_KV_HEADS, GQA_GROUP, 1, 1), sc.shape[:-1] + (1,))
    p = jax.nn.softmax(jnp.concatenate([sc, s_sink], axis=-1), axis=-1)
    o = jnp.einsum('bhglm,bmhd->blhgd', p[..., :n_ctx].astype(v.dtype), v)
    return o.reshape(bn, n_ctx, ATT_W)

def conformer_conv(a, b_glu, conv_w, conv_b, ln_g, ln_b):
    u = a * jax.nn.sigmoid(b_glu)
    y = lax.conv_general_dilated(
        u, conv_w[:, None, :], window_strides=(1,),
        padding=[(CONV_K // 2, CONV_K // 2)],
        dimension_numbers=('NWC', 'WIO', 'NWC'),
        feature_group_count=CONV_W) + conv_b
    return jax.nn.silu(layer_norm(y, ln_g, ln_b))

def fourier_mix(u, w_four, b_four):
    bn, n = u.shape[0], u.shape[1]
    uh = u.reshape(bn, n, FOUR_HEADS, FOUR_HEAD_DIM).astype(jnp.float32)
    f = jnp.fft.fftn(uh, axes=(1, 3), norm='ortho').real
    f = f.reshape(bn, n, FOUR_W).astype(u.dtype)
    return f @ w_four + b_four

def mixer_out(attn, parts, conv_w, conv_b, ln_g, ln_b, w_four, b_four, w_out):
    _, _, _, g_att, c_a, c_b, g_conv, f_u, g_four = parts
    y_conv = conformer_conv(c_a, c_b, conv_w, conv_b, ln_g, ln_b)
    y_four = fourier_mix(f_u, w_four, b_four)
    y = jnp.concatenate([attn * jax.nn.silu(g_att),
                         y_conv * jax.nn.silu(g_conv),
                         y_four * jax.nn.silu(g_four)], axis=-1)
    return y @ w_out

def first_inputs(seed: int = 0) -> dict:
    key = jax.random.key(seed)
    ks = jax.random.split(key, 20)
    f32 = jnp.float32
    nrm = lambda k, shp, s: jax.random.normal(k, shp, f32) * s
    return {
        'x': nrm(ks[0], (BATCH, SEQ, D_MODEL), 1.0),
        'c': nrm(ks[1], (BATCH, D_MODEL), 1.0),
        'ctx': nrm(ks[2], (BATCH, CTX_LEN, D_MODEL), 1.0),
        'c_ctx': nrm(ks[3], (D_MODEL,), 1.0),
        'w_ada': nrm(ks[4], (DEPTH, D_MODEL, 3 * D_MODEL), 0.5 * D_MODEL ** -0.5),
        'b_ada': nrm(ks[5], (DEPTH, 3 * D_MODEL), 0.02),
        'norm_g': 1.0 + nrm(ks[6], (DEPTH, D_MODEL), 0.02),
        'w_in': nrm(ks[7], (DEPTH, D_MODEL, IN_W), D_MODEL ** -0.5),
        'attn_sink': nrm(ks[8], (DEPTH, N_HEADS), 0.5),
        'conv_w': nrm(ks[9], (DEPTH, CONV_K, CONV_W), CONV_K ** -0.5),
        'conv_b': nrm(ks[10], (DEPTH, CONV_W), 0.02),
        'conv_ln_g': 1.0 + nrm(ks[11], (DEPTH, CONV_W), 0.02),
        'conv_ln_b': nrm(ks[12], (DEPTH, CONV_W), 0.02),
        'w_four': nrm(ks[13], (DEPTH, FOUR_W, FOUR_W), FOUR_W ** -0.5),
        'b_four': nrm(ks[14], (DEPTH, FOUR_W), 0.02),
        'w_out': nrm(ks[15], (DEPTH, D_MIX, D_MODEL), D_MIX ** -0.5),
        'final_g': 1.0 + nrm(ks[16], (D_MODEL,), 0.02),
    }

def first_block(x, c, ctx, c_ctx, w_ada, b_ada, norm_g, w_in, attn_sink, conv_w, conv_b,
              conv_ln_g, conv_ln_b, w_four, b_four, w_out, final_g):
    bn, s, _ = x.shape
    n_ctx = ctx.shape[1]
    ROWS = s // GRID_W
    row_pos = jnp.repeat(jnp.arange(ROWS, dtype=jnp.float32), GRID_W)
    col_pos = jnp.tile(jnp.arange(GRID_W, dtype=jnp.float32), ROWS)
    sc = jax.nn.silu(c)
    scc = jax.nn.silu(c_ctx)
    h_ctx = ctx
    for l in range(DEPTH):
        shift, scale, gate = jnp.split(sc @ w_ada[l] + b_ada[l], 3, axis=-1)
        shift_c, scale_c, gate_c = jnp.split(scc @ w_ada[l] + b_ada[l], 3, axis=-1)
        hc = rms_norm(h_ctx, norm_g[l]) * (1.0 + scale_c) + shift_c
        if l < DEPTH - 1:
            pc = split_cols(hc @ w_in[l])
            kc_raw, vc_raw = pc[1], pc[2]
        else:
            kv = hc @ w_in[l][:, ATT_W:ATT_W + 2 * KV_W]
            kc_raw, vc_raw = kv[..., :KV_W], kv[..., KV_W:]
        kc = kc_raw.reshape(bn, n_ctx, N_KV_HEADS, HEAD_DIM)
        vc = vc_raw.reshape(bn, n_ctx, N_KV_HEADS, HEAD_DIM)

        hx = rms_norm(x, norm_g[l]) * (1.0 + scale[:, None, :]) + shift[:, None, :]
        px = split_cols(hx @ w_in[l])
        q = rope_2d(px[0].reshape(bn, s, N_HEADS, HEAD_DIM), row_pos, col_pos)
        k = rope_2d(px[1].reshape(bn, s, N_KV_HEADS, HEAD_DIM), row_pos, col_pos)
        v = px[2].reshape(bn, s, N_KV_HEADS, HEAD_DIM)
        attn = windowed_attention(q, k, v, kc, vc, attn_sink[l])
        y = mixer_out(attn, px, conv_w[l], conv_b[l], conv_ln_g[l], conv_ln_b[l],
                      w_four[l], b_four[l], w_out[l])

        if l < DEPTH - 1:
            qc = pc[0].reshape(bn, n_ctx, N_HEADS, HEAD_DIM)
            attn_c = context_attention(qc, kc, vc, attn_sink[l])
            yc = mixer_out(attn_c, pc, conv_w[l], conv_b[l], conv_ln_g[l], conv_ln_b[l],
                           w_four[l], b_four[l], w_out[l])
            h_ctx = h_ctx + gate_c * yc
        x = x + gate[:, None, :] * y
    return rms_norm(x, final_g)


DEPTH_2 = 1

ROPE_THETA = 10000.0
RMS_EPS = 1e-6
Q_BLOCK = 128

A_HEADS = 8
A_KV_HEADS = 2
IDX_HEADS = 4
IDX_DIM = 64
TOPK_MAX = 256

B_PATTERNS = ((128, 1), (512, 4), (2048, 16))
B_N_GROUPS = 3
B_HEADS = 8

MEM_LEN = 256
M_HEADS = 4
M_HEAD_DIM = 128

BRANCH_WIDTH = 512
N_BRANCHES = 3

MOE_GROUPS = 4
EXPERTS_PER_GROUP = 4
N_EXPERTS = 16
MOE_TOPK = 2
EXPERT_HIDDEN = 512

IN_SPLITS = (512, 128, 128, 256, 64, 4, 1536, 1536, 1536, 512)
IN_WIDTH = 6212


def rmsnorm(x, g):
    xf = x.astype(jnp.float32)
    y = xf * lax.rsqrt(jnp.mean(xf * xf, axis=-1, keepdims=True) + RMS_EPS)
    return (y * g.astype(jnp.float32)).astype(x.dtype)

def rope(x):
    s, dh = x.shape[1], x.shape[-1]
    half = dh // 2
    inv = ROPE_THETA ** (-jnp.arange(half, dtype=jnp.float32) / half)
    ang = jnp.arange(s, dtype=jnp.float32)[:, None] * inv[None, :]
    cos = jnp.cos(ang)[None, :, None, :]
    sin = jnp.sin(ang)[None, :, None, :]
    xf = x.astype(jnp.float32)
    x1, x2 = xf[..., :half], xf[..., half:]
    return jnp.concatenate([x1 * cos - x2 * sin, x2 * cos + x1 * sin], axis=-1).astype(x.dtype)

def split_cols_2(a, sizes):
    out, off = [], 0
    for n in sizes:
        out.append(a[..., off:off + n])
        off += n
    return out

def sweep_query_blocks(fn, seq_len):
    out = lax.map(fn, jnp.arange(seq_len // Q_BLOCK))
    nb, b = out.shape[0], out.shape[1]
    return jnp.moveaxis(out, 0, 1).reshape(b, nb * Q_BLOCK, *out.shape[3:])

def dsa_attention(q, k, v, q_idx, k_idx, w_idx):
    b, s, h, dh = q.shape
    kvh = k.shape[2]
    g = h // kvh
    topk = min(TOPK_MAX, s // 4)
    key_pos = jnp.arange(s)
    local = jnp.arange(Q_BLOCK)
    k_idx_f = k_idx.astype(jnp.float32)

    def block(i):
        q0 = i * Q_BLOCK
        qpos = q0 + local
        qi = lax.dynamic_slice_in_dim(q_idx, q0, Q_BLOCK, axis=1).astype(jnp.float32)
        wi = lax.dynamic_slice_in_dim(w_idx, q0, Q_BLOCK, axis=1).astype(jnp.float32)
        dots = jnp.einsum('bqhd,bsd->bqhs', qi, k_idx_f) * (IDX_DIM ** -0.5)
        score = jnp.einsum('bqhs,bqh->bqs', jax.nn.relu(dots), wi) * (IDX_HEADS ** -0.5)
        causal = key_pos[None, :] <= qpos[:, None]
        score = jnp.where(causal[None], score, -jnp.inf)
        _, sel = lax.top_k(score, topk)
        valid = sel <= qpos[None, :, None]
        ks = jax.vmap(lambda kk, ii: kk[ii])(k, sel)
        vs = jax.vmap(lambda vv, ii: vv[ii])(v, sel)
        qb = lax.dynamic_slice_in_dim(q, q0, Q_BLOCK, axis=1).reshape(b, Q_BLOCK, kvh, g, dh)
        logits = jnp.einsum('bqkgd,bqjkd->bqkgj', qb, ks).astype(jnp.float32) * (dh ** -0.5)
        logits = jnp.where(valid[:, :, None, None, :], logits, -jnp.inf)
        p = jax.nn.softmax(logits, axis=-1)
        o = jnp.einsum('bqkgj,bqjkd->bqkgd', p.astype(vs.dtype), vs)
        return o.reshape(b, Q_BLOCK, h * dh)

    return sweep_query_blocks(block, s)

def dilated_attention(q, k, v):
    b, s, ng, h, dh = q.shape
    local = jnp.arange(Q_BLOCK)
    qs = [q[:, :, gi] for gi in range(ng)]
    kp = [jnp.pad(k[:, :, gi], ((0, 0), (w, 0), (0, 0), (0, 0))) for gi, (w, _) in enumerate(B_PATTERNS)]
    vp = [jnp.pad(v[:, :, gi], ((0, 0), (w, 0), (0, 0), (0, 0))) for gi, (w, _) in enumerate(B_PATTERNS)]

    def block(i):
        q0 = i * Q_BLOCK
        outs, lses = [], []
        for gi, (window, dil) in enumerate(B_PATTERNS):
            steps = jnp.arange(window // dil + 1)
            back = local[:, None] - steps[None, :] * dil
            valid = (q0 + back) >= 0
            rel = window + back
            ks = lax.dynamic_slice_in_dim(kp[gi], q0, window + Q_BLOCK, axis=1)[:, rel]
            vs = lax.dynamic_slice_in_dim(vp[gi], q0, window + Q_BLOCK, axis=1)[:, rel]
            qg = lax.dynamic_slice_in_dim(qs[gi], q0, Q_BLOCK, axis=1)
            logits = jnp.einsum('bqhd,bqjhd->bqhj', qg, ks).astype(jnp.float32) * (dh ** -0.5)
            logits = jnp.where(valid[None, :, None, :], logits, -jnp.inf)
            lse = jax.nn.logsumexp(logits, axis=-1)
            p = jnp.exp(logits - lse[..., None])
            outs.append(jnp.einsum('bqhj,bqjhd->bqhd', p.astype(vs.dtype), vs))
            lses.append(lse)
        alpha = jax.nn.softmax(jnp.stack(lses, axis=2), axis=2)
        o = jnp.einsum('bqgh,bqghd->bqhd', alpha.astype(outs[0].dtype), jnp.stack(outs, axis=2))
        return o.reshape(b, Q_BLOCK, h * dh)

    return sweep_query_blocks(block, s)

def memory_attention(qm, mem_n, w_mem_kv):
    b, m, _ = mem_n.shape
    km, vm = split_cols_2(mem_n @ w_mem_kv, (M_HEADS * M_HEAD_DIM, M_HEADS * M_HEAD_DIM))
    km = km.reshape(b, m, M_HEADS, M_HEAD_DIM)
    vm = vm.reshape(b, m, M_HEADS, M_HEAD_DIM)
    logits = jnp.einsum('bshd,bmhd->bhsm', qm, km).astype(jnp.float32) * (M_HEAD_DIM ** -0.5)
    p = jax.nn.softmax(logits, axis=-1)
    o = jnp.einsum('bhsm,bmhd->bshd', p.astype(vm.dtype), vm)
    return o.reshape(b, qm.shape[1], M_HEADS * M_HEAD_DIM)

def hier_moe(xn, w_group, b_group, w_sub, b_sub, w1, w3, w2):
    b, s, d = xn.shape
    t = xn.reshape(b * s, d)
    gl = (t @ w_group).astype(jnp.float32) + b_group.astype(jnp.float32)
    gp = jax.nn.softmax(gl, axis=-1)
    g_w, g_sel = lax.top_k(gp, 1)
    sl = jnp.einsum('td,gde->tge', t, w_sub).astype(jnp.float32) + b_sub.astype(jnp.float32)
    sl = jnp.take_along_axis(sl, g_sel[:, :, None], axis=1)[:, 0]
    sp = jax.nn.softmax(sl, axis=-1)
    top_p, top_e = lax.top_k(sp, MOE_TOPK)
    top_p = top_p / jnp.sum(top_p, axis=-1, keepdims=True)
    expert_id = g_sel * EXPERTS_PER_GROUP + top_e
    combine = jnp.einsum('tk,tke->te', g_w * top_p, jax.nn.one_hot(expert_id, N_EXPERTS, dtype=jnp.float32))
    out = jnp.zeros((b * s, d), jnp.float32)
    for e in range(N_EXPERTS):
        hid = jax.nn.silu(t @ w1[e]) * (t @ w3[e])
        out = out + combine[:, e:e + 1] * (hid @ w2[e]).astype(jnp.float32)
    return out.astype(xn.dtype).reshape(b, s, d)

def second_inputs(seed: int = 0) -> dict:
    key = jax.random.key(seed)
    ks = jax.random.split(key, 19)
    f32 = jnp.float32
    L, D = DEPTH_2, D_MODEL

    def dense(k, shape, fan_in):
        return jax.random.normal(k, shape, f32) * (fan_in ** -0.5)

    def gain(k, shape):
        return 1.0 + 0.02 * jax.random.normal(k, shape, f32)

    def small(k, shape, scale):
        return scale * jax.random.normal(k, shape, f32)

    return {
        'x': jax.random.normal(ks[0], (BATCH, SEQ, D), f32),
        'mem': jax.random.normal(ks[1], (BATCH, MEM_LEN, D), f32),
        'g_mix': gain(ks[2], (L, D)),
        'g_mem': gain(ks[3], (L, D)),
        'w_in': dense(ks[4], (L, D, IN_WIDTH), D),
        'w_mem_kv': dense(ks[5], (L, D, 2 * M_HEADS * M_HEAD_DIM), D),
        'w_gate': dense(ks[6], (L, D, N_BRANCHES * D), D),
        'b_gate': small(ks[7], (L, N_BRANCHES * D), 0.1),
        'w_branch': dense(ks[8], (L, N_BRANCHES, BRANCH_WIDTH, D), BRANCH_WIDTH),
        'w_out': dense(ks[9], (L, D, D), D),
        'g_ffn': gain(ks[10], (L, D)),
        'w_group': dense(ks[11], (L, D, MOE_GROUPS), D),
        'b_group': small(ks[12], (L, MOE_GROUPS), 0.01),
        'w_sub': dense(ks[13], (L, MOE_GROUPS, D, EXPERTS_PER_GROUP), D),
        'b_sub': small(ks[14], (L, MOE_GROUPS, EXPERTS_PER_GROUP), 0.01),
        'w1': dense(ks[15], (L, N_EXPERTS, D, EXPERT_HIDDEN), D),
        'w3': dense(ks[16], (L, N_EXPERTS, D, EXPERT_HIDDEN), D),
        'w2': dense(ks[17], (L, N_EXPERTS, EXPERT_HIDDEN, D), EXPERT_HIDDEN),
        'g_final': gain(ks[18], (D,)),
    }

def second_block(x, mem, g_mix, g_mem, w_in, w_mem_kv, w_gate, b_gate, w_branch, w_out, g_ffn,
              w_group, b_group, w_sub, b_sub, w1, w3, w2, g_final):
    b, s, d = x.shape
    h = x
    for l in range(DEPTH_2):
        n = rmsnorm(h, g_mix[l])
        aq, ak, av, iq, ik, iw, bq, bk, bv, mq = split_cols_2(n @ w_in[l], IN_SPLITS)
        aq = rope(aq.reshape(b, s, A_HEADS, HEAD_DIM))
        ak = rope(ak.reshape(b, s, A_KV_HEADS, HEAD_DIM))
        av = av.reshape(b, s, A_KV_HEADS, HEAD_DIM)
        iq = rope(iq.reshape(b, s, IDX_HEADS, IDX_DIM))
        ik = rope(ik.reshape(b, s, 1, IDX_DIM))[:, :, 0]
        y_a = dsa_attention(aq, ak, av, iq, ik, iw)
        bq = rope(bq.reshape(b, s, B_N_GROUPS * B_HEADS, HEAD_DIM)).reshape(b, s, B_N_GROUPS, B_HEADS, HEAD_DIM)
        bk = rope(bk.reshape(b, s, B_N_GROUPS * B_HEADS, HEAD_DIM)).reshape(b, s, B_N_GROUPS, B_HEADS, HEAD_DIM)
        bv = bv.reshape(b, s, B_N_GROUPS, B_HEADS, HEAD_DIM)
        y_b = dilated_attention(bq, bk, bv)
        y_m = memory_attention(mq.reshape(b, s, M_HEADS, M_HEAD_DIM), rmsnorm(mem, g_mem[l]), w_mem_kv[l])
        gates = jax.nn.sigmoid((n @ w_gate[l] + b_gate[l]).astype(jnp.float32)).astype(n.dtype)
        gates = gates.reshape(b, s, N_BRANCHES, d)
        merged = (gates[:, :, 0] * (y_a @ w_branch[l, 0])
                  + gates[:, :, 1] * (y_b @ w_branch[l, 1])
                  + gates[:, :, 2] * (y_m @ w_branch[l, 2]))
        h = h + merged @ w_out[l]
        h = h + hier_moe(rmsnorm(h, g_ffn[l]), w_group[l], b_group[l], w_sub[l], b_sub[l], w1[l], w3[l], w2[l])
    return rmsnorm(h, g_final)


def setup_inputs(seed=0):
    out = dict(first_inputs(seed))
    for name, value in second_inputs(seed + 1).items():
        if name != "x":
            out[name + "_2"] = value
    return out


def reference(
    x, c, ctx, c_ctx, w_ada, b_ada, norm_g, w_in, attn_sink, conv_w, conv_b, conv_ln_g,
    conv_ln_b, w_four, b_four, w_out, final_g, mem_2, g_mix_2, g_mem_2, w_in_2, w_mem_kv_2,
    w_gate_2, b_gate_2, w_branch_2, w_out_2, g_ffn_2, w_group_2, b_group_2, w_sub_2, b_sub_2,
    w1_2, w3_2, w2_2, g_final_2,
):
    x = first_block(
        x, c, ctx, c_ctx, w_ada, b_ada, norm_g, w_in, attn_sink, conv_w, conv_b, conv_ln_g,
        conv_ln_b, w_four, b_four, w_out, final_g,
    )
    return second_block(
        x, mem_2, g_mix_2, g_mem_2, w_in_2, w_mem_kv_2, w_gate_2, b_gate_2, w_branch_2, w_out_2,
        g_ffn_2, w_group_2, b_group_2, w_sub_2, b_sub_2, w1_2, w3_2, w2_2, g_final_2,
    )


_drawn_inputs = setup_inputs


def setup_inputs(seed=0):
    import zlib

    import numpy as np

    out = dict(_drawn_inputs(seed))
    spreads = {}
    factors = {'attn_sink': 8.0,
     'conv_b': 3.333,
     'conv_ln_g': 4.75,
     'conv_ln_b': 3.989,
     'b_four': 4.503,
     'g_mem_2': 8.0,
     'b_gate_2': 2.725,
     'b_group_2': 29.84,
     'b_sub_2': 43.792,
     'g_final_2': 7.774,
     'g_ffn_2': 6.942}
    for name, (base, spread) in spreads.items():
        noise = np.random.default_rng([zlib.crc32(name.encode()), seed]).standard_normal(out[name].shape)
        drawn = base * np.exp(spread * noise) if base else spread * noise
        out[name] = jnp.asarray(drawn.astype(out[name].dtype))
    for name, factor in factors.items():
        out[name] = (out[name] * factor).astype(out[name].dtype)
    return out
```

```python
from contextlib import ExitStack

import numpy as np
import concourse.bass as bass
from concourse import mybir

ALU = mybir.AluOpType
ACT = mybir.ActivationFunctionType
AX = mybir.AxisListType
F32 = mybir.dt.float32

P = 128
D = 1024
KT = D // P
SEQ = 256
TT = SEQ // P
DEPTH = 2
HEADS, KVH, HD = 8, 2, 64
CONV_W, CONV_K = 256, 31
PAD = CONV_K // 2
N_EXP, EPG, TOPK = 16, 4, 64
NEG = -1e30
GONE = -3e38
EPS = 1e-6

CB, CA, KK, VV, QQ, FU, GA, GC, GF = 0, 2, 4, 5, 6, 10, 12, 16, 18
IN1 = 20
AQ, AK, AV, IQ, IK, BQ, BK, BV, MQ = 0, 4, 5, 6, 8, 9, 21, 33, 45
IN2 = 49
MK, MV = IN2, IN2 + 4
AT = {AQ + i: i for i in range(5)} | {IQ + i: 5 + i for i in range(3)} | {BQ + i: 8 + i for i in range(24)} \
    | {MQ + i: 32 + i for i in range(4)} | {MK + i: 36 + i for i in range(4)}
ADA = 24
N_HEAD_BLOCKS = DEPTH * (ADA + IN1 + KT) + IN2 + 8 + ADA + 12 + KT
PADDED = N_HEAD_BLOCKS + N_HEAD_BLOCKS % 2
UNIT = 2
SLOTS = 6
EXP_UNITS = 6
N_UNITS = PADDED // UNIT + N_EXP * EXP_UNITS

COL = {}
_n = 0
for _name, _w in [("c", 16), ("b_ada0", 24), ("b_ada1", 24), ("norm_g0", 8), ("norm_g1", 8), ("final_g", 8),
                  ("g_mix", 8), ("g_mem", 8), ("g_ffn", 8), ("g_final", 8), ("b_gate", 24),
                  ("conv_w0", 62), ("conv_w1", 62), ("conv_b0", 2), ("conv_b1", 2), ("ln_g0", 2), ("ln_g1", 2),
                  ("ln_b0", 2), ("ln_b1", 2), ("b_four0", 2), ("b_four1", 2), ("sink", 16), ("b_route", 20),
                  ("eps", 1)]:
    COL[_name] = (_n, _n + _w)
    _n += _w
N_COL = _n

C0 = {}
_n = 0
for _name, _w in [("ident", 128), ("ones_d", 128), ("ones_c", 128), ("tri", 256)]:
    C0[_name] = (_n, _n + _w)
    _n += _w
N_C0 = _n
C1 = {}
_n = 0
for _name, _w in [("rot", 128), ("cos", 256), ("sin", 256), ("dft0", 512), ("dft1", 512), ("bc", 128), ("bs", 128),
                  ("band0", 512), ("band1", 512)]:
    C1[_name] = (_n, _n + _w)
    _n += _w
N_C1 = _n
C2 = {}
_n = 0
for _name, _w in [("rot", 128), ("cos", 256), ("sin", 256), ("dil0", 384), ("dil1", 768), ("zero", 256),
                  ("causal0", 128), ("causal1", 256)]:
    C2[_name] = (_n, _n + _w)
    _n += _w
N_C2 = _n


def constants():
    f = np.float32
    c0, c1, c2 = np.zeros((P, N_C0), f), np.zeros((P, N_C1), f), np.zeros((P, N_C2), f)
    i = np.arange(P)
    c0[:, slice(*C0["ident"])] = np.eye(P)
    c0[:, slice(*C0["ones_d"])] = 1.0 / D
    c0[:, slice(*C0["ones_c"])] = 1.0 / CONV_W
    c0[:, slice(*C0["tri"])] = np.concatenate([(i[:, None] < i[None, :]), np.ones((P, P))], 1)
    tok = np.arange(SEQ)

    def rope(c, table, half, pos_of):
        d = i % (2 * half)
        freq = f(10000.0) ** (-np.arange(half, dtype=f) / f(half))
        ang = (pos_of[i // (2 * half) % 2][:, tok].astype(f) * freq[d % half][:, None]).astype(f)
        c[:, slice(*table["cos"])] = np.cos(ang)
        c[:, slice(*table["sin"])] = np.sin(ang)
        rot = np.zeros((P, P), f)
        for m in range(P):
            if m % (2 * half) < half:
                rot[m + half, m] = -1.0
            else:
                rot[m - half, m] = 1.0
        c[:, slice(*table["rot"])] = rot

    rope(c1, C1, 16, np.stack([tok // 64, tok % 64]))
    rope(c2, C2, 32, np.stack([tok, tok]))
    ang = 2 * np.pi * ((tok[:, None] * tok[None, :]) % SEQ) / SEQ
    cs = np.concatenate([np.cos(ang), np.sin(ang)], 1)
    c1[:, slice(*C1["dft0"])] = cs[:P]
    c1[:, slice(*C1["dft1"])] = cs[P:]
    a64 = 2 * np.pi * ((i[:, None] * i[None, :]) % HD) / HD
    same = (i[:, None] // HD) == (i[None, :] // HD)
    norm = 1.0 / np.sqrt(SEQ * HD)
    c1[:, slice(*C1["bc"])] = np.where(same, np.cos(a64), 0) * norm
    c1[:, slice(*C1["bs"])] = np.where(same, -np.sin(a64), 0) * norm
    for t in range(TT):
        q = t * P + i[:, None]
        band = np.where(np.abs(q - tok[None, :]) <= 128, 0.0, NEG)
        c1[:, slice(*C1[f"band{t}"])] = np.concatenate([band, np.zeros((P, SEQ))], 1)
        ks = np.arange(P * (t + 1))[None, :]
        c2[:, slice(*C2[f"dil{t}"])] = np.concatenate(
            [np.where((ks <= q) & ((q - ks) % dil == 0) & (q - ks <= win), 0.0, NEG)
             for win, dil in ((128, 1), (512, 4), (2048, 16))], 1)
        c2[:, slice(*C2[f"causal{t}"])] = np.where(ks <= q, 0.0, NEG)
    return c0, c1, c2



def build(nc, w_stream, x_in, mem_in, cols_in, wfour_in, wsmall_in, c0_in, c1_in, c2_in, out):
    ctx = ExitStack()
    with ctx:
        def sb(name, shape):
            return ctx.enter_context(nc.sbuf_tensor(name, shape, F32))

        def sem(name):
            return ctx.enter_context(nc.semaphore(name))

        ring = sb("ring", [P, SLOTS, UNIT, KT * P])
        X = sb("X", [P, 2, KT, SEQ])
        H = sb("H", [P, 2, KT, SEQ])
        PR = sb("PR", [P, 2 * IN1, SEQ])
        UN = sb("UN", [P, 4352])
        Y = sb("Y", [P, 16, SEQ])
        RS = sb("RS", [P, 512])
        RI = sb("RI", [P, 512])
        MOD = sb("MOD", [P, DEPTH, ADA, 2])
        GS = sb("GS", [P, KT, 2])
        SC = sb("SC", [P, KT, 2])
        cols = sb("cols", [P, N_COL])
        SK = sb("SK", [P, DEPTH * HEADS])
        ST = sb("ST", [P, 4, 4])
        O = sb("O", [P, 4, 512])
        S = sb("S", [P, 2, 772])
        PT = sb("PT", [P, 2, 768])
        SQ = sb("SQ", [P, 2, 512])
        RT = sb("RT", [P, 2, SEQ])
        c0 = sb("c0", [P, N_C0])
        cb = sb("cb", [P, N_C1])
        wfour = sb("wfour", [P, DEPTH, 2, 256])
        wsmall = sb("wsmall", [P, KT, 24])
        IW = sb("IW", [P, TT, 8])
        M8 = sb("M8", [P, TT, 8])
        RO = sb("RO", [P, TT, 96])
        CM = sb("CM", [P, TT, N_EXP])

        P1 = PR.rearrange("p (t s) n -> p t s n", s=2)
        YB = Y.rearrange("p (t s) n -> p t s n", s=2)
        U = UN[:, 0:1144].rearrange("p (t s n) -> p t s n", t=2, s=2)
        CV = UN[:, 1144:2168].rearrange("p (t s n) -> p t s n", t=2, s=2)
        FT = UN[:, 2168:3192].rearrange("p (t n) -> p t n", t=4)
        VT = UN[:, 3192:3704].rearrange("p (t n) -> p t n", t=4)
        H1 = H.rearrange("p s k n -> p (s k n)")
        CS = H1[:, 0:2048].rearrange("p (f s n) -> p f s n", f=2, s=2)
        FF = H1[:, 2048:3072].rearrange("p (f s n) -> p f s n", f=2, s=2)
        BVT = UN[:, 0:3072].rearrange("p (t n) -> p t n", t=TT)
        AVT = UN[:, 3072:3328].rearrange("p (t n) -> p t n", t=TT)
        MVT = UN[:, 3328:4352].rearrange("p (t n) -> p t n", t=TT)
        X1 = X[:, 1, :, :].rearrange("p k n -> p (k n)")
        DS = X1[:, 0:512].rearrange("p (t n) -> p t n", t=TT)
        MA = X1[:, 512:1024].rearrange("p (t n) -> p t n", t=TT)
        RL = X1[:, 1024:2048].rearrange("p (h n) -> p h n", h=4)
        E1 = PR.rearrange("p t n -> p (t n)")
        SG = E1[:, 0:512].rearrange("p (b n) -> p b n", b=2)
        HI = E1[:, 512:1536].rearrange("p (k n) -> p k n", k=4)
        CW = E1[:, 1536:1792]
        DG = E1[:, 1792:2048].rearrange("p (t n) -> p t n", t=TT)

        lin = [ctx.enter_context(nc.psum_tensor(f"lin{i}", [P, 512], F32)) for i in range(2)]
        aux = [ctx.enter_context(nc.psum_tensor(f"aux{i}", [P, 512], F32)) for i in range(2)]
        sc = ctx.enter_context(nc.psum_tensor("sc", [P, 2, 1024], F32))

        unit_in = [sem(f"unit_in{i}") for i in range(SLOTS)]
        unit_free = sem("unit_free")
        cols_in_s, x_in_s, consts_in, mem_in_s, c2_in_s, out_s = (
            sem(n) for n in ("cols_in", "x_in", "consts_in", "mem_in", "c2_in", "out_stored"))
        lin_ready, lin_taken = sem("lin_ready"), sem("lin_taken")
        aux_ready, aux_taken = sem("aux_ready"), sem("aux_taken")
        scores_ready, scores_taken = sem("scores_ready"), sem("scores_taken")
        bias_ready, probs_ready, sink_in = (sem(n) for n in ("bias_ready", "probs_ready", "sink_in"))
        silu_c, sinks_ready, pads_ready = sem("silu_c"), sem("sinks_ready"), sem("pads_ready")
        sq_ready, sq_used = sem("sq_ready"), sem("sq_used")
        dve_step = sem("dve_step")
        roped, conv_done, conv_sq, conv_norm, conv_act = (
            sem(n) for n in ("roped", "conv_done", "conv_sq", "conv_norm", "conv_act"))
        idx_mask, merged, gains_ready = sem("idx_mask"), sem("merged"), sem("gains_ready")
        NORMS = ["l0", "l1", "fin1", "mix", "mem", "ffn", "fin2"]
        normed = {n: sem(f"normed_{n}") for n in NORMS}
        shifted = {n: sem(f"shifted_{n}") for n in ("l0", "l1")}
        route_a, route_b = sem("route_logits"), sem("route_exp")
        e_diag, e_cwp, e_cw, e_a, e_b, e_sg, e_hid, e_out, e_acc, e_pe = (
            sem(n) for n in ("e_diag", "e_cw_sum", "e_cw", "e_first", "e_second", "e_silu", "e_hidden",
                             "e_out", "e_added", "e_hidden_used"))

        def col(name, i=0, n=1):
            a = COL[name][0] + i
            return cols[:, a:a + n]

        def t0(name):
            return c0[:, slice(*C0[name])]

        def t1(name):
            return cb[:, slice(*C1[name])]

        def t2(name):
            return cb[:, slice(*C2[name])]

        def item(q, ks, mask, vs, o, scale, sink=None):
            return dict(q=q, ks=ks, mask=mask, vs=vs, o=o, scale=scale, sink=sink, w=sum(k.shape[-1] for k in ks))

        def layer_items(layer):
            found = []
            for s in range(2 if layer == 0 else 1):
                for h in range(HEADS):
                    g = h // (HEADS // KVH)
                    rows = slice(g * HD, g * HD + HD)
                    for t in range(TT):
                        q = P1[rows, QQ + h % 4, s, t * P:(t + 1) * P]
                        if s == 0:
                            ks, mask, js = [P1[rows, KK, :, :].rearrange("p s n -> p (s n)")], t1(f"band{t}"), range(4)
                        else:
                            ks, mask, js = [P1[rows, KK, 1, :]], t1("band0")[:, 256:512], (2, 3)
                        found.append(item(q, ks, mask, [VT[:, j, g * HD:g * HD + HD] for j in js],
                                          O[:, 2 * s + t, h * HD:h * HD + HD], HD ** -0.5, layer * HEADS + h))
            return found

        def branch_a():
            return [item(PR[g * HD:g * HD + HD, AT[AQ] + h % 4, t * P:(t + 1) * P],
                         [PR[g * HD:g * HD + HD, AT[AK], 0:P * (t + 1)]], MA[:, t, 0:P * (t + 1)],
                         [AVT[:, j, g * HD:g * HD + HD] for j in range(t + 1)],
                         O[:, t, h * HD:h * HD + HD], HD ** -0.5)
                    for h in range(HEADS) for g in [h // 4] for t in range(TT)]

        def branch_b():
            return [item(PR[0:HD, AT[BQ], 0:P], [PR[r, AT[BK] + 4 * g + h // 2, 0:P * (t + 1)] for g in range(3)],
                         t2(f"dil{t}"),
                         [BVT[:, j, (4 * g + h // 2) * P + r.start:(4 * g + h // 2) * P + r.start + HD]
                          for g in range(3) for j in range(t + 1)],
                         O[:, 2 + t, h * HD:h * HD + HD], HD ** -0.5)
                    | dict(qs=[PR[r, AT[BQ] + 4 * g + h // 2, t * P:(t + 1) * P] for g in range(3)])
                    for h in range(HEADS) for r in [slice(h % 2 * HD, h % 2 * HD + HD)] for t in range(TT)]

        def branch_m():
            return [item(PR[:, AT[MQ] + h, t * P:(t + 1) * P], [PR[:, AT[MK] + h, :]], t2("zero"),
                         [MVT[:, j, h * P:(h + 1) * P] for j in range(TT)], O[:, t, h * P:(h + 1) * P], P ** -0.5)
                    for h in range(4) for t in range(TT)]

        STAGES = {"l0": layer_items(0), "l1": layer_items(1), "a": branch_a(), "b": branch_b(), "m": branch_m()}
        first, scored_first, n, extra = {}, {}, 0, 0
        for name, items in STAGES.items():
            if name == "a":
                extra = TT
            first[name], scored_first[name] = n, n + extra
            n += len(items)
        IDX_TURN = first["a"]

        turn = {}
        T_LAST = {}
        V_TURN = {}

        block = ctx.enter_context(nc.Block())

        @block.tensor
        def _(pe):
            mm, tr = nc.tensor.matmul, nc.tensor.transpose
            at = {"lin": 0, "aux": 0, "block": 0, "step": 0, "sq": 0}

            def lin_bank(key=None):
                n = at["lin"]
                if n >= 2:
                    pe.wait_ge(lin_taken, n - 1)
                at["lin"] += 1
                if key is not None:
                    turn[key] = n
                return lin[n % 2]

            def aux_bank(key=None):
                n = at["aux"]
                if n >= 2:
                    pe.wait_ge(aux_taken, n - 1)
                at["aux"] += 1
                if key is not None:
                    turn[key] = n
                return aux[n % 2]

            def block_of_weights():
                b = at["block"]
                at["block"] += 1
                u = b // UNIT
                if b % UNIT == 0:
                    pe.wait_ge(unit_in[u % SLOTS], 16 * (u // SLOTS + 1))
                return ring[:, u % SLOTS, b % UNIT, :].rearrange("p (k m) -> p k m", m=P), b % UNIT == 0 and b > 0

            def product(dst, rhs, wait_k=None):
                w, frees = block_of_weights()
                for k in range(KT):
                    if wait_k:
                        wait_k(k)
                    m = mm(dst, w[:, k, :], rhs(k), start=k == 0, stop=k == KT - 1)
                    if k == 0 and frees:
                        m.then_inc(unit_free, 1)
                return m

            def mean_square(name, ns):
                bank = lin_bank(name)
                for k in range(KT):
                    pe.wait_ge(sq_ready, at["sq"] * KT + k + 1)
                    m = mm(bank[:, 0:ns * SEQ], t0("ones_d"), SQ[:, k % 2, 0:ns * SEQ], start=k == 0, stop=k == KT - 1)
                    m.then_inc(lin_ready if k == KT - 1 else sq_used, 1)
                at["sq"] += 1

            def modulation(layer):
                bank = lin_bank(("ada", layer))
                for t in range(ADA):
                    m = product(bank[:, 2 * t:2 * t + 2], lambda k: SC[:, k, :])
                m.then_inc(lin_ready, 1)

            def rotate(key, src, n_done):
                pe.wait_ge(lin_taken, n_done + 1)
                mm(aux_bank(("rot", key))[:, 0:SEQ], cb[:, 0:P], src, start=True, stop=True).then_inc(aux_ready, 1)

            def turn_tile(key, n_done, v, n):
                pe.wait_ge(lin_taken, n_done + 1)
                bank = aux_bank(("turn", key))
                for j in range(n):
                    m = tr(bank[:, j * P:(j + 1) * P], SQ[:, v % 2, j * P:(j + 1) * P], t0("ident"))
                m.then_inc(aux_ready, 1)

            def attention(name):
                items = STAGES[name]
                for i in range(len(items) + 2):
                    if i < len(items):
                        it, s = items[i], scored_first[name] + i
                        if s >= 2:
                            pe.wait_ge(scores_taken, s - 1)
                        a = 0
                        for j, k in enumerate(it["ks"]):
                            q = it["qs"][j] if "qs" in it else it["q"]
                            m = mm(sc[:, s % 2, a:a + k.shape[-1]], q, k, start=True, stop=True, skip_group_check=True)
                            a += k.shape[-1]
                        m.then_inc(scores_ready, 1)
                    if 1 <= i <= len(items):
                        it, g = items[i - 1], first[name] + i - 1
                        pe.wait_ge(probs_ready, g + 1)
                        nk = it["w"] // P
                        for j in range(nk):
                            if j % 4 == 0:
                                bank = lin_bank()
                            m = tr(bank[:, j % 4 * P:(j % 4 + 1) * P], S[:, g % 2, 1 + j * P:1 + (j + 1) * P], t0("ident"))
                            if j % 4 == 3 or j == nk - 1:
                                m.then_inc(lin_ready, 1)
                        T_LAST[g] = at["lin"] - 1
                    if i >= 2:
                        it, g = items[i - 2], first[name] + i - 2
                        pe.wait_ge(lin_taken, T_LAST[g] + 1)
                        V_TURN[g] = at["aux"]
                        bank = aux_bank()
                        nk = len(it["vs"])
                        for j, v in enumerate(it["vs"]):
                            m = mm(bank[:, 0:v.shape[-1]], PT[:, g % 2, j * P:(j + 1) * P], v, start=j == 0, stop=j == nk - 1)
                        m.then_inc(aux_ready, 1)

            def outputs_turned(name, key, base, ns):
                pe.wait_ge(aux_taken, V_TURN[first[name] + len(STAGES[name]) - 1] + 1)
                for j in range(4):
                    bank = aux_bank((key, j))
                    for t in range(ns * TT):
                        m = tr(bank[:, t * P:(t + 1) * P], O[:, base + t, j * P:(j + 1) * P], t0("ident"))
                    m.then_inc(aux_ready, 1)

            pe.wait_ge(silu_c, 1)
            modulation(0)
            pe.wait_ge(consts_in, 4 * 16)
            for layer in range(DEPTH):
                L = f"l{layer}"
                ns = 2 if layer == 0 else 1
                mean_square(L, 2)
                later, v = None, 0
                for t in range(IN1):
                    both = layer == 0 or t in (KK, VV)
                    n = 512 if both else 256
                    bank = lin_bank((L, t))
                    product(bank[:, 0:n], (lambda k: H[:, 0:2, k, :]) if both else (lambda k: H[:, 0, k, :]),
                            (lambda k: pe.wait_ge(shifted[L], 2 * k + 2)) if t == 0 else None).then_inc(lin_ready, 1)
                    if later:
                        later()
                        later = None
                    if t == KK or QQ <= t < FU:
                        later = lambda t=t: rotate((L, t), P1[:, t, 0, :], turn[L, t])
                    elif t == VV or FU <= t < GA:
                        later = lambda t=t, v=v: turn_tile((L, t), turn[L, t], v, 4 if t == VV else ns * TT)
                        v += 1
                n = ns * SEQ
                pe.wait_ge(conv_done, layer + 1)
                bank = aux_bank((L, "mean"))
                for t in range(2):
                    m = mm(bank[:, 0:n], t0("ones_c"), CV[:, t, 0:ns, :], start=t == 0, stop=t == 1)
                m.then_inc(aux_ready, 1)
                pe.wait_ge(aux_taken, turn["turn", (L, FU + 1)] + 1)
                for s in range(ns):
                    for f in range(2):
                        bank = aux_bank((L, "dft", s, f))
                        for t in range(TT):
                            m = mm(bank[:, :], FT[:, s * TT + t, f * P:(f + 1) * P], t1(f"dft{t}"), start=t == 0, stop=t == 1)
                        m.then_inc(aux_ready, 1)
                pe.wait_ge(conv_sq, layer + 1)
                bank = lin_bank((L, "var"))
                for t in range(2):
                    m = mm(bank[:, 0:n], t0("ones_c"), SQ[:, t, 0:n], start=t == 0, stop=t == 1)
                m.then_inc(lin_ready, 1)
                for f in range(2):
                    pe.wait_ge(aux_taken, turn[L, "dft", ns - 1, f] + 1)
                    bank = aux_bank((L, "mix", f))
                    mm(bank[:, 0:n], t1("bc"), CS[:, f, 0:ns, 0:256], start=True, stop=False)
                    mm(bank[:, 0:n], t1("bs"), CS[:, f, 0:ns, 256:512], start=False, stop=True).then_inc(aux_ready, 1)
                pe.wait_ge(aux_taken, turn[L, "mix", 1] + 1)
                for t in range(2):
                    bank = aux_bank((L, "four", t))
                    for f in range(2):
                        m = mm(bank[:, 0:n], wfour[:, layer, f, t * P:(t + 1) * P], FF[:, f, 0:ns, :], start=f == 0, stop=f == 1)
                    m.then_inc(aux_ready, 1)
                if layer == 0:
                    modulation(1)
                pe.wait_ge(roped, 5 * (layer + 1))
                attention(L)
                outputs_turned(L, (L, "o"), 0, ns)
                pe.wait_ge(aux_taken, turn[(L, "o"), 3] + 1)
                for t in range(KT):
                    bank = aux_bank((L, "out", t))
                    product(bank[:, 0:n], lambda k: YB[:, k, 0:ns, :]).then_inc(aux_ready, 1)
            mean_square("fin1", 1)
            mean_square("mix", 1)
            mean_square("mem", 1)

            pe.wait_ge(c2_in_s, 16)
            later, v, ropes = None, 0, 5 * DEPTH
            for t in range(IN2):
                bank = lin_bank(("in2", t))
                product(bank[:, 0:SEQ], lambda k: H[:, 0, k, :],
                        (lambda k: pe.wait_ge(normed["mix"], k + 1)) if t == 0 else None).then_inc(lin_ready, 1)
                if later:
                    later()
                    later = None
                if t == AV or BV <= t < MQ:
                    later = lambda t=t, v=v: turn_tile(("in2", t), turn["in2", t], v, TT)
                    v += 1
                elif t < MQ:
                    later = lambda t=t: rotate(("in2", t), PR[:, AT[t], :], turn["in2", t])
                    ropes += 1
                if t == BQ:
                    bank = aux_bank("iw")
                    for tt in range(TT):
                        for k in range(KT):
                            m = mm(bank[:, 4 * tt:4 * tt + 4], H[:, 0, k, tt * P:(tt + 1) * P], wsmall[:, k, 20:24],
                                   start=k == 0, stop=k == KT - 1)
                    m.then_inc(aux_ready, 1)
                if t == BQ + 2:
                    pe.wait_ge(roped, 5 * DEPTH + 8)
                    for tt in range(TT):
                        s, w = IDX_TURN + tt, P * (tt + 1)
                        pe.wait_ge(scores_taken, s - 1)
                        for h in range(4):
                            r = slice(h % 2 * HD, h % 2 * HD + HD)
                            a = h % 2 * 512 + h // 2 * w
                            m = mm(sc[:, s % 2, a:a + w], PR[r, AT[IQ] + h // 2, tt * P:(tt + 1) * P],
                                   PR[r, AT[IK], 0:w], start=True, stop=True, skip_group_check=True)
                        m.then_inc(scores_ready, 1)
            for t in range(MK, MK + 8):
                bank = lin_bank(("in2", t))
                product(bank[:, 0:SEQ], lambda k: H[:, 1, k, :],
                        (lambda k: pe.wait_ge(normed["mem"], k + 1)) if t == MK else None).then_inc(lin_ready, 1)
                if later:
                    later()
                    later = None
                if t >= MV:
                    later = lambda t=t, v=v: turn_tile(("in2", t), turn["in2", t], v, TT)
                    v += 1
            later()
            pe.wait_ge(roped, ropes)
            pe.wait_ge(aux_taken, turn["turn", ("in2", MV + 3)] + 1)
            pe.wait_ge(idx_mask, 1)
            attention("a")
            outputs_turned("a", "oa", 0, 1)
            attention("b")
            outputs_turned("b", "ob", 2, 1)
            attention("m")
            outputs_turned("m", "om", 0, 1)
            for mp in range(4):
                for t in (2 * mp, 2 * mp + 1):
                    for b in range(3):
                        bank = lin_bank(("gate", t, b))
                        product(bank[:, 0:SEQ], lambda k: H[:, 0, k, :]).then_inc(lin_ready, 1)
                if mp == 0:
                    pe.wait_ge(aux_taken, turn["om", 3] + 1)
                for b in range(3):
                    w, frees = block_of_weights()
                    for i in range(2):
                        bank = aux_bank(("branch", 2 * mp + i, b))
                        for k in range(4):
                            m = mm(bank[:, 0:SEQ], w[:, 4 * i + k, :], Y[:, 4 * b + k, :], start=k == 0, stop=k == 3)
                            if frees and i == 0 and k == 0:
                                m.then_inc(unit_free, 1)
                        m.then_inc(aux_ready, 1)
            for t in range(KT):
                bank = aux_bank(("out2", t))
                product(bank[:, 0:SEQ], lambda k: H[:, 1, k, :],
                        (lambda k: pe.wait_ge(merged, k + 1)) if t == 0 else None).then_inc(aux_ready, 1)
            mean_square("ffn", 1)
            bank = aux_bank("route")
            for tt in range(TT):
                for k in range(KT):
                    pe.wait_ge(normed["ffn"], k + 1)
                    m = mm(bank[:, 20 * tt:20 * tt + 20], H[:, 0, k, tt * P:(tt + 1) * P], wsmall[:, k, 0:20],
                           start=k == 0, stop=k == KT - 1)
            m.then_inc(aux_ready, 1)
            pe.wait_ge(aux_taken, at["aux"])
            pe.wait_ge(lin_taken, at["lin"])
            base = PADDED // UNIT
            pe.sem_inc(e_cwp, 1)

            with pe.Fori(0, N_EXP) as e:
                def unit(j):
                    u = base + j
                    pe.wait_ge(unit_in[u % SLOTS], 16 * (u // SLOTS + 1) + 16 * e)
                    return ring[:, u % SLOTS, :, :]

                pe.wait_ge(e_diag, e + 1)
                for tt in range(TT):
                    m = mm(sc[:, 0, tt * P:(tt + 1) * P], t0("tri")[:, P:2 * P], DG[:, tt, :], start=True, stop=True,
                           skip_group_check=True)
                m.then_inc(e_cwp, 1)
                for t in range(4):
                    w = unit(t).rearrange("p b (k m) -> p b k m", m=P)
                    pe.wait_ge(e_sg, 4 * e + max(t - 1, 0) + 1)
                    for k in range(KT):
                        m = mm(lin[t % 2][:, 0:SEQ], w[:, 0, k, :], H[:, 0, k, :], start=k == 0, stop=k == KT - 1)
                        if k == 0:
                            m.then_inc(unit_free, 1)
                    m.then_inc(e_a, 1)
                    pe.wait_ge(e_hid, 4 * e + max(t - 1, 0) + 1)
                    for k in range(KT):
                        m = mm(aux[t % 2][:, 0:SEQ], w[:, 1, k, :], H[:, 0, k, :], start=k == 0, stop=k == KT - 1)
                    m.then_inc(e_b, 1)
                pe.wait_ge(e_hid, 4 * e + 5)
                pe.wait_ge(e_acc, 4 * e + 1)
                pe.wait_ge(e_cw, e + 1)
                for j in range(2):
                    w = unit(4 + j).rearrange("p b (i k m) -> p b i k m", m=P, i=2)
                    for b in range(2):
                        mp = 2 * j + b
                        for i in range(2):
                            for k in range(4):
                                m = mm(sc[:, mp // 2, mp % 2 * 512 + i * SEQ:mp % 2 * 512 + (i + 1) * SEQ], w[:, b, i, k, :],
                                       HI[:, k, :], start=k == 0, stop=k == 3, skip_group_check=True)
                                if b == 0 and i == 0 and k == 0:
                                    m.then_inc(unit_free, 1)
                        m.then_inc(e_out, 1)
            bank = lin[0]
            turn["fin2"] = at["lin"]
            at["lin"] += 1
            for k in range(KT):
                pe.wait_ge(sq_ready, at["sq"] * KT + k + 1)
                m = mm(bank[:, 0:SEQ], t0("ones_d"), SQ[:, k % 2, 0:SEQ], start=k == 0, stop=k == KT - 1)
                m.then_inc(lin_ready if k == KT - 1 else sq_used, 1)

        @block.sync
        def _(sp):
            def load(u, slot):
                src = w_stream[u] if isinstance(u, int) else w_stream[bass.ds(u, 1)].rearrange("u p b n -> (u p) b n")
                sp.dma_start(ring[:, slot, :, :], src).then_inc(unit_in[slot], 16)

            rounds = N_UNITS // SLOTS
            for slot in range(SLOTS):
                load(slot, slot)
            with sp.Fori(1, rounds) as r:
                for slot in range(SLOTS):
                    sp.wait_ge(unit_free, SLOTS * r + slot - SLOTS + 1)
                    load(SLOTS * r + slot, slot)
            for u in range(rounds * SLOTS, N_UNITS):
                sp.wait_ge(unit_free, u - SLOTS + 1)
                load(u, u % SLOTS)
            sp.wait_ge(normed["fin2"], KT)
            sp.dma_start(out, H[:, 0, :, :]).then_inc(out_s, 16)
            sp.wait_ge(out_s, 16)

        @block.scalar
        def _(act):
            fn = nc.scalar.activation
            at = {"lin": 0, "sq": 0}

            def take():
                n = at["lin"]
                at["lin"] += 1
                act.wait_ge(lin_ready, n + 1)
                return lin[n % 2]

            def squares(name, src, ns, ready):
                for k in range(KT):
                    ready(k)
                    if k >= 2:
                        act.wait_ge(sq_used, (KT - 1) * at["sq"] + k - 1)
                    fn(SQ[:, k % 2, 0:ns * SEQ], src(k), ACT.Square).then_inc(sq_ready, 1)
                at["sq"] += 1
                if name == "mem":
                    act.wait_ge(normed["mix"], 1)
                fn(RS[:, 0:ns * SEQ], take()[:, 0:ns * SEQ], ACT.Sqrt, bias=col("eps")).then_inc(lin_taken, 1)

            def attention(name):
                items = STAGES[name]
                sinks = sum(x["sink"] is not None for n_, its in STAGES.items() for x in its if first[n_] < first[name])
                for i in range(len(items) + 1):
                    if i < len(items):
                        it, g = items[i], first[name] + i
                        act.wait_ge(bias_ready, g + 1)
                        lo = 1
                        if it["sink"] is not None:
                            sinks += 1
                            act.wait_ge(sink_in, sinks)
                            lo = 0
                        p = S[:, g % 2, lo:1 + it["w"]]
                        fn(p, p, ACT.Exp, bias=ST[:, g % 4, 1:2], scale=it["scale"],
                           accum_out=ST[:, g % 4, 2:3]).then_inc(probs_ready, 1)
                    if i >= 1:
                        it, g = items[i - 1], first[name] + i - 1
                        if g >= 2:
                            act.wait_ge(aux_ready, V_TURN[g - 2] + 1)
                        for a in range(0, it["w"], 512):
                            b = min(a + 512, it["w"])
                            fn(PT[:, g % 2, a:b], take()[:, 0:b - a], ACT.Copy).then_inc(lin_taken, 1)

            act.dma_start(cols[:, :], cols_in).then_inc(cols_in_s, 16)
            act.dma_start(X[:, :, :, :], x_in).then_inc(x_in_s, 16)
            act.dma_start(c0[:, :], c0_in).then_inc(consts_in, 16)
            act.dma_start(cb[:, :], c1_in).then_inc(consts_in, 16)
            act.dma_start(wfour[:, :, :, :], wfour_in).then_inc(consts_in, 16)
            act.dma_start(wsmall[:, :, :], wsmall_in).then_inc(consts_in, 16)
            act.wait_ge(cols_in_s, 16)
            fn(SC.rearrange("p k s -> p (k s)"), col("c", 0, 16), ACT.Silu).then_inc(silu_c, 1)
            fn(MOD[:, 0, :, :].rearrange("p t s -> p (t s)"), take()[:, 0:2 * ADA], ACT.Copy).then_inc(lin_taken, 1)

            for layer in range(DEPTH):
                L = f"l{layer}"
                ns = 2 if layer == 0 else 1
                last = (lambda k: None) if layer == 0 else (lambda k: act.wait_ge(aux_taken, turn["l0", "out", k] + 1))
                if layer == 0:
                    act.wait_ge(x_in_s, 16)
                squares(L, lambda k: X[:, 0:2, k, :], 2, last)
                for k in range(KT):
                    for s in range(2):
                        act.wait_ge(normed[L], 2 * k + s + 1)
                        fn(H[:, s, k, :], H[:, s, k, :], ACT.Identity, bias=MOD[:, layer, k, s:s + 1]).then_inc(shifted[L], 1)
                v = 0
                for t in range(IN1):
                    n = 2 if layer == 0 or t in (KK, VV) else 1
                    bank = take()[:, 0:n * SEQ]
                    if t == VV or FU <= t < GA:
                        if v >= 2:
                            act.wait_ge(aux_ready, turn["turn", (L, FU + v - 3 if v > 2 else VV)] + 1)
                        fn(SQ[:, v % 2, 0:n * SEQ], bank, ACT.Copy).then_inc(lin_taken, 1)
                        v += 1
                    else:
                        f = ACT.Sigmoid if t < CA else ACT.Silu if t >= GA else ACT.Copy
                        fn(P1[:, t, 0:n, :], bank, f).then_inc(lin_taken, 1)
                n = ns * SEQ
                fn(RS[:, 0:n], take()[:, 0:n], ACT.Sqrt, bias=col("eps")).then_inc(lin_taken, 1)
                act.wait_ge(conv_norm, layer + 1)
                for t in range(2):
                    v_ = CV[:, t, 0:ns, :]
                    fn(v_, v_, ACT.Silu, bias=col(f"ln_b{layer}", t), scale=col(f"ln_g{layer}", t)).then_inc(conv_act, 1)
                if layer == 0:
                    fn(MOD[:, 1, :, :].rearrange("p t s -> p (t s)"), take()[:, 0:2 * ADA], ACT.Copy).then_inc(lin_taken, 1)
                attention(L)
            squares("fin1", lambda k: X[:, 0, k, :], 1, lambda k: act.wait_ge(aux_taken, turn["l1", "out", k] + 1))
            act.dma_start(cb[:, 0:N_C2], c2_in).then_inc(c2_in_s, 16)
            act.dma_start(X[:, 1, :, :], mem_in).then_inc(mem_in_s, 16)
            squares("mix", lambda k: X[:, 0, k, :], 1, lambda k: act.wait_ge(normed["fin1"], k + 1))
            squares("mem", lambda k: X[:, 1, k, :], 1, lambda k: act.wait_ge(mem_in_s, 16))
            v = 0
            turned = [AV] + list(range(BV, MQ)) + list(range(MV, MV + 4))
            for t in range(MV + 4):
                bank = take()[:, 0:SEQ]
                if t in turned:
                    if v >= 2:
                        act.wait_ge(aux_ready, turn["turn", ("in2", turned[v - 2])] + 1)
                    fn(SQ[:, v % 2, 0:SEQ], bank, ACT.Copy).then_inc(lin_taken, 1)
                    v += 1
                else:
                    fn(PR[:, AT[t], :], bank, ACT.Copy).then_inc(lin_taken, 1)
            for name in "abm":
                attention(name)
            for t in range(KT):
                for b in range(3):
                    fn(PR[:, 3 * t + b, :], take()[:, 0:SEQ], ACT.Sigmoid, bias=col("b_gate", b * KT + t)).then_inc(lin_taken, 1)
            squares("ffn", lambda k: X[:, 0, k, :], 1, lambda k: act.wait_ge(aux_taken, turn["out2", k] + 1))
            act.wait_ge(route_a, 1)
            for tt in range(TT):
                r = RO[:, tt, :]
                fn(r[:, 44:48], r[:, 0:4], ACT.Exp, bias=r[:, 24:25], accum_out=r[:, 25:26])
                fn(r[:, 26:27], r[:, 27:28], ACT.Exp, bias=r[:, 28:29]).then_inc(route_b, 1)
            act.sem_inc(e_sg, 1)
            with act.Fori(0, N_EXP) as e:
                for t in range(4):
                    act.wait_ge(e_a, 4 * e + t + 1)
                    act.wait_ge(e_hid, 4 * e + max(t - 1, 0) + 1)
                    fn(SG[:, t % 2, :], lin[t % 2][:, 0:SEQ], ACT.Silu).then_inc(e_sg, 1)
            act.wait_ge(e_acc, 4 * N_EXP + 1)
            for k in range(KT):
                if k >= 2:
                    act.wait_ge(sq_used, (KT - 1) * at["sq"] + k - 1)
                fn(SQ[:, k % 2, 0:SEQ], X[:, 0, k, :], ACT.Square).then_inc(sq_ready, 1)
            act.wait_ge(lin_ready, at["lin"] + 1)
            fn(RS[:, 0:SEQ], lin[0][:, 0:SEQ], ACT.Sqrt, bias=col("eps")).then_inc(lin_taken, 1)

        @block.gpsimd
        def _(pool):
            nc.gpsimd.memset(U[:, :, :, 0:PAD], 0.0)
            nc.gpsimd.memset(U[:, :, :, PAD + SEQ:], 0.0).then_inc(pads_ready, 1)
            pool.wait_ge(sinks_ready, 1)
            n = 0
            for name in ("l0", "l1"):
                for i, it in enumerate(STAGES[name]):
                    g = first[name] + i
                    if g >= 2:
                        pool.wait_ge(probs_ready, g - 1)
                    nc.gpsimd.tensor_copy(S[:, g % 2, 0:1], SK[:, it["sink"]:it["sink"] + 1]).then_inc(sink_in, 1)

        @block.vector
        def _(dve):
            v = nc.vector
            at = {"aux": 0, "step": 0}

            def step(ins):
                at["step"] += 1
                ins.then_inc(dve_step, 1)
                return at["step"]

            def after(n):
                dve.wait_ge(dve_step, n)

            def take(key=None):
                n = at["aux"]
                assert key is None or turn[key] == n, (key, turn[key], n)
                at["aux"] += 1
                dve.wait_ge(aux_ready, n + 1)
                return aux[n % 2]

            def norm(name, src, dst, gain, ns):
                n = ns * SEQ
                dve.wait_ge(lin_taken, turn[name] + 1)
                after(step(v.reciprocal(RI[:, 0:n], RS[:, 0:n])))
                for k in range(KT):
                    for s in range(ns):
                        v.scalar_tensor_tensor(out=dst(k, s), in0=src(k, s), scalar=gain(k, s), in1=RI[:, s * SEQ:(s + 1) * SEQ],
                                               op0=ALU.mult, op1=ALU.mult).then_inc(normed[name], 1)
                dve.wait_ge(normed[name], ns * KT)

            def modulation(layer):
                dve.wait_ge(lin_taken, turn["ada", layer] + 1)
                for s in range(2):
                    n = step(v.tensor_tensor(MOD[:, layer, :, s], MOD[:, layer, :, s], col(f"b_ada{layer}", 0, ADA), ALU.add))
                return n

            def gains(layer, n):
                after(n)
                for s in range(2):
                    n = step(v.scalar_tensor_tensor(out=GS[:, :, s], in0=MOD[:, layer, KT:2 * KT, s], scalar=1.0,
                                                    in1=col(f"norm_g{layer}", 0, KT), op0=ALU.add, op1=ALU.mult))
                after(n)

            ropes = [0]

            def rope(key, x, cos, sin):
                b = ropes[0] % 2
                ropes[0] += 1
                bank = take(("rot", key))
                v.tensor_tensor(RT[:, b, :], bank[:, 0:SEQ], sin, ALU.mult).then_inc(aux_taken, 1)
                n = step(v.tensor_tensor(x, x, cos, ALU.mult))
                after(n)
                v.tensor_tensor(x, x, RT[:, b, :], ALU.add).then_inc(roped, 1)

            def attention(name):
                items = STAGES[name]
                for i in range(len(items) + 2):
                    if i < len(items):
                        it, s, g = items[i], scored_first[name] + i, first[name] + i
                        if g >= 2:
                            dve.wait_ge(lin_ready, T_LAST[g - 2] + 1)
                        dve.wait_ge(scores_ready, s + 1)
                        w, st = it["w"], ST[:, g % 4, :]
                        most = SK[:, it["sink"]:it["sink"] + 1] if it["sink"] is not None else -3e38
                        v.tensor_tensor_reduce(out=S[:, g % 2, 1:1 + w], in0=sc[:, s % 2, 0:w], in1=it["mask"], scale=1.0,
                                               scalar=most, op0=ALU.add, op1=ALU.max, accum_out=st[:, 0:1]).then_inc(scores_taken, 1)
                        dve.wait_ge(scores_taken, s + 1)
                        v.tensor_scalar(st[:, 1:2], st[:, 0:1], -it["scale"], None, ALU.mult).then_inc(bias_ready, 1)
                    if i >= 2:
                        it, g = items[i - 2], first[name] + i - 2
                        st = ST[:, g % 4, :]
                        dve.wait_ge(probs_ready, g + 1)
                        after(step(v.reciprocal(st[:, 3:4], st[:, 2:3])))
                        bank = take()
                        v.tensor_scalar(it["o"], bank[:, 0:it["o"].shape[-1]], st[:, 3:4], None, ALU.mult).then_inc(aux_taken, 1)

            dve.wait_ge(cols_in_s, 16)
            v.tensor_scalar(SK[:, :], col("sink", 0, 16), float(HD) ** 0.5, None, ALU.mult).then_inc(sinks_ready, 1)
            n_mod = modulation(0)
            for layer in range(DEPTH):
                L = f"l{layer}"
                ns = 2 if layer == 0 else 1
                n = ns * SEQ
                gains(layer, n_mod)
                if layer == 0:
                    dve.wait_ge(x_in_s, 16)
                norm(L, lambda k, s: X[:, s, k, :], lambda k, s: H[:, s, k, :], lambda k, s: GS[:, k, s:s + 1], 2)

                dve.wait_ge(lin_taken, turn[L, CA + 1] + 1)
                dve.wait_ge(pads_ready, 1)
                last = {}
                for t in range(2):
                    last[t] = step(v.tensor_tensor(U[:, t, 0:ns, PAD:PAD + SEQ], P1[:, CA + t, 0:ns, :], P1[:, CB + t, 0:ns, :], ALU.mult))
                taps = [(k, t) for k in range(CONV_K) for t in range(2)]

                def conv(n_taps):
                    for _ in range(min(n_taps, len(taps))):
                        k, t = taps.pop(0)
                        after(last[t])
                        w, u = col(f"conv_w{layer}", t * CONV_K + k), U[:, t, 0:ns, k:k + SEQ]
                        if k == 0:
                            ins = v.tensor_scalar(CV[:, t, 0:ns, :], u, w, col(f"conv_b{layer}", t), ALU.mult, ALU.add)
                        else:
                            ins = v.scalar_tensor_tensor(out=CV[:, t, 0:ns, :], in0=u, scalar=w, in1=CV[:, t, 0:ns, :],
                                                         op0=ALU.mult, op1=ALU.add)
                        if taps:
                            last[t] = step(ins)
                        else:
                            ins.then_inc(conv_done, 1)

                for t in [KK, VV, QQ, QQ + 1, QQ + 2, QQ + 3, FU, FU + 1]:
                    conv(7)
                    if t == VV:
                        bank = take(("turn", (L, t)))
                        v.tensor_copy(VT.rearrange("p t n -> p (t n)"), bank[:, :]).then_inc(aux_taken, 1)
                    elif t >= FU:
                        bank = take(("turn", (L, t)))
                        v.tensor_copy(FT[:, 0:2 * ns, (t - FU) * P:(t - FU + 1) * P],
                                      bank[:, 0:n].rearrange("p (j n) -> p j n", n=P)).then_inc(aux_taken, 1)
                    else:
                        dve.wait_ge(lin_taken, turn[L, t] + 1)
                        rope((L, t), P1[:, t, 0, :], t1("cos"), t1("sin"))
                conv(len(taps))
                bank = take((L, "mean"))
                for t in range(2):
                    ins = v.tensor_tensor(CV[:, t, 0:ns, :], CV[:, t, 0:ns, :], bank[:, 0:n].rearrange("p (s n) -> p s n", s=ns), ALU.subtract)
                ins.then_inc(aux_taken, 1)
                dve.wait_ge(aux_taken, at["aux"])
                for t in range(2):
                    ins = v.tensor_tensor(SQ[:, t, 0:n].rearrange("p (s n) -> p s n", s=ns), CV[:, t, 0:ns, :], CV[:, t, 0:ns, :], ALU.mult)
                ins.then_inc(conv_sq, 1)
                for s in range(ns):
                    for f in range(2):
                        v.tensor_copy(CS[:, f, s, :], take((L, "dft", s, f))[:, :]).then_inc(aux_taken, 1)
                dve.wait_ge(lin_taken, turn[L, "var"] + 1)
                after(step(v.reciprocal(RI[:, 0:n], RS[:, 0:n])))
                for t in range(2):
                    ins = v.tensor_tensor(CV[:, t, 0:ns, :], CV[:, t, 0:ns, :], RI[:, 0:n].rearrange("p (s n) -> p s n", s=ns), ALU.mult)
                ins.then_inc(conv_norm, 1)
                for f in range(2):
                    v.tensor_copy(FF[:, f, 0:ns, :], take((L, "mix", f))[:, 0:n].rearrange("p (s n) -> p s n", s=ns)).then_inc(aux_taken, 1)
                dve.wait_ge(lin_taken, turn[L, GF + 1] + 1)
                for t in range(2):
                    bank = take((L, "four", t))
                    v.scalar_tensor_tensor(out=YB[:, 6 + t, 0:ns, :], in0=bank[:, 0:n].rearrange("p (s n) -> p s n", s=ns),
                                           scalar=col(f"b_four{layer}", t), in1=P1[:, GF + t, 0:ns, :],
                                           op0=ALU.add, op1=ALU.mult).then_inc(aux_taken, 1)
                for t in range(2):
                    dve.wait_ge(conv_act, 2 * layer + t + 1)
                    v.tensor_tensor(YB[:, 4 + t, 0:ns, :], CV[:, t, 0:ns, :], P1[:, GC + t, 0:ns, :], ALU.mult)
                if layer == 0:
                    n_mod = modulation(1)
                attention(L)
                for j in range(4):
                    bank = take(((L, "o"), j))
                    v.tensor_tensor(YB[:, j, 0:ns, :], bank[:, 0:n].rearrange("p (s n) -> p s n", s=ns), P1[:, GA + j, 0:ns, :],
                                    ALU.mult).then_inc(aux_taken, 1)
                for t in range(KT):
                    bank = take((L, "out", t))
                    for s in range(ns):
                        ins = v.scalar_tensor_tensor(out=X[:, s, t, :], in0=bank[:, s * SEQ:(s + 1) * SEQ],
                                                     scalar=MOD[:, layer, 2 * KT + t, s:s + 1], in1=X[:, s, t, :],
                                                     op0=ALU.mult, op1=ALU.add)
                    ins.then_inc(aux_taken, 1)

            def plain(name, src, dst, gain):
                norm(name, lambda k, s: src[:, k, :], lambda k, s: dst[:, k, :], lambda k, s: col(gain, k), 1)

            dve.wait_ge(aux_taken, at["aux"])
            plain("fin1", X[:, 0], X[:, 0], "final_g")
            dve.wait_ge(normed["fin1"], KT)
            plain("mix", X[:, 0], H[:, 0], "g_mix")
            plain("mem", X[:, 1], H[:, 1], "g_mem")

            dve.wait_ge(c2_in_s, 16)
            for t in range(MV + 4):
                key = ("in2", t)
                if t == AV:
                    v.tensor_copy(AVT[:, :, :], take(("turn", key))[:, 0:SEQ].rearrange("p (t n) -> p t n", t=TT)).then_inc(aux_taken, 1)
                elif BV <= t < MQ:
                    v.tensor_copy(BVT[:, :, (t - BV) * P:(t - BV + 1) * P],
                                  take(("turn", key))[:, 0:SEQ].rearrange("p (t n) -> p t n", t=TT)).then_inc(aux_taken, 1)
                elif t >= MV:
                    v.tensor_copy(MVT[:, :, (t - MV) * P:(t - MV + 1) * P],
                                  take(("turn", key))[:, 0:SEQ].rearrange("p (t n) -> p t n", t=TT)).then_inc(aux_taken, 1)
                elif t < MQ:
                    dve.wait_ge(lin_taken, turn[key] + 1)
                    rope(key, PR[:, AT[t], :], t2("cos"), t2("sin"))
                if t == BQ - 1:
                    v.tensor_copy(IW[:, :, 0:4], take("iw")[:, 0:8].rearrange("p (t n) -> p t n", t=TT)).then_inc(aux_taken, 1)
                    dve.wait_ge(aux_taken, at["aux"])
                if t == BQ + 1:
                    rounds = []
                    for tt in range(TT):
                        s, w = IDX_TURN + tt, P * (tt + 1)
                        dve.wait_ge(scores_ready, s + 1)
                        n = []
                        for h in range(4):
                            a = h % 2 * 512 + h // 2 * w
                            ins = v.tensor_scalar(RL[:, h, 0:w], sc[:, s % 2, a:a + w], 0.0, IW[:, tt, h:h + 1], ALU.max, ALU.mult)
                            n = step(ins) if h < 3 else None
                        ins.then_inc(scores_taken, 1)
                        dve.wait_ge(scores_taken, s + 1)
                        x = DS[:, tt, 0:w]
                        after(step(v.tensor_tensor(x, RL[:, 0, 0:w], RL[:, 1, 0:w], ALU.add)))
                        after(step(v.tensor_tensor(x, x, RL[:, 2, 0:w], ALU.add)))
                        after(step(v.tensor_tensor(x, x, RL[:, 3, 0:w], ALU.add)))
                        after(step(v.tensor_tensor(x, x, t2(f"causal{tt}"), ALU.add)))
                if BQ + 1 <= t < BQ + 1 + TOPK // 8:
                    for tt in range(TT):
                        x = DS[:, tt, 0:P * (tt + 1)]
                        after(step(v.max(M8[:, tt, :], x)))
                        after(step(v.match_replace(x, M8[:, tt, :], x, GONE)))
                if t == BQ + 1 + TOPK // 8:
                    for tt in range(TT):
                        w = P * (tt + 1)
                        after(step(v.tensor_scalar(MA[:, tt, 0:w], DS[:, tt, 0:w], GONE, NEG, ALU.not_equal, ALU.mult)))
                        ins = v.tensor_tensor(MA[:, tt, 0:w], MA[:, tt, 0:w], t2(f"causal{tt}"), ALU.add)
                        if tt == 0:
                            step(ins)
                    ins.then_inc(idx_mask, 1)
                    dve.wait_ge(idx_mask, 1)

            for b, name in enumerate("abm"):
                attention(name)
                for j in range(4):
                    v.tensor_copy(Y[:, 4 * b + j, :], take(("o" + name, j))[:, 0:SEQ]).then_inc(aux_taken, 1)
            for mp in range(4):
                for b in range(3):
                    for t in (2 * mp, 2 * mp + 1):
                        dve.wait_ge(lin_taken, turn["gate", t, b] + 1)
                        g = PR[:, 3 * t + b, :]
                        v.tensor_tensor(g, take(("branch", t, b))[:, 0:SEQ], g, ALU.mult).then_inc(aux_taken, 1)
                dve.wait_ge(aux_taken, at["aux"])
                for t in (2 * mp, 2 * mp + 1):
                    n = step(v.tensor_tensor(PR[:, 3 * t, :], PR[:, 3 * t, :], PR[:, 3 * t + 1, :], ALU.add))
                after(n)
                for t in (2 * mp, 2 * mp + 1):
                    v.tensor_tensor(H[:, 1, t, :], PR[:, 3 * t, :], PR[:, 3 * t + 2, :], ALU.add).then_inc(merged, 1)
            for t in range(KT):
                v.tensor_tensor(X[:, 0, t, :], take(("out2", t))[:, 0:SEQ], X[:, 0, t, :], ALU.add).then_inc(aux_taken, 1)
            dve.wait_ge(aux_taken, at["aux"])
            plain("ffn", X[:, 0], H[:, 0], "g_ffn")

            bank = take("route")
            for tt in range(TT):
                r = RO[:, tt, :]
                ins = v.tensor_tensor(r[:, 0:20], bank[:, 20 * tt:20 * tt + 20], col("b_route", 0, 20), ALU.add)
                if tt == 0:
                    step(ins)
            ins.then_inc(aux_taken, 1)
            dve.wait_ge(aux_taken, at["aux"])

            def link(ins):
                after(step(ins))

            def first_max(out_, x, top, r):
                link(v.tensor_reduce(top, x, AX.X, ALU.max))
                link(v.tensor_scalar(r[:, 80:84], x, top, None, ALU.is_ge))
                link(v.tensor_tensor_scan(r[:, 84:88], r[:, 88:92], r[:, 80:84], 0.0, ALU.mult, ALU.add))
                link(v.scalar_tensor_tensor(out=out_, in0=r[:, 84:88], scalar=1.0, in1=r[:, 80:84], op0=ALU.is_le, op1=ALU.mult))

            for tt in range(TT):
                r = RO[:, tt, :]
                link(v.memset(r[:, 88:92], 1.0))
                first_max(r[:, 32:36], r[:, 0:4], r[:, 20:21], r)
                link(v.tensor_scalar(r[:, 24:25], r[:, 20:21], -1.0, None, ALU.mult))
                link(v.tensor_scalar(r[:, 36:40], r[:, 4:8], r[:, 32:33], None, ALU.mult))
                for g in range(1, 4):
                    link(v.scalar_tensor_tensor(out=r[:, 36:40], in0=r[:, 4 + 4 * g:8 + 4 * g], scalar=r[:, 32 + g:33 + g],
                                                in1=r[:, 36:40], op0=ALU.mult, op1=ALU.add))
                first_max(r[:, 48:52], r[:, 36:40], r[:, 21:22], r)
                link(v.tensor_scalar(r[:, 28:29], r[:, 21:22], -1.0, None, ALU.mult))
                link(v.scalar_tensor_tensor(out=r[:, 40:44], in0=r[:, 48:52], scalar=NEG, in1=r[:, 36:40], op0=ALU.mult, op1=ALU.add))
                first_max(r[:, 52:56], r[:, 40:44], r[:, 27:28], r)
            v.memset(RO[:, 0, 92:93], 0.0).then_inc(route_a, 1)
            for tt in range(TT):
                r = RO[:, tt, :]
                dve.wait_ge(route_b, tt + 1)
                link(v.tensor_scalar(r[:, 56:57], r[:, 26:27], 1.0, r[:, 25:26], ALU.add, ALU.mult))
                link(v.reciprocal(r[:, 57:58], r[:, 56:57]))
                link(v.tensor_scalar(r[:, 58:59], r[:, 26:27], r[:, 57:58], None, ALU.mult))
                link(v.tensor_scalar(r[:, 60:64], r[:, 48:52], r[:, 57:58], None, ALU.mult))
                link(v.scalar_tensor_tensor(out=r[:, 60:64], in0=r[:, 52:56], scalar=r[:, 58:59], in1=r[:, 60:64],
                                            op0=ALU.mult, op1=ALU.add))
                for g in range(4):
                    link(v.tensor_scalar(CM[:, tt, 4 * g:4 * g + 4], r[:, 60:64], r[:, 32 + g:33 + g], None, ALU.mult))

            dve.sem_inc(e_hid, 1)
            dve.sem_inc(e_acc, 1)
            with dve.Fori(0, N_EXP) as e:
                dve.wait_ge(e_cwp, e + 1)
                for tt in range(TT):
                    ins = v.tensor_scalar(DG[:, tt, :], t0("ident"), CM[:, tt, bass.ds(e, 1)], None, ALU.mult)
                ins.then_inc(e_diag, 1)
                dve.wait_ge(e_cwp, e + 2)
                v.tensor_copy(CW, sc[:, 0, 0:SEQ]).then_inc(e_cw, 1)
                dve.wait_ge(e_cw, e + 1)
                for t in range(4):
                    dve.wait_ge(e_sg, 4 * e + t + 2)
                    v.tensor_tensor(SG[:, t % 2, :], SG[:, t % 2, :], CW, ALU.mult).then_inc(e_pe, 1)
                    dve.wait_ge(e_b, 4 * e + t + 1)
                    dve.wait_ge(e_pe, 4 * e + t + 1)
                    v.tensor_tensor(HI[:, t, :], aux[t % 2][:, 0:SEQ], SG[:, t % 2, :], ALU.mult).then_inc(e_hid, 1)
                for mp in range(4):
                    dve.wait_ge(e_out, 4 * e + mp + 1)
                    x = X[:, 0, 2 * mp:2 * mp + 2, :].rearrange("p k n -> p (k n)")
                    v.tensor_tensor(x, sc[:, mp // 2, mp % 2 * 512:mp % 2 * 512 + 512], x, ALU.add).then_inc(e_acc, 1)
                dve.wait_ge(e_acc, 4 * e + 5)
            plain("fin2", X[:, 0], H[:, 0], "g_final")


def tiles_of(w, n):
    return w.reshape(KT, P, n, P).transpose(2, 1, 0, 3).reshape(n, P, KT * P)


def pairs_of(w):
    n = w.shape[1] // 256
    return w.reshape(4, P, n, 2, P).transpose(2, 1, 3, 0, 4).reshape(n, P, KT * P)


def per_feature(v):
    return v.reshape(-1, P).T


def kernel(**inputs):
    import concourse.bacc as bacc
    from concourse.bass_utils import run_bass_kernel_spmd

    a = {k: np.asarray(v) for k, v in inputs.items()}
    grouped = np.concatenate([np.arange(h * HD, h * HD + HD) for t in range(4) for h in (t, t + 4)])
    o = np.cumsum([0, 512, 128, 128, 512, 256, 256, 256, 256, 256])
    q, k, v, ga, ca, cbb, gc, fu, gf = (np.arange(o[i], o[i + 1]) for i in range(9))
    in1 = np.concatenate([cbb, ca, k, v, q[grouped], fu, ga, gc, gf])
    o = np.cumsum([0, 512, 128, 128, 256, 64, 4, 1536, 1536, 1536, 512])
    aq, ak, av, iq, ik, iw, bq, bk, bv, mq = (np.arange(o[i], o[i + 1]) for i in range(10))
    in2 = np.concatenate([aq[grouped], ak, av, iq, ik, ik, bq, bk, bv, mq])
    stream = [tiles_of(a["w_ada"][0], ADA), tiles_of(a["w_in"][0][:, in1], IN1), tiles_of(a["w_ada"][1], ADA),
              tiles_of(a["w_out"][0], KT), tiles_of(a["w_in"][1][:, in1], IN1), tiles_of(a["w_out"][1], KT),
              tiles_of(a["w_in_2"][0][:, in2], IN2), tiles_of(a["w_mem_kv_2"][0], 8)]
    gates = tiles_of(a["w_gate_2"][0], ADA)
    branches = [pairs_of(a["w_branch_2"][0, b]) for b in range(3)]
    for mp in range(4):
        stream += [gates[b * KT + t][None] for t in (2 * mp, 2 * mp + 1) for b in range(3)]
        stream += [branches[b][mp][None] for b in range(3)]
    stream.append(tiles_of(a["w_out_2"][0], KT))
    stream.append(np.zeros((PADDED - N_HEAD_BLOCKS, P, KT * P), np.float32))
    for e in range(N_EXP):
        w1, w3 = tiles_of(a["w1_2"][0, e], 4), tiles_of(a["w3_2"][0, e], 4)
        stream.append(np.stack([w1, w3], 1).reshape(8, P, KT * P))
        stream.append(pairs_of(a["w2_2"][0, e]))
    w_stream = np.concatenate(stream).reshape(N_UNITS, UNIT, P, KT * P).transpose(0, 2, 1, 3)

    cols = np.zeros((P, N_COL), np.float32)

    def put(name, x):
        cols[:, slice(*COL[name])] = x

    put("c", np.stack([per_feature(a["c"][0]), per_feature(a["c_ctx"])], 2).reshape(P, 16))
    for name in ("final_g",):
        put(name, per_feature(a[name]))
    for name, key in (("g_mix", "g_mix_2"), ("g_mem", "g_mem_2"), ("g_ffn", "g_ffn_2"), ("b_gate", "b_gate_2")):
        put(name, per_feature(a[key][0]))
    put("g_final", per_feature(a["g_final_2"]))
    for l in range(DEPTH):
        put(f"b_ada{l}", per_feature(a["b_ada"][l]))
        put(f"norm_g{l}", per_feature(a["norm_g"][l]))
        put(f"conv_w{l}", a["conv_w"][l].T.reshape(2, P, CONV_K).transpose(1, 0, 2).reshape(P, 2 * CONV_K))
        put(f"conv_b{l}", per_feature(a["conv_b"][l]))
        put(f"ln_g{l}", per_feature(a["conv_ln_g"][l]))
        put(f"ln_b{l}", per_feature(a["conv_ln_b"][l]))
        put(f"b_four{l}", per_feature(a["b_four"][l]))
    put("sink", np.broadcast_to(a["attn_sink"].reshape(1, 16), (P, 16)))
    put("b_route", np.broadcast_to(np.concatenate([a["b_group_2"][0], a["b_sub_2"][0].reshape(16)])[None], (P, 20)))
    put("eps", np.full((P, 1), EPS, np.float32))
    x_in = np.stack([a["x"][0], a["ctx"][0]]).transpose(2, 0, 1).reshape(KT, P, 2, SEQ).transpose(1, 2, 0, 3)
    mem_in = a["mem_2"][0].T.reshape(KT, P, SEQ).transpose(1, 0, 2)
    wfour = a["w_four"].reshape(DEPTH, 2, P, 256).transpose(2, 0, 1, 3)
    small = np.concatenate([a["w_group_2"][0], a["w_sub_2"][0].transpose(1, 0, 2).reshape(D, 16), a["w_in_2"][0][:, iw]], 1)
    small = small.reshape(KT, P, 24).transpose(1, 0, 2)
    c0, c1, c2 = constants()

    nc = bacc.Bacc("TRN2", target_bir_lowering=False, num_devices=1)
    arrays, args = {}, []
    for name, x in (("w_stream", w_stream), ("x_in", x_in), ("mem_in", mem_in), ("cols_in", cols), ("wfour_in", wfour),
                    ("wsmall_in", small), ("c0_in", c0), ("c1_in", c1), ("c2_in", c2)):
        arrays[name] = np.ascontiguousarray(x)
        args.append(nc.dram_tensor(name, x.shape, F32, kind="ExternalInput").ap())
    args.append(nc.dram_tensor("out", (P, KT, SEQ), F32, kind="ExternalOutput").ap())
    build(nc, *args)
    r = run_bass_kernel_spmd(nc, [arrays], core_ids=[0])
    y = r.results[0]["out"]
    return y.transpose(2, 1, 0).reshape(1, SEQ, D)
```

```python
from contextlib import ExitStack

import numpy as np
import concourse.bass as bass
from concourse import mybir

ALU = mybir.AluOpType
ACT = mybir.ActivationFunctionType
AX = mybir.AxisListType
F32 = mybir.dt.float32

P = 128
D = 1024
KT = D // P
SEQ = 256
TT = SEQ // P
DEPTH = 2
HEADS, KVH, HD = 8, 2, 64
CONV_W, CONV_K = 256, 31
PAD = CONV_K // 2
N_EXP, EPG, TOPK = 16, 4, 64
NEG = -1e30
GONE = -3e38
EPS = 1e-6

CB, CA, KK, VV, QQ, FU, GA, GC, GF = 0, 2, 4, 5, 6, 10, 12, 16, 18
IN1 = 20
AQ, AK, AV, IQ, IK, BQ, BK, BV, MQ = 0, 4, 5, 6, 8, 9, 21, 33, 45
IN2 = 49
MK, MV = IN2, IN2 + 4
AT = {AQ + i: i for i in range(5)} | {IQ + i: 5 + i for i in range(3)} | {BQ + i: 8 + i for i in range(24)} \
    | {MQ + i: 32 + i for i in range(4)} | {MK + i: 36 + i for i in range(4)}
ADA = 24
N_HEAD_BLOCKS = DEPTH * (ADA + IN1 + KT) + IN2 + 8 + ADA + 12 + KT
PADDED = N_HEAD_BLOCKS + N_HEAD_BLOCKS % 2
UNIT = 2
SLOTS = 6
BASE = PADDED // UNIT
PAIR_UNITS = 12
PAIRS = N_EXP // 2
N_UNITS = BASE + PAIRS * PAIR_UNITS
CAP = 64
PASSES = SEQ // CAP
EC = PASSES * N_EXP + 2

COL = {}
_n = 0
for _name, _w in [("c", 16), ("b_ada0", 24), ("b_ada1", 24), ("norm_g0", 8), ("norm_g1", 8), ("final_g", 8),
                  ("g_mix", 8), ("g_mem", 8), ("g_ffn", 8), ("g_final", 8), ("b_gate", 24),
                  ("conv_w0", 62), ("conv_w1", 62), ("conv_b0", 2), ("conv_b1", 2), ("ln_g0", 2), ("ln_g1", 2),
                  ("ln_b0", 2), ("ln_b1", 2), ("b_four0", 2), ("b_four1", 2), ("sink", 16), ("b_route", 20),
                  ("eps", 1)]:
    COL[_name] = (_n, _n + _w)
    _n += _w
N_COL = _n

C0 = {}
_n = 0
for _name, _w in [("ident", 128), ("ones_d", 128), ("ones_c", 128), ("tri", 256), ("iota", CAP)]:
    C0[_name] = (_n, _n + _w)
    _n += _w
N_C0 = _n
C1 = {}
_n = 0
for _name, _w in [("rot", 128), ("cos", 256), ("sin", 256), ("dft0", 512), ("dft1", 512), ("bc", 128), ("bs", 128),
                  ("band0", 512), ("band1", 512)]:
    C1[_name] = (_n, _n + _w)
    _n += _w
N_C1 = _n
C2 = {}
_n = 0
for _name, _w in [("rot", 128), ("cos", 256), ("sin", 256), ("dil0", 384), ("dil1", 768), ("zero", 256),
                  ("causal0", 128), ("causal1", 256)]:
    C2[_name] = (_n, _n + _w)
    _n += _w
N_C2 = _n


def constants():
    f = np.float32
    c0, c1, c2 = np.zeros((P, N_C0), f), np.zeros((P, N_C1), f), np.zeros((P, N_C2), f)
    i = np.arange(P)
    c0[:, slice(*C0["ident"])] = np.eye(P)
    c0[:, slice(*C0["ones_d"])] = 1.0 / D
    c0[:, slice(*C0["ones_c"])] = 1.0 / CONV_W
    c0[:, slice(*C0["tri"])] = np.concatenate([(i[:, None] < i[None, :]), np.ones((P, P))], 1)
    c0[:, slice(*C0["iota"])] = np.arange(CAP)
    tok = np.arange(SEQ)

    def rope(c, table, half, pos_of):
        d = i % (2 * half)
        freq = f(10000.0) ** (-np.arange(half, dtype=f) / f(half))
        ang = (pos_of[i // (2 * half) % 2][:, tok].astype(f) * freq[d % half][:, None]).astype(f)
        c[:, slice(*table["cos"])] = np.cos(ang)
        c[:, slice(*table["sin"])] = np.sin(ang)
        rot = np.zeros((P, P), f)
        for m in range(P):
            if m % (2 * half) < half:
                rot[m + half, m] = -1.0
            else:
                rot[m - half, m] = 1.0
        c[:, slice(*table["rot"])] = rot

    rope(c1, C1, 16, np.stack([tok // 64, tok % 64]))
    rope(c2, C2, 32, np.stack([tok, tok]))
    ang = 2 * np.pi * ((tok[:, None] * tok[None, :]) % SEQ) / SEQ
    cs = np.concatenate([np.cos(ang), np.sin(ang)], 1)
    c1[:, slice(*C1["dft0"])] = cs[:P]
    c1[:, slice(*C1["dft1"])] = cs[P:]
    a64 = 2 * np.pi * ((i[:, None] * i[None, :]) % HD) / HD
    same = (i[:, None] // HD) == (i[None, :] // HD)
    norm = 1.0 / np.sqrt(SEQ * HD)
    c1[:, slice(*C1["bc"])] = np.where(same, np.cos(a64), 0) * norm
    c1[:, slice(*C1["bs"])] = np.where(same, -np.sin(a64), 0) * norm
    for t in range(TT):
        q = t * P + i[:, None]
        band = np.where(np.abs(q - tok[None, :]) <= 128, 0.0, NEG)
        c1[:, slice(*C1[f"band{t}"])] = np.concatenate([band, np.zeros((P, SEQ))], 1)
        ks = np.arange(P * (t + 1))[None, :]
        c2[:, slice(*C2[f"dil{t}"])] = np.concatenate(
            [np.where((ks <= q) & ((q - ks) % dil == 0) & (q - ks <= win), 0.0, NEG)
             for win, dil in ((128, 1), (512, 4), (2048, 16))], 1)
        c2[:, slice(*C2[f"causal{t}"])] = np.where(ks <= q, 0.0, NEG)
    return c0, c1, c2



def build(nc, w_stream, x_in, mem_in, cols_in, wfour_in, wsmall_in, c0_in, c1_in, c2_in, out):
    ctx = ExitStack()
    with ctx:
        def sb(name, shape):
            return ctx.enter_context(nc.sbuf_tensor(name, shape, F32))

        def sem(name):
            return ctx.enter_context(nc.semaphore(name))

        ring = sb("ring", [P, SLOTS, UNIT, KT * P])
        X = sb("X", [P, 2, KT, SEQ])
        H = sb("H", [P, 2, KT, SEQ])
        PR = sb("PR", [P, 2 * IN1, SEQ])
        UN = sb("UN", [P, 4352])
        Y = sb("Y", [P, 16, SEQ])
        RS = sb("RS", [P, 512])
        RI = sb("RI", [P, 512])
        MOD = sb("MOD", [P, DEPTH, ADA, 2])
        GS = sb("GS", [P, KT, 2])
        SC = sb("SC", [P, KT, 2])
        cols = sb("cols", [P, N_COL])
        SK = sb("SK", [P, DEPTH * HEADS])
        ST = sb("ST", [P, 4, 4])
        O = sb("O", [P, 4, 512])
        S = sb("S", [P, 2, 772])
        PT = sb("PT", [P, 2, 768])
        SQ = sb("SQ", [P, 2, 512])
        RT = sb("RT", [P, 2, SEQ])
        c0 = sb("c0", [P, N_C0])
        cb = sb("cb", [P, N_C1])
        wfour = sb("wfour", [P, DEPTH, 2, 256])
        wsmall = sb("wsmall", [P, KT, 24])
        NP = ctx.enter_context(nc.sbuf_tensor("NP", [P, 1], mybir.dt.int32))
        IW = sb("IW", [P, TT, 8])
        M8 = sb("M8", [P, TT, 8])
        RO = sb("RO", [P, TT, 96])
        CM = sb("CM", [P, TT, N_EXP])

        P1 = PR.rearrange("p (t s) n -> p t s n", s=2)
        YB = Y.rearrange("p (t s) n -> p t s n", s=2)
        U = UN[:, 0:1144].rearrange("p (t s n) -> p t s n", t=2, s=2)
        CV = UN[:, 1144:2168].rearrange("p (t s n) -> p t s n", t=2, s=2)
        FT = UN[:, 2168:3192].rearrange("p (t n) -> p t n", t=4)
        VT = UN[:, 3192:3704].rearrange("p (t n) -> p t n", t=4)
        H1 = H.rearrange("p s k n -> p (s k n)")
        CS = H1[:, 0:2048].rearrange("p (f s n) -> p f s n", f=2, s=2)
        FF = H1[:, 2048:3072].rearrange("p (f s n) -> p f s n", f=2, s=2)
        BVT = UN[:, 0:3072].rearrange("p (t n) -> p t n", t=TT)
        AVT = UN[:, 3072:3328].rearrange("p (t n) -> p t n", t=TT)
        MVT = UN[:, 3328:4352].rearrange("p (t n) -> p t n", t=TT)
        X1 = X[:, 1, :, :].rearrange("p k n -> p (k n)")
        DS = X1[:, 0:512].rearrange("p (t n) -> p t n", t=TT)
        MA = X1[:, 512:1024].rearrange("p (t n) -> p t n", t=TT)
        RL = X1[:, 1024:2048].rearrange("p (h n) -> p h n", h=4)
        E1 = PR.rearrange("p t n -> p (t n)")
        TK = E1[:, 0:2048].rearrange("p (t n) -> p t n", t=TT)
        TE = E1[:, 2048:3072].rearrange("p (k n) -> p k n", k=KT)
        SG = E1[:, 3072:3584]
        HS = E1[:, 3584:4096]
        HT = E1[:, 4096:4608].rearrange("p (k n) -> p k n", k=4)
        YS = E1[:, 4608:5632]
        SEL = E1[:, 5632:5888].rearrange("p (t n) -> p t n", t=TT)
        SW = E1[:, 5888:6144].rearrange("p (t n) -> p t n", t=TT)
        SWT = E1[:, 6144:6400]
        PX = E1[:, 6400:6400 + TT * EC].rearrange("p (t n) -> p t n", t=TT)
        CX = E1[:, 6600:6600 + TT * EC].rearrange("p (t n) -> p t n", t=TT)
        MK1 = E1[:, 6800:6832].rearrange("p (t n) -> p t n", t=TT)
        CN = E1[:, 6832:6840]

        lin = [ctx.enter_context(nc.psum_tensor(f"lin{i}", [P, 512], F32)) for i in range(2)]
        aux = [ctx.enter_context(nc.psum_tensor(f"aux{i}", [P, 512], F32)) for i in range(2)]
        sc = ctx.enter_context(nc.psum_tensor("sc", [P, 2, 1024], F32))

        unit_in = [sem(f"unit_in{i}") for i in range(SLOTS)]
        unit_free = sem("unit_free")
        cols_in_s, x_in_s, consts_in, mem_in_s, c2_in_s, out_s = (
            sem(n) for n in ("cols_in", "x_in", "consts_in", "mem_in", "c2_in", "out_stored"))
        lin_ready, lin_taken = sem("lin_ready"), sem("lin_taken")
        aux_ready, aux_taken = sem("aux_ready"), sem("aux_taken")
        scores_ready, scores_taken = sem("scores_ready"), sem("scores_taken")
        bias_ready, probs_ready, sink_in = (sem(n) for n in ("bias_ready", "probs_ready", "sink_in"))
        silu_c, sinks_ready, pads_ready = sem("silu_c"), sem("sinks_ready"), sem("pads_ready")
        sq_ready, sq_used = sem("sq_ready"), sem("sq_used")
        dve_step = sem("dve_step")
        roped, conv_done, conv_sq, conv_norm, conv_act = (
            sem(n) for n in ("roped", "conv_done", "conv_sq", "conv_norm", "conv_act"))
        idx_mask, merged, gains_ready = sem("idx_mask"), sem("merged"), sem("gains_ready")
        NORMS = ["l0", "l1", "fin1", "mix", "mem", "ffn", "fin2"]
        normed = {n: sem(f"normed_{n}") for n in NORMS}
        shifted = {n: sem(f"shifted_{n}") for n in ("l0", "l1")}
        route_a, route_b, places_from = sem("route_logits"), sem("route_exp"), sem("places_from")
        rows_turned = sem("rows_turned")
        (e_first, e_third, e_silu, e_hidden, e_turned, e_hid_in, e_gathered, e_te_in, e_y, e_y_lo, e_y_hi, e_sel, e_sw,
         e_swt, e_swt_in, e_out, e_added, pairs_in) = (sem(n) for n in (
             "e_first", "e_third", "e_silu", "e_hidden", "e_turned", "e_hid_in", "e_gathered", "e_te_in", "e_y", "e_y_lo",
             "e_y_hi", "e_sel", "e_sw", "e_swt", "e_swt_in", "e_out", "e_added", "pairs_in"))

        def col(name, i=0, n=1):
            a = COL[name][0] + i
            return cols[:, a:a + n]

        def t0(name):
            return c0[:, slice(*C0[name])]

        def t1(name):
            return cb[:, slice(*C1[name])]

        def t2(name):
            return cb[:, slice(*C2[name])]

        def item(q, ks, mask, vs, o, scale, sink=None):
            return dict(q=q, ks=ks, mask=mask, vs=vs, o=o, scale=scale, sink=sink, w=sum(k.shape[-1] for k in ks))

        def layer_items(layer):
            found = []
            for s in range(2 if layer == 0 else 1):
                for h in range(HEADS):
                    g = h // (HEADS // KVH)
                    rows = slice(g * HD, g * HD + HD)
                    for t in range(TT):
                        q = P1[rows, QQ + h % 4, s, t * P:(t + 1) * P]
                        if s == 0:
                            ks, mask, js = [P1[rows, KK, :, :].rearrange("p s n -> p (s n)")], t1(f"band{t}"), range(4)
                        else:
                            ks, mask, js = [P1[rows, KK, 1, :]], t1("band0")[:, 256:512], (2, 3)
                        found.append(item(q, ks, mask, [VT[:, j, g * HD:g * HD + HD] for j in js],
                                          O[:, 2 * s + t, h * HD:h * HD + HD], HD ** -0.5, layer * HEADS + h))
            return found

        def branch_a():
            return [item(PR[g * HD:g * HD + HD, AT[AQ] + h % 4, t * P:(t + 1) * P],
                         [PR[g * HD:g * HD + HD, AT[AK], 0:P * (t + 1)]], MA[:, t, 0:P * (t + 1)],
                         [AVT[:, j, g * HD:g * HD + HD] for j in range(t + 1)],
                         O[:, t, h * HD:h * HD + HD], HD ** -0.5)
                    for h in range(HEADS) for g in [h // 4] for t in range(TT)]

        def branch_b():
            return [item(PR[0:HD, AT[BQ], 0:P], [PR[r, AT[BK] + 4 * g + h // 2, 0:P * (t + 1)] for g in range(3)],
                         t2(f"dil{t}"),
                         [BVT[:, j, (4 * g + h // 2) * P + r.start:(4 * g + h // 2) * P + r.start + HD]
                          for g in range(3) for j in range(t + 1)],
                         O[:, 2 + t, h * HD:h * HD + HD], HD ** -0.5)
                    | dict(qs=[PR[r, AT[BQ] + 4 * g + h // 2, t * P:(t + 1) * P] for g in range(3)])
                    for h in range(HEADS) for r in [slice(h % 2 * HD, h % 2 * HD + HD)] for t in range(TT)]

        def branch_m():
            return [item(PR[:, AT[MQ] + h, t * P:(t + 1) * P], [PR[:, AT[MK] + h, :]], t2("zero"),
                         [MVT[:, j, h * P:(h + 1) * P] for j in range(TT)], O[:, t, h * P:(h + 1) * P], P ** -0.5)
                    for h in range(4) for t in range(TT)]

        STAGES = {"l0": layer_items(0), "l1": layer_items(1), "a": branch_a(), "b": branch_b(), "m": branch_m()}
        first, scored_first, n, extra = {}, {}, 0, 0
        for name, items in STAGES.items():
            if name == "a":
                extra = TT
            first[name], scored_first[name] = n, n + extra
            n += len(items)
        IDX_TURN = first["a"]

        turn = {}
        T_LAST = {}
        V_TURN = {}

        block = ctx.enter_context(nc.Block())

        @block.tensor
        def _(pe):
            mm, tr = nc.tensor.matmul, nc.tensor.transpose
            at = {"lin": 0, "aux": 0, "block": 0, "sq": 0, "owed": 0, "open": 0}

            def lin_bank(key=None):
                n = at["lin"]
                if n >= 2:
                    pe.wait_ge(lin_taken, n - 1)
                at["lin"] += 1
                if key is not None:
                    turn[key] = n
                return lin[n % 2]

            def aux_bank(key=None):
                n = at["aux"]
                if n >= 2:
                    pe.wait_ge(aux_taken, n - 1)
                at["aux"] += 1
                if key is not None:
                    turn[key] = n
                return aux[n % 2]

            def frees(m):
                if at["owed"]:
                    at["owed"] -= 1
                    m.then_inc(unit_free, 1)

            def unit_of_weights():
                u = at["block"] // UNIT
                at["block"] += UNIT
                at["owed"], at["open"] = at["owed"] + at["open"], 0
                pe.wait_ge(unit_in[u % SLOTS], 16 * (u // SLOTS + 1))
                return ring[:, u % SLOTS, :, :].rearrange("p b (k n) -> p (b k) n", n=512)

            def block_of_weights():
                b = at["block"]
                at["block"] += 1
                u = b // UNIT
                if b % UNIT == 0:
                    pe.wait_ge(unit_in[u % SLOTS], 16 * (u // SLOTS + 1))
                    at["owed"], at["open"] = at["owed"] + at["open"], 1
                return ring[:, u % SLOTS, b % UNIT, :].rearrange("p (k m) -> p k m", m=P)

            def product(dst, rhs, wait_k=None):
                w = block_of_weights()
                for k in range(KT):
                    if wait_k:
                        wait_k(k)
                    m = mm(dst, w[:, k, :], rhs(k), start=k == 0, stop=k == KT - 1)
                    if k < KT - 1:
                        frees(m)
                return m

            def mean_square(name, ns):
                bank = lin_bank(name)
                for k in range(KT):
                    pe.wait_ge(sq_ready, at["sq"] * KT + k + 1)
                    m = mm(bank[:, 0:ns * SEQ], t0("ones_d"), SQ[:, k % 2, 0:ns * SEQ], start=k == 0, stop=k == KT - 1)
                    m.then_inc(lin_ready if k == KT - 1 else sq_used, 1)
                at["sq"] += 1

            def modulation(layer):
                for r in range(2):
                    bank = lin_bank(("ada", layer, r))
                    for half in range(2):
                        w = [unit_of_weights() for _ in range(3)]
                        for k in range(4):
                            for j in range(3):
                                m = mm(bank[32 * j:32 * j + 2, :], SC[:, 4 * half + k, :], w[j][:, k, :],
                                       start=half == 0 and k == 0, stop=half == 1 and k == 3)
                                if half == 0 or k < 3 or j < 2:
                                    frees(m)
                        if half == 0:
                            at["owed"] += 3
                    m.then_inc(lin_ready, 1)
                    at["owed"] += 3
                bank = None
                for r in range(2):
                    pe.wait_ge(lin_taken, turn["ada", layer, r] + 1)
                bank = lin_bank(("mod", layer))
                for j in range(3):
                    if j:
                        pe.wait_ge(rows_turned, 2 * layer + j)
                    q = slice(32 * j, 32 * j + 2)
                    for r in range(2):
                        for c in range(4):
                            t = 12 * r + 4 * j + c
                            m = tr(bank[:, 2 * t:2 * t + 2], S[q, r, 1 + c * P:1 + (c + 1) * P], t0("ident")[q, 32 * j:32 * j + 2])
                    if j < 2:
                        m.then_inc(rows_turned, 1)
                m.then_inc(lin_ready, 1)

            def rotate(key, src, n_done):
                pe.wait_ge(lin_taken, n_done + 1)
                mm(aux_bank(("rot", key))[:, 0:SEQ], cb[:, 0:P], src, start=True, stop=True).then_inc(aux_ready, 1)

            def turn_tile(key, n_done, v, n):
                pe.wait_ge(lin_taken, n_done + 1)
                bank = aux_bank(("turn", key))
                for j in range(n):
                    m = tr(bank[:, j * P:(j + 1) * P], SQ[:, v % 2, j * P:(j + 1) * P], t0("ident"))
                m.then_inc(aux_ready, 1)

            def attention(name):
                items = STAGES[name]
                for i in range(len(items) + 2):
                    if i < len(items):
                        it, s = items[i], scored_first[name] + i
                        if s >= 2:
                            pe.wait_ge(scores_taken, s - 1)
                        a = 0
                        for j, k in enumerate(it["ks"]):
                            q = it["qs"][j] if "qs" in it else it["q"]
                            m = mm(sc[:, s % 2, a:a + k.shape[-1]], q, k, start=True, stop=True, skip_group_check=True)
                            a += k.shape[-1]
                        m.then_inc(scores_ready, 1)
                    if 1 <= i <= len(items):
                        it, g = items[i - 1], first[name] + i - 1
                        pe.wait_ge(probs_ready, g + 1)
                        nk = it["w"] // P
                        for j in range(nk):
                            if j % 4 == 0:
                                bank = lin_bank()
                            m = tr(bank[:, j % 4 * P:(j % 4 + 1) * P], S[:, g % 2, 1 + j * P:1 + (j + 1) * P], t0("ident"))
                            if j % 4 == 3 or j == nk - 1:
                                m.then_inc(lin_ready, 1)
                        T_LAST[g] = at["lin"] - 1
                    if i >= 2:
                        it, g = items[i - 2], first[name] + i - 2
                        pe.wait_ge(lin_taken, T_LAST[g] + 1)
                        V_TURN[g] = at["aux"]
                        bank = aux_bank()
                        nk = len(it["vs"])
                        for j, v in enumerate(it["vs"]):
                            m = mm(bank[:, 0:v.shape[-1]], PT[:, g % 2, j * P:(j + 1) * P], v, start=j == 0, stop=j == nk - 1)
                        m.then_inc(aux_ready, 1)

            def outputs_turned(name, key, base, ns):
                pe.wait_ge(aux_taken, V_TURN[first[name] + len(STAGES[name]) - 1] + 1)
                for j in range(4):
                    bank = aux_bank((key, j))
                    for t in range(ns * TT):
                        m = tr(bank[:, t * P:(t + 1) * P], O[:, base + t, j * P:(j + 1) * P], t0("ident"))
                    m.then_inc(aux_ready, 1)

            pe.wait_ge(consts_in, 4 * 16)
            mean_square("l0", 2)
            pe.wait_ge(silu_c, 1)
            modulation(0)
            for layer in range(DEPTH):
                L = f"l{layer}"
                ns = 2 if layer == 0 else 1
                if layer:
                    mean_square(L, 2)
                later, v = None, 0
                for t in range(IN1):
                    both = layer == 0 or t in (KK, VV)
                    n = 512 if both else 256
                    bank = lin_bank((L, t))
                    product(bank[:, 0:n], (lambda k: H[:, 0:2, k, :]) if both else (lambda k: H[:, 0, k, :]),
                            (lambda k: pe.wait_ge(shifted[L], 2 * k + 2)) if t == 0 else None).then_inc(lin_ready, 1)
                    if later:
                        later()
                        later = None
                    if t == KK or QQ <= t < FU:
                        later = lambda t=t: rotate((L, t), P1[:, t, 0, :], turn[L, t])
                    elif t == VV or FU <= t < GA:
                        later = lambda t=t, v=v: turn_tile((L, t), turn[L, t], v, 4 if t == VV else ns * TT)
                        v += 1
                n = ns * SEQ
                pe.wait_ge(conv_done, layer + 1)
                bank = aux_bank((L, "mean"))
                for t in range(2):
                    m = mm(bank[:, 0:n], t0("ones_c"), CV[:, t, 0:ns, :], start=t == 0, stop=t == 1)
                m.then_inc(aux_ready, 1)
                pe.wait_ge(aux_taken, turn["turn", (L, FU + 1)] + 1)
                for s in range(ns):
                    for f in range(2):
                        bank = aux_bank((L, "dft", s, f))
                        for t in range(TT):
                            m = mm(bank[:, :], FT[:, s * TT + t, f * P:(f + 1) * P], t1(f"dft{t}"), start=t == 0, stop=t == 1)
                        m.then_inc(aux_ready, 1)
                pe.wait_ge(conv_sq, layer + 1)
                bank = lin_bank((L, "var"))
                for t in range(2):
                    m = mm(bank[:, 0:n], t0("ones_c"), SQ[:, t, 0:n], start=t == 0, stop=t == 1)
                m.then_inc(lin_ready, 1)
                for f in range(2):
                    pe.wait_ge(aux_taken, turn[L, "dft", ns - 1, f] + 1)
                    bank = aux_bank((L, "mix", f))
                    mm(bank[:, 0:n], t1("bc"), CS[:, f, 0:ns, 0:256], start=True, stop=False)
                    mm(bank[:, 0:n], t1("bs"), CS[:, f, 0:ns, 256:512], start=False, stop=True).then_inc(aux_ready, 1)
                pe.wait_ge(aux_taken, turn[L, "mix", 1] + 1)
                for t in range(2):
                    bank = aux_bank((L, "four", t))
                    for f in range(2):
                        m = mm(bank[:, 0:n], wfour[:, layer, f, t * P:(t + 1) * P], FF[:, f, 0:ns, :], start=f == 0, stop=f == 1)
                    m.then_inc(aux_ready, 1)
                if layer == 0:
                    modulation(1)
                pe.wait_ge(roped, 5 * (layer + 1))
                attention(L)
                outputs_turned(L, (L, "o"), 0, ns)
                pe.wait_ge(aux_taken, turn[(L, "o"), 3] + 1)
                for t in range(KT):
                    bank = aux_bank((L, "out", t))
                    product(bank[:, 0:n], lambda k: YB[:, k, 0:ns, :]).then_inc(aux_ready, 1)
            mean_square("fin1", 1)
            mean_square("mix", 1)
            mean_square("mem", 1)

            pe.wait_ge(c2_in_s, 16)
            later, v, ropes = None, 0, 5 * DEPTH
            for t in range(IN2):
                bank = lin_bank(("in2", t))
                product(bank[:, 0:SEQ], lambda k: H[:, 0, k, :],
                        (lambda k: pe.wait_ge(normed["mix"], k + 1)) if t == 0 else None).then_inc(lin_ready, 1)
                if later:
                    later()
                    later = None
                if t == AV or BV <= t < MQ:
                    later = lambda t=t, v=v: turn_tile(("in2", t), turn["in2", t], v, TT)
                    v += 1
                elif t < MQ:
                    later = lambda t=t: rotate(("in2", t), PR[:, AT[t], :], turn["in2", t])
                    ropes += 1
                if t == BQ:
                    bank = aux_bank("iw")
                    for tt in range(TT):
                        for k in range(KT):
                            m = mm(bank[:, 4 * tt:4 * tt + 4], H[:, 0, k, tt * P:(tt + 1) * P], wsmall[:, k, 20:24],
                                   start=k == 0, stop=k == KT - 1)
                    m.then_inc(aux_ready, 1)
                if t == BQ + 2:
                    pe.wait_ge(roped, 5 * DEPTH + 8)
                    for tt in range(TT):
                        s, w = IDX_TURN + tt, P * (tt + 1)
                        pe.wait_ge(scores_taken, s - 1)
                        for h in range(4):
                            r = slice(h % 2 * HD, h % 2 * HD + HD)
                            a = h % 2 * 512 + h // 2 * w
                            m = mm(sc[:, s % 2, a:a + w], PR[r, AT[IQ] + h // 2, tt * P:(tt + 1) * P],
                                   PR[r, AT[IK], 0:w], start=True, stop=True, skip_group_check=True)
                        m.then_inc(scores_ready, 1)
            for t in range(MK, MK + 8):
                bank = lin_bank(("in2", t))
                product(bank[:, 0:SEQ], lambda k: H[:, 1, k, :],
                        (lambda k: pe.wait_ge(normed["mem"], k + 1)) if t == MK else None).then_inc(lin_ready, 1)
                if later:
                    later()
                    later = None
                if t >= MV:
                    later = lambda t=t, v=v: turn_tile(("in2", t), turn["in2", t], v, TT)
                    v += 1
            later()
            pe.wait_ge(roped, ropes)
            pe.wait_ge(aux_taken, turn["turn", ("in2", MV + 3)] + 1)
            pe.wait_ge(idx_mask, 1)
            attention("a")
            outputs_turned("a", "oa", 0, 1)
            attention("b")
            outputs_turned("b", "ob", 2, 1)
            attention("m")
            outputs_turned("m", "om", 0, 1)
            for mp in range(4):
                for t in (2 * mp, 2 * mp + 1):
                    for b in range(3):
                        bank = lin_bank(("gate", t, b))
                        product(bank[:, 0:SEQ], lambda k: H[:, 0, k, :]).then_inc(lin_ready, 1)
                if mp == 0:
                    pe.wait_ge(aux_taken, turn["om", 3] + 1)
                for b in range(3):
                    w = block_of_weights()
                    for i in range(2):
                        bank = aux_bank(("branch", 2 * mp + i, b))
                        for k in range(4):
                            m = mm(bank[:, 0:SEQ], w[:, 4 * i + k, :], Y[:, 4 * b + k, :], start=k == 0, stop=k == 3)
                            if k < 3:
                                frees(m)
                        m.then_inc(aux_ready, 1)
            for t in range(KT):
                bank = aux_bank(("out2", t))
                product(bank[:, 0:SEQ], lambda k: H[:, 1, k, :],
                        (lambda k: pe.wait_ge(merged, k + 1)) if t == 0 else None).then_inc(aux_ready, 1)
            mean_square("ffn", 1)
            bank = aux_bank("route")
            for tt in range(TT):
                for k in range(KT):
                    pe.wait_ge(normed["ffn"], k + 1)
                    m = mm(bank[:, 20 * tt:20 * tt + 20], H[:, 0, k, tt * P:(tt + 1) * P], wsmall[:, k, 0:20],
                           start=k == 0, stop=k == KT - 1)
            m.then_inc(aux_ready, 1)
            for tt in range(TT):
                for half in range(2):
                    bank = lin_bank()
                    for k in range(4):
                        m = tr(bank[:, k * P:(k + 1) * P], H[:, 0, 4 * half + k, tt * P:(tt + 1) * P], t0("ident"))
                    m.then_inc(lin_ready, 1)
            pe.wait_ge(places_from, 1)
            bank = aux_bank("places")
            one, before = t0("tri")[:, P:2 * P], t0("tri")[:, 0:P]
            mm(bank[:, 0:16], before, MK1[:, 0, :], start=True, stop=True)
            mm(bank[:, 16:32], before, MK1[:, 1, :], start=True, stop=False)
            mm(bank[:, 16:32], one, MK1[:, 0, :], start=False, stop=True)
            mm(bank[:, 32:48], one, MK1[:, 0, :], start=True, stop=False)
            mm(bank[:, 32:48], one, MK1[:, 1, :], start=False, stop=True).then_inc(aux_ready, 1)

            def gather():
                for half in range(2):
                    for k in range(4):
                        for tt in range(TT):
                            a = 4 * half + k
                            m = mm(sc[:, 0, a * P:(a + 1) * P], TK[:, tt, a * P:(a + 1) * P], SEL[:, tt, :],
                                   start=tt == 0, stop=tt == TT - 1)
                    m.then_inc(e_gathered, 1)

            def scatter(i):
                pe.wait_ge(e_y_lo, i + 1)
                pe.wait_ge(e_y_hi, i + 1)
                pe.wait_ge(e_swt_in, i + 1)
                for q in range(4):
                    if q >= 2:
                        pe.wait_ge(e_added, 4 * i + q - 1)
                    for b in range(2):
                        a = 2 * q + b
                        m = mm(sc[:, 1, q % 2 * 512 + b * SEQ:q % 2 * 512 + (b + 1) * SEQ], YS[:, a * P:(a + 1) * P], SWT,
                               start=True, stop=True)
                    m.then_inc(e_out, 1)

            pe.wait_ge(aux_taken, at["aux"])
            pe.wait_ge(lin_taken, at["lin"])
            pe.wait_ge(e_sel, 1)
            gather()
            assert at["owed"] == 0
            at["owed"] = 1
            pe.wait_ge(pairs_in, 1)
            n_pairs = pe.value_load(NP[0:1, 0:1], min_val=PAIRS, max_val=PAIRS * PASSES)
            with pe.Fori(0, n_pairs) as i:
                def unit(j):
                    u = BASE + j
                    pe.wait_ge(unit_in[u % SLOTS], 16 * (u // SLOTS + 1) + 16 * (PAIR_UNITS // SLOTS) * i)
                    return ring[:, u % SLOTS, :, :].rearrange("p b (k n) -> p (b k) n", n=512)

                def both(bank, left, n_k, j0, done):
                    for half in range(n_k // 4):
                        w = [unit(j0 + 2 * half + x) for x in range(2)]
                        for k in range(4):
                            for x in range(2):
                                c = slice(x * CAP, (x + 1) * CAP)
                                last = 4 * half + k == n_k - 1
                                m = mm(bank[c, :], left[:, 4 * half + k, c], w[x][:, k, :], start=half + k == 0, stop=last)
                                if not (last and x == 1):
                                    frees(m)
                        at["owed"] += 2
                    m.then_inc(done, 1)

                for half in range(2):
                    pe.wait_ge(e_te_in, 2 * i + half + 1)
                both(lin[0], TE, KT, 0, e_first)
                both(lin[1], TE, KT, 4, e_third)
                scatter(i)
                pe.wait_ge(e_sel, i + 2)
                gather()
                pe.wait_ge(e_hidden, i + 1)
                for k in range(4):
                    m = tr(aux[0][:, k * P:(k + 1) * P], HS[:, k * P:(k + 1) * P], t0("ident"))
                m.then_inc(e_turned, 1)
                pe.wait_ge(e_hid_in, i + 1)
                both(aux[1], HT, 4, 8, e_y)
                both(aux[0], HT, 4, 10, e_y)
                pe.wait_ge(e_sw, i + 1)
                pe.wait_ge(e_added, 4 * i + 4)
                for tt in range(TT):
                    m = tr(sc[:, 1, 512 + tt * P:512 + (tt + 1) * P], SW[:, tt, :], t0("ident"))
                    if tt == 0:
                        frees(m)
                m.then_inc(e_swt, 1)
                assert at["owed"] == 1
            scatter(n_pairs)
            bank = lin[0]
            turn["fin2"] = at["lin"]
            at["lin"] += 1
            for k in range(KT):
                pe.wait_ge(sq_ready, at["sq"] * KT + k + 1)
                m = mm(bank[:, 0:SEQ], t0("ones_d"), SQ[:, k % 2, 0:SEQ], start=k == 0, stop=k == KT - 1)
                m.then_inc(lin_ready if k == KT - 1 else sq_used, 1)

        @block.sync
        def _(sp):
            def load(u, slot):
                src = w_stream[u] if isinstance(u, int) else w_stream[bass.ds(u, 1)].rearrange("u p b n -> (u p) b n")
                sp.dma_start(ring[:, slot, :, :], src).then_inc(unit_in[slot], 16)

            rounds = N_UNITS // SLOTS
            for slot in range(SLOTS):
                load(slot, slot)
            with sp.Fori(1, rounds) as r:
                for slot in range(SLOTS):
                    sp.wait_ge(unit_free, SLOTS * r + slot - SLOTS + 1)
                    load(SLOTS * r + slot, slot)
            for u in range(rounds * SLOTS, N_UNITS):
                sp.wait_ge(unit_free, u - SLOTS + 1)
                load(u, u % SLOTS)
            sp.wait_ge(pairs_in, 1)
            n_pairs = sp.value_load(NP[0:1, 0:1], min_val=PAIRS, max_val=PAIRS * PASSES)
            with sp.If(n_pairs > PAIRS):
                with sp.Fori(PAIRS, n_pairs) as i:
                    for j in range(PAIR_UNITS):
                        sp.wait_ge(unit_free, BASE + PAIR_UNITS * i + j - SLOTS + 1)
                        load(BASE + PAIR_UNITS * (i % PAIRS) + j, (BASE + j) % SLOTS)
            sp.wait_ge(normed["fin2"], KT)
            sp.dma_start(out, H[:, 0, :, :]).then_inc(out_s, 16)
            sp.wait_ge(out_s, 16)

        @block.scalar
        def _(act):
            fn = nc.scalar.activation
            at = {"lin": 0, "sq": 0}

            def take():
                n = at["lin"]
                at["lin"] += 1
                act.wait_ge(lin_ready, n + 1)
                return lin[n % 2]

            def squares(name, src, ns, ready):
                for k in range(KT):
                    ready(k)
                    if k >= 2:
                        act.wait_ge(sq_used, (KT - 1) * at["sq"] + k - 1)
                    fn(SQ[:, k % 2, 0:ns * SEQ], src(k), ACT.Square).then_inc(sq_ready, 1)
                at["sq"] += 1
                if name == "mem":
                    act.wait_ge(normed["mix"], 1)
                fn(RS[:, 0:ns * SEQ], take()[:, 0:ns * SEQ], ACT.Sqrt, bias=col("eps")).then_inc(lin_taken, 1)

            def attention(name):
                items = STAGES[name]
                sinks = sum(x["sink"] is not None for n_, its in STAGES.items() for x in its if first[n_] < first[name])
                for i in range(len(items) + 1):
                    if i < len(items):
                        it, g = items[i], first[name] + i
                        act.wait_ge(bias_ready, g + 1)
                        lo = 1
                        if it["sink"] is not None:
                            sinks += 1
                            act.wait_ge(sink_in, sinks)
                            lo = 0
                        p = S[:, g % 2, lo:1 + it["w"]]
                        fn(p, p, ACT.Exp, bias=ST[:, g % 4, 1:2], scale=it["scale"],
                           accum_out=ST[:, g % 4, 2:3]).then_inc(probs_ready, 1)
                    if i >= 1:
                        it, g = items[i - 1], first[name] + i - 1
                        if g >= 2:
                            act.wait_ge(aux_ready, V_TURN[g - 2] + 1)
                        for a in range(0, it["w"], 512):
                            b = min(a + 512, it["w"])
                            fn(PT[:, g % 2, a:b], take()[:, 0:b - a], ACT.Copy).then_inc(lin_taken, 1)

            act.dma_start(cols[:, :], cols_in).then_inc(cols_in_s, 16)
            act.dma_start(X[:, :, :, :], x_in).then_inc(x_in_s, 16)
            act.dma_start(c0[:, :], c0_in).then_inc(consts_in, 16)
            act.dma_start(cb[:, :], c1_in).then_inc(consts_in, 16)
            act.dma_start(wfour[:, :, :, :], wfour_in).then_inc(consts_in, 16)
            act.dma_start(wsmall[:, :, :], wsmall_in).then_inc(consts_in, 16)
            act.wait_ge(cols_in_s, 16)
            fn(SC.rearrange("p k s -> p (k s)"), col("c", 0, 16), ACT.Silu).then_inc(silu_c, 1)

            def modulation(layer):
                for r in range(2):
                    bank = take()
                    for j in range(3):
                        q = slice(32 * j, 32 * j + 2)
                        m = fn(S[q, r, 1:513], bank[q, :], ACT.Copy)
                    m.then_inc(lin_taken, 1)
                fn(MOD[:, layer, :, :].rearrange("p t s -> p (t s)"), take()[:, 0:2 * ADA], ACT.Copy).then_inc(lin_taken, 1)

            for layer in range(DEPTH):
                L = f"l{layer}"
                ns = 2 if layer == 0 else 1
                last = (lambda k: None) if layer == 0 else (lambda k: act.wait_ge(aux_taken, turn["l0", "out", k] + 1))
                if layer == 0:
                    act.wait_ge(x_in_s, 16)
                squares(L, lambda k: X[:, 0:2, k, :], 2, last)
                if layer == 0:
                    modulation(0)
                for k in range(KT):
                    for s in range(2):
                        act.wait_ge(normed[L], 2 * k + s + 1)
                        fn(H[:, s, k, :], H[:, s, k, :], ACT.Identity, bias=MOD[:, layer, k, s:s + 1]).then_inc(shifted[L], 1)
                v = 0
                for t in range(IN1):
                    n = 2 if layer == 0 or t in (KK, VV) else 1
                    bank = take()[:, 0:n * SEQ]
                    if t == VV or FU <= t < GA:
                        if v >= 2:
                            act.wait_ge(aux_ready, turn["turn", (L, FU + v - 3 if v > 2 else VV)] + 1)
                        fn(SQ[:, v % 2, 0:n * SEQ], bank, ACT.Copy).then_inc(lin_taken, 1)
                        v += 1
                    else:
                        f = ACT.Sigmoid if t < CA else ACT.Silu if t >= GA else ACT.Copy
                        fn(P1[:, t, 0:n, :], bank, f).then_inc(lin_taken, 1)
                n = ns * SEQ
                fn(RS[:, 0:n], take()[:, 0:n], ACT.Sqrt, bias=col("eps")).then_inc(lin_taken, 1)
                act.wait_ge(conv_norm, layer + 1)
                for t in range(2):
                    v_ = CV[:, t, 0:ns, :]
                    fn(v_, v_, ACT.Silu, bias=col(f"ln_b{layer}", t), scale=col(f"ln_g{layer}", t)).then_inc(conv_act, 1)
                if layer == 0:
                    modulation(1)
                attention(L)
            squares("fin1", lambda k: X[:, 0, k, :], 1, lambda k: act.wait_ge(aux_taken, turn["l1", "out", k] + 1))
            act.dma_start(cb[:, 0:N_C2], c2_in).then_inc(c2_in_s, 16)
            act.dma_start(X[:, 1, :, :], mem_in).then_inc(mem_in_s, 16)
            squares("mix", lambda k: X[:, 0, k, :], 1, lambda k: act.wait_ge(normed["fin1"], k + 1))
            squares("mem", lambda k: X[:, 1, k, :], 1, lambda k: act.wait_ge(mem_in_s, 16))
            v = 0
            turned = [AV] + list(range(BV, MQ)) + list(range(MV, MV + 4))
            for t in range(MV + 4):
                bank = take()[:, 0:SEQ]
                if t in turned:
                    if v >= 2:
                        act.wait_ge(aux_ready, turn["turn", ("in2", turned[v - 2])] + 1)
                    fn(SQ[:, v % 2, 0:SEQ], bank, ACT.Copy).then_inc(lin_taken, 1)
                    v += 1
                else:
                    fn(PR[:, AT[t], :], bank, ACT.Copy).then_inc(lin_taken, 1)
            for name in "abm":
                attention(name)
            for t in range(KT):
                for b in range(3):
                    fn(PR[:, 3 * t + b, :], take()[:, 0:SEQ], ACT.Sigmoid, bias=col("b_gate", b * KT + t)).then_inc(lin_taken, 1)
            squares("ffn", lambda k: X[:, 0, k, :], 1, lambda k: act.wait_ge(aux_taken, turn["out2", k] + 1))
            for tt in range(TT):
                for half in range(2):
                    fn(TK[:, tt, 512 * half:512 * half + 512], take()[:, :], ACT.Copy).then_inc(lin_taken, 1)
            act.wait_ge(route_a, 1)
            for tt in range(TT):
                r = RO[:, tt, :]
                fn(r[:, 44:48], r[:, 0:4], ACT.Exp, bias=r[:, 24:25], accum_out=r[:, 25:26])
                fn(r[:, 26:27], r[:, 27:28], ACT.Exp, bias=r[:, 28:29]).then_inc(route_b, 1)
            act.wait_ge(pairs_in, 1)
            n_pairs = act.value_load(NP[0:1, 0:1], min_val=PAIRS, max_val=PAIRS * PASSES)

            def gathered(n):
                for half in range(2):
                    act.wait_ge(e_gathered, 2 * n + half + 1)
                    fn(TE[:, 4 * half:4 * half + 4, :].rearrange("p k n -> p (k n)"), sc[:, 0, half * 512:(half + 1) * 512],
                       ACT.Copy).then_inc(e_te_in, 1)

            gathered(0)
            with act.Fori(0, n_pairs) as i:
                act.wait_ge(e_first, i + 1)
                fn(SG, lin[0][:, :], ACT.Silu).then_inc(e_silu, 1)
                gathered(i + 1)
                act.wait_ge(e_turned, i + 1)
                fn(HT.rearrange("p k n -> p (k n)"), aux[0][:, :], ACT.Copy).then_inc(e_hid_in, 1)
                act.wait_ge(e_y, 2 * i + 1)
                fn(YS[:, 0:512], aux[1][:, :], ACT.Copy).then_inc(e_y_lo, 1)
            act.wait_ge(e_added, 4 * n_pairs + 4)
            for k in range(KT):
                if k >= 2:
                    act.wait_ge(sq_used, (KT - 1) * at["sq"] + k - 1)
                fn(SQ[:, k % 2, 0:SEQ], X[:, 0, k, :], ACT.Square).then_inc(sq_ready, 1)
            act.wait_ge(lin_ready, at["lin"] + 1)
            fn(RS[:, 0:SEQ], lin[0][:, 0:SEQ], ACT.Sqrt, bias=col("eps")).then_inc(lin_taken, 1)

        @block.gpsimd
        def _(pool):
            nc.gpsimd.memset(U[:, :, :, 0:PAD], 0.0)
            nc.gpsimd.memset(U[:, :, :, PAD + SEQ:], 0.0).then_inc(pads_ready, 1)
            pool.wait_ge(sinks_ready, 1)
            n = 0
            for name in ("l0", "l1"):
                for i, it in enumerate(STAGES[name]):
                    g = first[name] + i
                    if g >= 2:
                        pool.wait_ge(probs_ready, g - 1)
                    nc.gpsimd.tensor_copy(S[:, g % 2, 0:1], SK[:, it["sink"]:it["sink"] + 1]).then_inc(sink_in, 1)

        @block.vector
        def _(dve):
            v = nc.vector
            at = {"aux": 0, "step": 0}

            def step(ins):
                at["step"] += 1
                ins.then_inc(dve_step, 1)
                return at["step"]

            def after(n):
                dve.wait_ge(dve_step, n)

            def take(key=None):
                n = at["aux"]
                assert key is None or turn[key] == n, (key, turn[key], n)
                at["aux"] += 1
                dve.wait_ge(aux_ready, n + 1)
                return aux[n % 2]

            def norm(name, src, dst, gain, ns):
                n = ns * SEQ
                dve.wait_ge(lin_taken, turn[name] + 1)
                after(step(v.reciprocal(RI[:, 0:n], RS[:, 0:n])))
                for k in range(KT):
                    for s in range(ns):
                        v.scalar_tensor_tensor(out=dst(k, s), in0=src(k, s), scalar=gain(k, s), in1=RI[:, s * SEQ:(s + 1) * SEQ],
                                               op0=ALU.mult, op1=ALU.mult).then_inc(normed[name], 1)
                dve.wait_ge(normed[name], ns * KT)

            def modulation(layer):
                dve.wait_ge(lin_taken, turn["mod", layer] + 1)
                for s in range(2):
                    n = step(v.tensor_tensor(MOD[:, layer, :, s], MOD[:, layer, :, s], col(f"b_ada{layer}", 0, ADA), ALU.add))
                return n

            def gains(layer, n):
                after(n)
                for s in range(2):
                    n = step(v.scalar_tensor_tensor(out=GS[:, :, s], in0=MOD[:, layer, KT:2 * KT, s], scalar=1.0,
                                                    in1=col(f"norm_g{layer}", 0, KT), op0=ALU.add, op1=ALU.mult))
                after(n)

            ropes = [0]

            def rope(key, x, cos, sin):
                b = ropes[0] % 2
                ropes[0] += 1
                bank = take(("rot", key))
                v.tensor_tensor(RT[:, b, :], bank[:, 0:SEQ], sin, ALU.mult).then_inc(aux_taken, 1)
                n = step(v.tensor_tensor(x, x, cos, ALU.mult))
                after(n)
                v.tensor_tensor(x, x, RT[:, b, :], ALU.add).then_inc(roped, 1)

            def attention(name):
                items = STAGES[name]
                for i in range(len(items) + 2):
                    if i < len(items):
                        it, s, g = items[i], scored_first[name] + i, first[name] + i
                        if g >= 2:
                            dve.wait_ge(lin_ready, T_LAST[g - 2] + 1)
                        dve.wait_ge(scores_ready, s + 1)
                        w, st = it["w"], ST[:, g % 4, :]
                        most = SK[:, it["sink"]:it["sink"] + 1] if it["sink"] is not None else -3e38
                        v.tensor_tensor_reduce(out=S[:, g % 2, 1:1 + w], in0=sc[:, s % 2, 0:w], in1=it["mask"], scale=1.0,
                                               scalar=most, op0=ALU.add, op1=ALU.max, accum_out=st[:, 0:1]).then_inc(scores_taken, 1)
                        dve.wait_ge(scores_taken, s + 1)
                        v.tensor_scalar(st[:, 1:2], st[:, 0:1], -it["scale"], None, ALU.mult).then_inc(bias_ready, 1)
                    if i >= 2:
                        it, g = items[i - 2], first[name] + i - 2
                        st = ST[:, g % 4, :]
                        dve.wait_ge(probs_ready, g + 1)
                        after(step(v.reciprocal(st[:, 3:4], st[:, 2:3])))
                        bank = take()
                        v.tensor_scalar(it["o"], bank[:, 0:it["o"].shape[-1]], st[:, 3:4], None, ALU.mult).then_inc(aux_taken, 1)

            dve.wait_ge(cols_in_s, 16)
            v.tensor_scalar(SK[:, :], col("sink", 0, 16), float(HD) ** 0.5, None, ALU.mult).then_inc(sinks_ready, 1)
            n_mod = modulation(0)
            for layer in range(DEPTH):
                L = f"l{layer}"
                ns = 2 if layer == 0 else 1
                n = ns * SEQ
                gains(layer, n_mod)
                if layer == 0:
                    dve.wait_ge(x_in_s, 16)
                norm(L, lambda k, s: X[:, s, k, :], lambda k, s: H[:, s, k, :], lambda k, s: GS[:, k, s:s + 1], 2)

                dve.wait_ge(lin_taken, turn[L, CA + 1] + 1)
                dve.wait_ge(pads_ready, 1)
                last = {}
                for t in range(2):
                    last[t] = step(v.tensor_tensor(U[:, t, 0:ns, PAD:PAD + SEQ], P1[:, CA + t, 0:ns, :], P1[:, CB + t, 0:ns, :], ALU.mult))
                taps = [(k, t) for k in range(CONV_K) for t in range(2)]

                def conv(n_taps):
                    for _ in range(min(n_taps, len(taps))):
                        k, t = taps.pop(0)
                        after(last[t])
                        w, u = col(f"conv_w{layer}", t * CONV_K + k), U[:, t, 0:ns, k:k + SEQ]
                        if k == 0:
                            ins = v.tensor_scalar(CV[:, t, 0:ns, :], u, w, col(f"conv_b{layer}", t), ALU.mult, ALU.add)
                        else:
                            ins = v.scalar_tensor_tensor(out=CV[:, t, 0:ns, :], in0=u, scalar=w, in1=CV[:, t, 0:ns, :],
                                                         op0=ALU.mult, op1=ALU.add)
                        if taps:
                            last[t] = step(ins)
                        else:
                            ins.then_inc(conv_done, 1)

                for t in [KK, VV, QQ, QQ + 1, QQ + 2, QQ + 3, FU, FU + 1]:
                    conv(7)
                    if t == VV:
                        bank = take(("turn", (L, t)))
                        v.tensor_copy(VT.rearrange("p t n -> p (t n)"), bank[:, :]).then_inc(aux_taken, 1)
                    elif t >= FU:
                        bank = take(("turn", (L, t)))
                        v.tensor_copy(FT[:, 0:2 * ns, (t - FU) * P:(t - FU + 1) * P],
                                      bank[:, 0:n].rearrange("p (j n) -> p j n", n=P)).then_inc(aux_taken, 1)
                    else:
                        dve.wait_ge(lin_taken, turn[L, t] + 1)
                        rope((L, t), P1[:, t, 0, :], t1("cos"), t1("sin"))
                conv(len(taps))
                bank = take((L, "mean"))
                for t in range(2):
                    ins = v.tensor_tensor(CV[:, t, 0:ns, :], CV[:, t, 0:ns, :], bank[:, 0:n].rearrange("p (s n) -> p s n", s=ns), ALU.subtract)
                ins.then_inc(aux_taken, 1)
                dve.wait_ge(aux_taken, at["aux"])
                for t in range(2):
                    ins = v.tensor_tensor(SQ[:, t, 0:n].rearrange("p (s n) -> p s n", s=ns), CV[:, t, 0:ns, :], CV[:, t, 0:ns, :], ALU.mult)
                ins.then_inc(conv_sq, 1)
                for s in range(ns):
                    for f in range(2):
                        v.tensor_copy(CS[:, f, s, :], take((L, "dft", s, f))[:, :]).then_inc(aux_taken, 1)
                dve.wait_ge(lin_taken, turn[L, "var"] + 1)
                after(step(v.reciprocal(RI[:, 0:n], RS[:, 0:n])))
                for t in range(2):
                    ins = v.tensor_tensor(CV[:, t, 0:ns, :], CV[:, t, 0:ns, :], RI[:, 0:n].rearrange("p (s n) -> p s n", s=ns), ALU.mult)
                ins.then_inc(conv_norm, 1)
                for f in range(2):
                    v.tensor_copy(FF[:, f, 0:ns, :], take((L, "mix", f))[:, 0:n].rearrange("p (s n) -> p s n", s=ns)).then_inc(aux_taken, 1)
                dve.wait_ge(lin_taken, turn[L, GF + 1] + 1)
                for t in range(2):
                    bank = take((L, "four", t))
                    v.scalar_tensor_tensor(out=YB[:, 6 + t, 0:ns, :], in0=bank[:, 0:n].rearrange("p (s n) -> p s n", s=ns),
                                           scalar=col(f"b_four{layer}", t), in1=P1[:, GF + t, 0:ns, :],
                                           op0=ALU.add, op1=ALU.mult).then_inc(aux_taken, 1)
                for t in range(2):
                    dve.wait_ge(conv_act, 2 * layer + t + 1)
                    v.tensor_tensor(YB[:, 4 + t, 0:ns, :], CV[:, t, 0:ns, :], P1[:, GC + t, 0:ns, :], ALU.mult)
                if layer == 0:
                    n_mod = modulation(1)
                attention(L)
                for j in range(4):
                    bank = take(((L, "o"), j))
                    v.tensor_tensor(YB[:, j, 0:ns, :], bank[:, 0:n].rearrange("p (s n) -> p s n", s=ns), P1[:, GA + j, 0:ns, :],
                                    ALU.mult).then_inc(aux_taken, 1)
                for t in range(KT):
                    bank = take((L, "out", t))
                    for s in range(ns):
                        ins = v.scalar_tensor_tensor(out=X[:, s, t, :], in0=bank[:, s * SEQ:(s + 1) * SEQ],
                                                     scalar=MOD[:, layer, 2 * KT + t, s:s + 1], in1=X[:, s, t, :],
                                                     op0=ALU.mult, op1=ALU.add)
                    ins.then_inc(aux_taken, 1)

            def plain(name, src, dst, gain):
                norm(name, lambda k, s: src[:, k, :], lambda k, s: dst[:, k, :], lambda k, s: col(gain, k), 1)

            dve.wait_ge(aux_taken, at["aux"])
            plain("fin1", X[:, 0], X[:, 0], "final_g")
            dve.wait_ge(normed["fin1"], KT)
            plain("mix", X[:, 0], H[:, 0], "g_mix")
            plain("mem", X[:, 1], H[:, 1], "g_mem")

            dve.wait_ge(c2_in_s, 16)
            for t in range(MV + 4):
                key = ("in2", t)
                if t == AV:
                    v.tensor_copy(AVT[:, :, :], take(("turn", key))[:, 0:SEQ].rearrange("p (t n) -> p t n", t=TT)).then_inc(aux_taken, 1)
                elif BV <= t < MQ:
                    v.tensor_copy(BVT[:, :, (t - BV) * P:(t - BV + 1) * P],
                                  take(("turn", key))[:, 0:SEQ].rearrange("p (t n) -> p t n", t=TT)).then_inc(aux_taken, 1)
                elif t >= MV:
                    v.tensor_copy(MVT[:, :, (t - MV) * P:(t - MV + 1) * P],
                                  take(("turn", key))[:, 0:SEQ].rearrange("p (t n) -> p t n", t=TT)).then_inc(aux_taken, 1)
                elif t < MQ:
                    dve.wait_ge(lin_taken, turn[key] + 1)
                    rope(key, PR[:, AT[t], :], t2("cos"), t2("sin"))
                if t == BQ - 1:
                    v.tensor_copy(IW[:, :, 0:4], take("iw")[:, 0:8].rearrange("p (t n) -> p t n", t=TT)).then_inc(aux_taken, 1)
                    dve.wait_ge(aux_taken, at["aux"])
                if t == BQ + 1:
                    rounds = []
                    for tt in range(TT):
                        s, w = IDX_TURN + tt, P * (tt + 1)
                        dve.wait_ge(scores_ready, s + 1)
                        n = []
                        for h in range(4):
                            a = h % 2 * 512 + h // 2 * w
                            ins = v.tensor_scalar(RL[:, h, 0:w], sc[:, s % 2, a:a + w], 0.0, IW[:, tt, h:h + 1], ALU.max, ALU.mult)
                            n = step(ins) if h < 3 else None
                        ins.then_inc(scores_taken, 1)
                        dve.wait_ge(scores_taken, s + 1)
                        x = DS[:, tt, 0:w]
                        after(step(v.tensor_tensor(x, RL[:, 0, 0:w], RL[:, 1, 0:w], ALU.add)))
                        after(step(v.tensor_tensor(x, x, RL[:, 2, 0:w], ALU.add)))
                        after(step(v.tensor_tensor(x, x, RL[:, 3, 0:w], ALU.add)))
                        after(step(v.tensor_tensor(x, x, t2(f"causal{tt}"), ALU.add)))
                if BQ + 1 <= t < BQ + 1 + TOPK // 8:
                    for tt in range(TT):
                        x = DS[:, tt, 0:P * (tt + 1)]
                        after(step(v.max(M8[:, tt, :], x)))
                        after(step(v.match_replace(x, M8[:, tt, :], x, GONE)))
                if t == BQ + 1 + TOPK // 8:
                    for tt in range(TT):
                        w = P * (tt + 1)
                        after(step(v.tensor_scalar(MA[:, tt, 0:w], DS[:, tt, 0:w], GONE, NEG, ALU.not_equal, ALU.mult)))
                        ins = v.tensor_tensor(MA[:, tt, 0:w], MA[:, tt, 0:w], t2(f"causal{tt}"), ALU.add)
                        if tt == 0:
                            step(ins)
                    ins.then_inc(idx_mask, 1)
                    dve.wait_ge(idx_mask, 1)

            for b, name in enumerate("abm"):
                attention(name)
                for j in range(4):
                    v.tensor_copy(Y[:, 4 * b + j, :], take(("o" + name, j))[:, 0:SEQ]).then_inc(aux_taken, 1)
            for mp in range(4):
                for b in range(3):
                    for t in (2 * mp, 2 * mp + 1):
                        dve.wait_ge(lin_taken, turn["gate", t, b] + 1)
                        g = PR[:, 3 * t + b, :]
                        v.tensor_tensor(g, take(("branch", t, b))[:, 0:SEQ], g, ALU.mult).then_inc(aux_taken, 1)
                dve.wait_ge(aux_taken, at["aux"])
                for t in (2 * mp, 2 * mp + 1):
                    n = step(v.tensor_tensor(PR[:, 3 * t, :], PR[:, 3 * t, :], PR[:, 3 * t + 1, :], ALU.add))
                after(n)
                for t in (2 * mp, 2 * mp + 1):
                    v.tensor_tensor(H[:, 1, t, :], PR[:, 3 * t, :], PR[:, 3 * t + 2, :], ALU.add).then_inc(merged, 1)
            for t in range(KT):
                v.tensor_tensor(X[:, 0, t, :], take(("out2", t))[:, 0:SEQ], X[:, 0, t, :], ALU.add).then_inc(aux_taken, 1)
            dve.wait_ge(aux_taken, at["aux"])
            plain("ffn", X[:, 0], H[:, 0], "g_ffn")

            bank = take("route")
            for tt in range(TT):
                r = RO[:, tt, :]
                ins = v.tensor_tensor(r[:, 0:20], bank[:, 20 * tt:20 * tt + 20], col("b_route", 0, 20), ALU.add)
                if tt == 0:
                    step(ins)
            ins.then_inc(aux_taken, 1)
            dve.wait_ge(aux_taken, at["aux"])

            def link(ins):
                after(step(ins))

            def first_max(out_, x, top, r):
                link(v.tensor_reduce(top, x, AX.X, ALU.max))
                link(v.tensor_scalar(r[:, 80:84], x, top, None, ALU.is_ge))
                link(v.tensor_tensor_scan(r[:, 84:88], r[:, 88:92], r[:, 80:84], 0.0, ALU.mult, ALU.add))
                link(v.scalar_tensor_tensor(out=out_, in0=r[:, 84:88], scalar=1.0, in1=r[:, 80:84], op0=ALU.is_le, op1=ALU.mult))

            for tt in range(TT):
                r = RO[:, tt, :]
                link(v.memset(r[:, 88:92], 1.0))
                first_max(r[:, 32:36], r[:, 0:4], r[:, 20:21], r)
                link(v.tensor_scalar(r[:, 24:25], r[:, 20:21], -1.0, None, ALU.mult))
                link(v.tensor_scalar(r[:, 36:40], r[:, 4:8], r[:, 32:33], None, ALU.mult))
                for g in range(1, 4):
                    link(v.scalar_tensor_tensor(out=r[:, 36:40], in0=r[:, 4 + 4 * g:8 + 4 * g], scalar=r[:, 32 + g:33 + g],
                                                in1=r[:, 36:40], op0=ALU.mult, op1=ALU.add))
                first_max(r[:, 48:52], r[:, 36:40], r[:, 21:22], r)
                link(v.tensor_scalar(r[:, 28:29], r[:, 21:22], -1.0, None, ALU.mult))
                link(v.scalar_tensor_tensor(out=r[:, 40:44], in0=r[:, 48:52], scalar=NEG, in1=r[:, 36:40], op0=ALU.mult, op1=ALU.add))
                first_max(r[:, 52:56], r[:, 40:44], r[:, 27:28], r)
            v.memset(RO[:, 0, 92:93], 0.0).then_inc(route_a, 1)
            for tt in range(TT):
                r = RO[:, tt, :]
                dve.wait_ge(route_b, tt + 1)
                link(v.tensor_scalar(r[:, 56:57], r[:, 26:27], 1.0, r[:, 25:26], ALU.add, ALU.mult))
                link(v.reciprocal(r[:, 57:58], r[:, 56:57]))
                link(v.tensor_scalar(r[:, 58:59], r[:, 26:27], r[:, 57:58], None, ALU.mult))
                link(v.tensor_scalar(r[:, 60:64], r[:, 48:52], r[:, 57:58], None, ALU.mult))
                link(v.scalar_tensor_tensor(out=r[:, 60:64], in0=r[:, 52:56], scalar=r[:, 58:59], in1=r[:, 60:64],
                                            op0=ALU.mult, op1=ALU.add))
                for g in range(4):
                    link(v.tensor_scalar(CM[:, tt, 4 * g:4 * g + 4], r[:, 60:64], r[:, 32 + g:33 + g], None, ALU.mult))

            link(v.tensor_scalar(MK1.rearrange("p t n -> p (t n)"), CM.rearrange("p t n -> p (t n)"), 0.0, None, ALU.is_gt))
            link(v.memset(PX[:, :, :], -1.0))
            link(v.memset(CX[:, :, :], 0.0))
            v.memset(SWT, 0.0).then_inc(e_swt_in, 1)
            v.memset(YS[:, 0:512], 0.0).then_inc(e_y_lo, 1)
            v.memset(YS[:, 512:1024], 0.0).then_inc(e_y_hi, 1)
            v.memset(RO[:, 0, 93:94], 0.0).then_inc(places_from, 1)
            bank = take("places")
            for tt in range(TT):
                link(v.scalar_tensor_tensor(out=RO[:, tt, 0:16], in0=bank[:, 16 * tt:16 * tt + 16], scalar=1.0,
                                            in1=MK1[:, tt, :], op0=ALU.add, op1=ALU.mult))
            link(v.tensor_reduce(CN[:, 0:1], bank[:, 32:48], AX.X, ALU.max))
            for n in range(1, PASSES):
                link(v.tensor_scalar(CN[:, n:n + 1], CN[:, 0:1], float(CAP * n), float(PAIRS), ALU.is_gt, ALU.mult))
            link(v.tensor_scalar(CN[:, 1:2], CN[:, 1:2], CN[:, 2:3], CN[:, 3:4], ALU.add, ALU.add))
            v.tensor_scalar(NP[:, :], CN[:, 1:2], float(PAIRS), None, ALU.add).then_inc(pairs_in, 1)
            for n in range(PASSES):
                for tt in range(TT):
                    c = slice(N_EXP * n, N_EXP * (n + 1))
                    step(v.tensor_scalar(PX[:, tt, c], RO[:, tt, 0:16], float(-1 - CAP * n), None, ALU.add))
                    link(v.tensor_copy(CX[:, tt, c], CM[:, tt, :]))
            dve.wait_ge(pairs_in, 1)
            v.memset(RO[:, 0, 94:95], 0.0).then_inc(aux_taken, 1)
            n_pairs = dve.value_load(NP[0:1, 0:1], min_val=PAIRS, max_val=PAIRS * PASSES)

            def slots(dst, n, weight, done):
                for tt in range(TT):
                    for x in range(2):
                        w = CX[:, tt, bass.ds(2 * n + x, 1)] if weight else None
                        ins = v.tensor_scalar(dst[:, tt, x * CAP:(x + 1) * CAP], t0("iota"), PX[:, tt, bass.ds(2 * n + x, 1)], w,
                                              ALU.is_equal, *([ALU.mult] if weight else []))
                ins.then_inc(done, 1)

            def add_outputs(n):
                for q in range(4):
                    dve.wait_ge(e_out, 4 * n + q + 1)
                    x = X[:, 0, 2 * q:2 * q + 2, :].rearrange("p k n -> p (k n)")
                    v.tensor_tensor(x, sc[:, 1, q % 2 * 512:q % 2 * 512 + 512], x, ALU.add).then_inc(e_added, 1)

            slots(SEL, 0, False, e_sel)
            with dve.Fori(0, n_pairs) as i:
                dve.wait_ge(e_gathered, 2 * i + 2)
                slots(SEL, i + 1, False, e_sel)
                slots(SW, i, True, e_sw)
                dve.wait_ge(e_silu, i + 1)
                dve.wait_ge(e_third, i + 1)
                v.tensor_tensor(HS, lin[1][:, :], SG, ALU.mult).then_inc(e_hidden, 1)
                add_outputs(i)
                dve.wait_ge(e_y, 2 * i + 2)
                v.tensor_copy(YS[:, 512:1024], aux[0][:, :]).then_inc(e_y_hi, 1)
                dve.wait_ge(e_swt, i + 1)
                v.tensor_copy(SWT, sc[:, 1, 512:512 + SEQ]).then_inc(e_swt_in, 1)
                dve.wait_ge(e_added, 4 * i + 4)
            add_outputs(n_pairs)
            dve.wait_ge(e_added, 4 * n_pairs + 4)
            plain("fin2", X[:, 0], H[:, 0], "g_final")


def tiles_of(w, n):
    return w.reshape(KT, P, n, P).transpose(2, 1, 0, 3).reshape(n, P, KT * P)


def rows_of(w):
    return w.reshape(4, P, 512).transpose(1, 0, 2).reshape(P, 4 * 512)


def ada_of(w):
    return np.stack([rows_of(w[h * 512:(h + 1) * 512, (3 * r + j) * 512:(3 * r + j + 1) * 512])
                     for r in range(2) for h in range(2) for j in range(3)])


def pairs_of(w):
    n = w.shape[1] // 256
    return w.reshape(4, P, n, 2, P).transpose(2, 1, 3, 0, 4).reshape(n, P, KT * P)


def per_feature(v):
    return v.reshape(-1, P).T


def kernel(**inputs):
    import concourse.bacc as bacc
    from concourse.bass_utils import run_bass_kernel_spmd

    a = {k: np.asarray(v) for k, v in inputs.items()}
    grouped = np.concatenate([np.arange(h * HD, h * HD + HD) for t in range(4) for h in (t, t + 4)])
    o = np.cumsum([0, 512, 128, 128, 512, 256, 256, 256, 256, 256])
    q, k, v, ga, ca, cbb, gc, fu, gf = (np.arange(o[i], o[i + 1]) for i in range(9))
    in1 = np.concatenate([cbb, ca, k, v, q[grouped], fu, ga, gc, gf])
    o = np.cumsum([0, 512, 128, 128, 256, 64, 4, 1536, 1536, 1536, 512])
    aq, ak, av, iq, ik, iw, bq, bk, bv, mq = (np.arange(o[i], o[i + 1]) for i in range(10))
    in2 = np.concatenate([aq[grouped], ak, av, iq, ik, ik, bq, bk, bv, mq])
    def units(*blocks):
        b = np.concatenate(blocks)
        return b.reshape(len(b) // UNIT, UNIT, P, KT * P).transpose(0, 2, 1, 3).reshape(-1, P, UNIT * KT * P)

    head = [ada_of(a["w_ada"][0]), units(tiles_of(a["w_in"][0][:, in1], IN1)), ada_of(a["w_ada"][1])]
    stream = [tiles_of(a["w_out"][0], KT), tiles_of(a["w_in"][1][:, in1], IN1), tiles_of(a["w_out"][1], KT),
              tiles_of(a["w_in_2"][0][:, in2], IN2), tiles_of(a["w_mem_kv_2"][0], 8)]
    gates = tiles_of(a["w_gate_2"][0], ADA)
    branches = [pairs_of(a["w_branch_2"][0, b]) for b in range(3)]
    for mp in range(4):
        stream += [gates[b * KT + t][None] for t in (2 * mp, 2 * mp + 1) for b in range(3)]
        stream += [branches[b][mp][None] for b in range(3)]
    stream.append(tiles_of(a["w_out_2"][0], KT))
    stream.append(np.zeros((PADDED - N_HEAD_BLOCKS, P, KT * P), np.float32))
    tail = []
    for e in range(0, N_EXP, 2):
        for w in (a["w1_2"][0], a["w3_2"][0]):
            tail += [rows_of(w[e + x, h * 512:(h + 1) * 512]) for h in range(2) for x in range(2)]
        tail += [rows_of(a["w2_2"][0, e + x][:, n * 512:(n + 1) * 512]) for n in range(2) for x in range(2)]
    w_stream = np.concatenate(head + [units(*stream), np.stack(tail)]).reshape(N_UNITS, P, UNIT, KT * P)

    cols = np.zeros((P, N_COL), np.float32)

    def put(name, x):
        cols[:, slice(*COL[name])] = x

    put("c", np.stack([per_feature(a["c"][0]), per_feature(a["c_ctx"])], 2).reshape(P, 16))
    for name in ("final_g",):
        put(name, per_feature(a[name]))
    for name, key in (("g_mix", "g_mix_2"), ("g_mem", "g_mem_2"), ("g_ffn", "g_ffn_2"), ("b_gate", "b_gate_2")):
        put(name, per_feature(a[key][0]))
    put("g_final", per_feature(a["g_final_2"]))
    for l in range(DEPTH):
        put(f"b_ada{l}", per_feature(a["b_ada"][l]))
        put(f"norm_g{l}", per_feature(a["norm_g"][l]))
        put(f"conv_w{l}", a["conv_w"][l].T.reshape(2, P, CONV_K).transpose(1, 0, 2).reshape(P, 2 * CONV_K))
        put(f"conv_b{l}", per_feature(a["conv_b"][l]))
        put(f"ln_g{l}", per_feature(a["conv_ln_g"][l]))
        put(f"ln_b{l}", per_feature(a["conv_ln_b"][l]))
        put(f"b_four{l}", per_feature(a["b_four"][l]))
    put("sink", np.broadcast_to(a["attn_sink"].reshape(1, 16), (P, 16)))
    put("b_route", np.broadcast_to(np.concatenate([a["b_group_2"][0], a["b_sub_2"][0].reshape(16)])[None], (P, 20)))
    put("eps", np.full((P, 1), EPS, np.float32))
    x_in = np.stack([a["x"][0], a["ctx"][0]]).transpose(2, 0, 1).reshape(KT, P, 2, SEQ).transpose(1, 2, 0, 3)
    mem_in = a["mem_2"][0].T.reshape(KT, P, SEQ).transpose(1, 0, 2)
    wfour = a["w_four"].reshape(DEPTH, 2, P, 256).transpose(2, 0, 1, 3)
    small = np.concatenate([a["w_group_2"][0], a["w_sub_2"][0].transpose(1, 0, 2).reshape(D, 16), a["w_in_2"][0][:, iw]], 1)
    small = small.reshape(KT, P, 24).transpose(1, 0, 2)
    c0, c1, c2 = constants()

    nc = bacc.Bacc("TRN2", target_bir_lowering=False, num_devices=1)
    arrays, args = {}, []
    for name, x in (("w_stream", w_stream), ("x_in", x_in), ("mem_in", mem_in), ("cols_in", cols), ("wfour_in", wfour),
                    ("wsmall_in", small), ("c0_in", c0), ("c1_in", c1), ("c2_in", c2)):
        arrays[name] = np.ascontiguousarray(x)
        args.append(nc.dram_tensor(name, x.shape, F32, kind="ExternalInput").ap())
    args.append(nc.dram_tensor("out", (P, KT, SEQ), F32, kind="ExternalOutput").ap())
    build(nc, *args)
    r = run_bass_kernel_spmd(nc, [arrays], core_ids=[0])
    y = r.results[0]["out"]
    return y.transpose(2, 1, 0).reshape(1, SEQ, D)
```

```python
from contextlib import ExitStack

import numpy as np
import concourse.bass as bass
from concourse import mybir

ALU = mybir.AluOpType
ACT = mybir.ActivationFunctionType
AX = mybir.AxisListType
F32 = mybir.dt.float32

P = 128
D = 1024
KT = D // P
SEQ = 256
TT = SEQ // P
DEPTH = 2
HEADS, KVH, HD = 8, 2, 64
CONV_W, CONV_K = 256, 31
PAD = CONV_K // 2
N_EXP, EPG, TOPK = 16, 4, 64
NEG = -1e30
GONE = -3e38
EPS = 1e-6

CB, CA, KK, VV, QQ, FU, GA, GC, GF = 0, 2, 4, 5, 6, 10, 12, 16, 18
IN1 = 20
AQ, AK, AV, IQ, IK, BQ, BK, BV, MQ = 0, 4, 5, 6, 8, 9, 21, 33, 45
IN2 = 49
MK, MV = IN2, IN2 + 4
AT = {AQ + i: i for i in range(5)} | {IQ + i: 5 + i for i in range(3)} | {BQ + i: 8 + i for i in range(24)} \
    | {MQ + i: 32 + i for i in range(4)} | {MK + i: 36 + i for i in range(4)}
ADA = 24
FIRST1 = list(range(GA)) + [GF, GF + 1]
GATES = IN1 - len(FIRST1)
PER_STEP = (2, 4)
ADA_STEPS = (7, 15)
NORM_ORDER = (((0, 1),), ((0,), (1,)))
MIX_ORDER = (4, 5, 6, 7, 0, 1, 2, 3)
N_HEAD_BLOCKS = DEPTH * (ADA + IN1 + KT) + IN2 + 8 + ADA + 12 + KT
PADDED = N_HEAD_BLOCKS + N_HEAD_BLOCKS % 2
UNIT = 2
SLOTS = 6
BASE = PADDED // UNIT
PAIR_UNITS = 12
PAIRS = N_EXP // 2
N_UNITS = BASE + PAIRS * PAIR_UNITS
RINGED = (SLOTS, SLOTS + 2, SLOTS)
CAP = 64
PASSES = SEQ // CAP
EC = PASSES * N_EXP + 2

COL = {}
_n = 0
for _name, _w in [("c", 16), ("b_ada0", 24), ("b_ada1", 24), ("norm_g0", 8), ("norm_g1", 8), ("final_g", 8),
                  ("g_mix", 8), ("g_mem", 8), ("g_ffn", 8), ("g_final", 8), ("b_gate", 24),
                  ("conv_w0", 62), ("conv_w1", 62), ("conv_b0", 2), ("conv_b1", 2), ("ln_g0", 2), ("ln_g1", 2),
                  ("ln_b0", 2), ("ln_b1", 2), ("b_four0", 2), ("b_four1", 2), ("sink", 16), ("b_route", 40),
                  ("eps", 1)]:
    COL[_name] = (_n, _n + _w)
    _n += _w
N_COL = _n

C0 = {}
_n = 0
for _name, _w in [("ident", 128), ("ones_d", 128), ("ones_c", 128), ("tri", 256), ("iota", CAP), ("caps", PASSES - 1),
                  ("restart", 8)]:
    C0[_name] = (_n, _n + _w)
    _n += _w
N_C0 = _n
C1 = {}
_n = 0
for _name, _w in [("rot", 128), ("cos", 256), ("sin", 256), ("dft0", 512), ("dft1", 512), ("bc", 128), ("bs", 128),
                  ("band0", 512), ("band1", 512)]:
    C1[_name] = (_n, _n + _w)
    _n += _w
N_C1 = _n
C2 = {}
_n = 0
for _name, _w in [("rot", 128), ("cos", 256), ("sin", 256), ("dil0", 384), ("dil1", 768), ("zero", 256),
                  ("causal0", 128), ("causal1", 256)]:
    C2[_name] = (_n, _n + _w)
    _n += _w
N_C2 = _n


def constants():
    f = np.float32
    c0, c1, c2 = np.zeros((P, N_C0), f), np.zeros((P, N_C1), f), np.zeros((P, N_C2), f)
    i = np.arange(P)
    c0[:, slice(*C0["ident"])] = np.eye(P)
    c0[:, slice(*C0["ones_d"])] = 1.0 / D
    c0[:, slice(*C0["ones_c"])] = 1.0 / CONV_W
    c0[:, slice(*C0["tri"])] = np.concatenate([(i[:, None] < i[None, :]), np.ones((P, P))], 1)
    c0[:, slice(*C0["iota"])] = np.arange(CAP)
    c0[:, slice(*C0["caps"])] = CAP * np.arange(1, PASSES)
    c0[:, slice(*C0["restart"])] = np.arange(8) % EPG > 0
    tok = np.arange(SEQ)

    def rope(c, table, half, pos_of):
        d = i % (2 * half)
        freq = f(10000.0) ** (-np.arange(half, dtype=f) / f(half))
        ang = (pos_of[i // (2 * half) % 2][:, tok].astype(f) * freq[d % half][:, None]).astype(f)
        c[:, slice(*table["cos"])] = np.cos(ang)
        c[:, slice(*table["sin"])] = np.sin(ang)
        rot = np.zeros((P, P), f)
        for m in range(P):
            if m % (2 * half) < half:
                rot[m + half, m] = -1.0
            else:
                rot[m - half, m] = 1.0
        c[:, slice(*table["rot"])] = rot

    rope(c1, C1, 16, np.stack([tok // 64, tok % 64]))
    rope(c2, C2, 32, np.stack([tok, tok]))
    ang = 2 * np.pi * ((tok[:, None] * tok[None, :]) % SEQ) / SEQ
    cs = np.concatenate([np.cos(ang), np.sin(ang)], 1)
    c1[:, slice(*C1["dft0"])] = cs[:P]
    c1[:, slice(*C1["dft1"])] = cs[P:]
    a64 = 2 * np.pi * ((i[:, None] * i[None, :]) % HD) / HD
    same = (i[:, None] // HD) == (i[None, :] // HD)
    norm = 1.0 / np.sqrt(SEQ * HD)
    c1[:, slice(*C1["bc"])] = np.where(same, np.cos(a64), 0) * norm
    c1[:, slice(*C1["bs"])] = np.where(same, -np.sin(a64), 0) * norm
    for t in range(TT):
        q = t * P + i[:, None]
        band = np.where(np.abs(q - tok[None, :]) <= 128, 0.0, NEG)
        c1[:, slice(*C1[f"band{t}"])] = np.concatenate([band, np.zeros((P, SEQ))], 1)
        ks = np.arange(P * (t + 1))[None, :]
        c2[:, slice(*C2[f"dil{t}"])] = np.concatenate(
            [np.where((ks <= q) & ((q - ks) % dil == 0) & (q - ks <= win), 0.0, NEG)
             for win, dil in ((128, 1), (512, 4), (2048, 16))], 1)
        c2[:, slice(*C2[f"causal{t}"])] = np.where(ks <= q, 0.0, NEG)
    return c0, c1, c2



def build(nc, w_stream, x_in, mem_in, cols_in, wfour_in, wsmall_in, c0_in, c1_in, c2_in, out):
    ctx = ExitStack()
    with ctx:
        def sb(name, shape):
            return ctx.enter_context(nc.sbuf_tensor(name, shape, F32))

        def sem(name):
            return ctx.enter_context(nc.semaphore(name))

        ring = sb("ring", [P, SLOTS, UNIT, KT * P])
        X = sb("X", [P, 2, KT, SEQ])
        H = sb("H", [P, 2, KT, SEQ])
        PR = sb("PR", [P, 2 * IN1, SEQ])
        UN = sb("UN", [P, 4352])
        Y = sb("Y", [P, 16, SEQ])
        RS = sb("RS", [P, 512])
        RI = sb("RI", [P, 512])
        MOD = sb("MOD", [P, DEPTH, ADA, 2])
        GS = sb("GS", [P, KT, 2])
        SC = sb("SC", [P, KT, 2])
        cols = sb("cols", [P, N_COL])
        SK = sb("SK", [P, DEPTH * HEADS])
        ST = sb("ST", [P, 4, 4])
        S = sb("S", [P, 3, 772])
        PT = sb("PT", [P, 3, 768])
        SQ = sb("SQ", [P, 2, 512])
        SA = sb("SA", [P, 512])
        RT = sb("RT", [P, 2, SEQ])
        c0 = sb("c0", [P, N_C0])
        cb = sb("cb", [P, N_C1])
        wfour = sb("wfour", [P, DEPTH, 2, 256])
        wsmall = sb("wsmall", [P, KT, 24])
        NP = ctx.enter_context(nc.sbuf_tensor("NP", [P, 1], mybir.dt.int32))
        IW = sb("IW", [P, TT, 8])
        M8 = sb("M8", [P, TT, 8])
        RO = sb("RO", [P, 192])
        warm = sb("warm", [P, 1])
        CM = sb("CM", [P, TT, N_EXP])

        P1 = PR.rearrange("p (t s) n -> p t s n", s=2)
        YB = Y.rearrange("p (t s) n -> p t s n", s=2)
        U = UN[:, 0:1144].rearrange("p (t s n) -> p t s n", t=2, s=2)
        CV = UN[:, 1144:2168].rearrange("p (t s n) -> p t s n", t=2, s=2)
        FT = UN[:, 2168:3192].rearrange("p (t n) -> p t n", t=4)
        VT = UN[:, 3192:3704].rearrange("p (t n) -> p t n", t=4)
        G1 = P1[:, GA:GF, :, :].rearrange("p t s n -> p (t s n)")
        CS = G1[:, 0:2048].rearrange("p (f s n) -> p f s n", f=2, s=2)
        FF = G1[:, 2048:3072].rearrange("p (f s n) -> p f s n", f=2, s=2)
        BVT = UN[:, 0:3072].rearrange("p (t n) -> p t n", t=TT)
        AVT = UN[:, 3072:3328].rearrange("p (t n) -> p t n", t=TT)
        MVT = UN[:, 3328:4352].rearrange("p (t n) -> p t n", t=TT)
        X1 = X[:, 1, :, :].rearrange("p k n -> p (k n)")
        DS = X1[:, 0:512].rearrange("p (t n) -> p t n", t=TT)
        MA = X1[:, 512:1024].rearrange("p (t n) -> p t n", t=TT)
        RL = X1[:, 1024:2048].rearrange("p (h n) -> p h n", h=4)
        E1 = PR.rearrange("p t n -> p (t n)")
        TK = E1[:, 0:2048].rearrange("p (t n) -> p t n", t=TT)
        TE = E1[:, 2048:3072].rearrange("p (k n) -> p k n", k=KT)
        SG = E1[:, 3072:3584]
        HS = E1[:, 3584:4096]
        HT = E1[:, 4096:4608].rearrange("p (k n) -> p k n", k=4)
        YS = E1[:, 4608:5632]
        SEL = E1[:, 5632:5888].rearrange("p (t n) -> p t n", t=TT)
        SW = E1[:, 5888:6144].rearrange("p (t n) -> p t n", t=TT)
        SWT = E1[:, 6144:6400]
        PX = E1[:, 6400:6400 + TT * EC].rearrange("p (t n) -> p t n", t=TT)
        CX = E1[:, 6600:6600 + TT * EC].rearrange("p (t n) -> p t n", t=TT)
        MK1 = E1[:, 6800:6832].rearrange("p (t n) -> p t n", t=TT)
        CN = E1[:, 6832:6840]

        RF, n = {}, 0
        for name, w in (("logits", 20), ("of_group", 16), ("place", 16), ("d", 5), ("e", 5), ("group", 4), ("sub", 4),
                        ("first", 4), ("rest", 4), ("second", 4), ("is_max", 4), ("count", 4), ("top_g", 1), ("top_1", 1),
                        ("top_2", 1), ("sum", 1), ("w1", 1), ("w2", 1)):
            RF[name] = RO[:, n:n + TT * w].rearrange("p (t n) -> p t n", t=TT)
            n += TT * w
        RF["of_group"] = RF["of_group"].rearrange("p t (g e) -> p t g e", g=4)

        lin = [ctx.enter_context(nc.psum_tensor(f"lin{i}", [P, 512], F32)) for i in range(2)]
        aux = [ctx.enter_context(nc.psum_tensor(f"aux{i}", [P, 512], F32)) for i in range(2)]
        sc = ctx.enter_context(nc.psum_tensor("sc", [P, 2, 1024], F32))

        flat = [UN, Y.rearrange("p t n -> p (t n)"), S.rearrange("p b n -> p (b n)"), PT.rearrange("p b n -> p (b n)"),
                E1, X1, H.rearrange("p s k n -> p (s k n)"), cb]
        ASIDE = [flat[b][:, a:a + 2048] for b, a in ((0, 0), (0, 2048), (1, 0), (1, 2048), (2, 0), (3, 0),
                                                     (5, 0), (7, 0), (4, 6912), (6, 2048))]
        aside_in = [sem(f"aside_in{i}") for i in range(len(ASIDE) // 2)]
        unit_in = [sem(f"unit_in{i}") for i in range(SLOTS)]
        unit_free = sem("unit_free")
        cols_in_s, c0_in_s, x_in_s, consts_in, mem_in_s, c2_in_s, out_s = (
            sem(n) for n in ("cols_in", "c0_in", "x_in", "consts_in", "mem_in", "c2_in", "out_stored"))
        lin_ready, lin_taken = sem("lin_ready"), sem("lin_taken")
        aux_ready, aux_taken = sem("aux_ready"), sem("aux_taken")
        scores_ready, scores_taken = sem("scores_ready"), sem("scores_taken")
        bias_ready, probs_ready, sink_in = (sem(n) for n in ("bias_ready", "probs_ready", "sink_in"))
        fill_ready, fill_taken, gates_act, gated = (sem(n) for n in ("fill_ready", "fill_taken", "gates_act", "gated"))
        probs_scaled, gates_in = sem("probs_scaled"), sem("gates_in")
        silu_c, sinks_ready, pads_ready = sem("silu_c"), sem("sinks_ready"), sem("pads_ready")
        sq_ready, sq_added = sem("sq_ready"), sem("sq_added")
        dve_step = sem("dve_step")
        roped, conv_done, conv_sq, conv_norm, conv_act = (
            sem(n) for n in ("roped", "conv_done", "conv_sq", "conv_norm", "conv_act"))
        idx_mask, merged, gains_ready = sem("idx_mask"), sem("merged"), sem("gains_ready")
        NORMS = ["l0", "l1", "fin1", "mix", "mem", "ffn", "fin2"]
        normed = {n: sem(f"normed_{n}") for n in NORMS}
        shifted = {n: sem(f"shifted_{n}") for n in ("l0", "l1")}
        route_a, route_b, places_from = sem("route_logits"), sem("route_exp"), sem("places_from")
        rows_turned = sem("rows_turned")
        (e_first, e_third, e_silu, e_hidden, e_turned, e_hid_in, e_gathered, e_te_in, e_y, e_y_lo, e_y_hi, e_sel, e_sw,
         e_swt, e_swt_in, e_out, e_added, pairs_in) = (sem(n) for n in (
             "e_first", "e_third", "e_silu", "e_hidden", "e_turned", "e_hid_in", "e_gathered", "e_te_in", "e_y", "e_y_lo",
             "e_y_hi", "e_sel", "e_sw", "e_swt", "e_swt_in", "e_out", "e_added", "pairs_in"))

        def col(name, i=0, n=1):
            a = COL[name][0] + i
            return cols[:, a:a + n]

        def t0(name):
            return c0[:, slice(*C0[name])]

        def t1(name):
            return cb[:, slice(*C1[name])]

        def t2(name):
            return cb[:, slice(*C2[name])]

        GATE_STEPS = (2, 5, 8, 11, 14, 17)

        def GT(t, b):
            return H[:, 1, 2 + 3 * t + b, :] if t < 2 else PR[:, 3 * t + b, :]

        def item(q, ks, mask, vs, bank, scale, sink=None, to=None, qs=None):
            return dict(qs=qs or [q], ks=ks, mask=mask, vs=vs, bank=bank, scale=scale, sink=sink, to=to,
                        w=sum(k.shape[-1] for k in ks))

        HALVES = [slice(0, HD), slice(HD, P)]

        def layer_items(layer):
            found = []
            for s in range(2 if layer == 0 else 1):
                for j in range(4):
                    for t in range(TT):
                        c = slice(t * P, (t + 1) * P)
                        for g, rows in enumerate(HALVES):
                            if s == 0:
                                ks, mask, chunks = [P1[rows, KK, :, :].rearrange("p s n -> p (s n)")], t1(f"band{t}"), range(4)
                            else:
                                ks, mask, chunks = [P1[rows, KK, 1, :]], t1("band0")[:, 256:512], (2, 3)
                            found.append(item(P1[rows, QQ + j, s, c], ks, mask, [VT[:, x, rows] for x in chunks],
                                              (rows, slice(0, P)), HD ** -0.5, layer * HEADS + j + 4 * g,
                                              YB[:, j, s, c]))
            return found

        def branch_a():
            return [item(PR[rows, AT[AQ] + j, t * P:(t + 1) * P], [PR[rows, AT[AK], 0:P * (t + 1)]], MA[:, t, 0:P * (t + 1)],
                         [AVT[:, x, rows] for x in range(t + 1)], (rows, slice(0, P)), HD ** -0.5,
                         to=Y[:, j, t * P:(t + 1) * P])
                    for j in range(4) for t in range(TT) for rows in HALVES]

        def branch_b():
            return [item(None, [PR[rows, AT[BK] + 4 * g + j, 0:P * (t + 1)] for g in range(3)], t2(f"dil{t}"),
                         [BVT[:, x, (4 * g + j) * P + rows.start:(4 * g + j) * P + rows.stop]
                          for g in range(3) for x in range(t + 1)],
                         (rows, slice(0, P)), HD ** -0.5, to=Y[:, 4 + j, t * P:(t + 1) * P],
                         qs=[PR[rows, AT[BQ] + 4 * g + j, t * P:(t + 1) * P] for g in range(3)])
                    for j in range(4) for t in range(TT) for rows in HALVES]

        def branch_m():
            return [item(PR[:, AT[MQ] + h, t * P:(t + 1) * P], [PR[:, AT[MK] + h, :]], t2("zero"),
                         [MVT[:, x, h * P:(h + 1) * P] for x in range(TT)], (slice(0, P), slice(t * P, (t + 1) * P)), P ** -0.5,
                         to=Y[:, 8 + h, :])
                    for h in range(4) for t in range(TT)]

        STAGES = {"l0": layer_items(0), "l1": layer_items(1), "abm": branch_a() + branch_b() + branch_m()}
        first, scored_first, n, extra = {}, {}, 0, 0
        for name, items in STAGES.items():
            if name == "abm":
                extra = TT
            first[name], scored_first[name] = n, n + extra
            n += len(items)
        IDX_TURN = first["abm"]

        turn = {}
        T_LAST = {}
        V_TURN = {}

        block = ctx.enter_context(nc.Block())

        @block.tensor
        def _(pe):
            mm, tr = nc.tensor.matmul, nc.tensor.transpose
            at = {"lin": 0, "aux": 0, "block": 0, "sq": 0, "owed": 0, "open": 0}

            def lin_bank(key=None):
                n = at["lin"]
                if n >= 2:
                    pe.wait_ge(lin_taken, n - 1)
                at["lin"] += 1
                if key is not None:
                    turn[key] = n
                return lin[n % 2]

            def aux_bank(key=None):
                n = at["aux"]
                if n >= 2:
                    pe.wait_ge(aux_taken, n - 1)
                at["aux"] += 1
                if key is not None:
                    turn[key] = n
                return aux[n % 2]

            def frees(m):
                if at["owed"]:
                    at["owed"] -= 1
                    m.then_inc(unit_free, 1)

            def unit_of_weights():
                u = at["block"] // UNIT
                at["block"] += UNIT
                at["owed"], at["open"] = at["owed"] + at["open"], 0
                pe.wait_ge(unit_in[u % SLOTS], 16 * (u // SLOTS + 1))
                return ring[:, u % SLOTS, :, :].rearrange("p b (k n) -> p (b k) n", n=512)

            def block_of_weights():
                b = at["block"]
                at["block"] += 1
                u = b // UNIT
                if b % UNIT == 0:
                    pe.wait_ge(unit_in[u % SLOTS], 16 * (u // SLOTS + 1))
                    at["owed"], at["open"] = at["owed"] + at["open"], 1
                return ring[:, u % SLOTS, b % UNIT, :].rearrange("p (k m) -> p k m", m=P)

            def product(dst, rhs, wait_k=None, order=range(KT)):
                w = block_of_weights()
                for n, k in enumerate(order):
                    if wait_k:
                        wait_k(n)
                    m = mm(dst, w[:, k, :], rhs(k), start=n == 0, stop=n == KT - 1)
                    if n < KT - 1:
                        frees(m)
                return m

            filling = {}

            def fill(layer, i):
                t, k0 = divmod(i * PER_STEP[layer], KT)
                ns = 2 - layer
                if t < GATES:
                    n = GATES * layer + t
                    if k0 == 0:
                        if n >= 2:
                            pe.wait_ge(fill_taken, n - 1)
                        filling["w"] = block_of_weights()
                    for k in range(k0, k0 + PER_STEP[layer]):
                        m = mm(sc[:, t % 2, 512:512 + ns * SEQ], filling["w"][:, k, :], H[:, 0:ns, k, :],
                               start=k == 0, stop=k == KT - 1)
                        if k < KT - 1:
                            frees(m)
                        else:
                            m.then_inc(fill_ready, 1)
                if layer == 0 and i in ADA_STEPS:
                    ada_rows(1, ADA_STEPS.index(i))
                if layer == 0 and i == ADA_STEPS[1] + 3:
                    ada_turned(1, SQ)

            def mean_square(name, ns):
                bank = lin_bank(name)
                at["sq"] += 1
                pe.wait_ge(sq_added, (KT - 1) * at["sq"])
                mm(bank[:, 0:ns * SEQ], t0("ones_d"), SA[:, 0:ns * SEQ], start=True, stop=True).then_inc(lin_ready, 1)

            def projected_out(key, rhs, n, wait_k, order=range(KT), after_2=lambda: None):
                for t in range(KT):
                    if t == 3:
                        after_2()
                    bank = aux_bank((*key, t))
                    product(bank[:, 0:n], rhs, wait_k if t == 0 else None, order).then_inc(aux_ready, 1)

            def ada_rows(layer, r):
                bank = lin_bank(("ada", layer, r))
                for half in range(2):
                    w = [] if layer == 0 else [unit_of_weights() for _ in range(3)]
                    for k, j in [(k, j) for j in range(3) for k in range(4)] if layer == 0 else \
                            [(k, j) for k in range(4) for j in range(3)]:
                        if len(w) == j:
                            w.append(unit_of_weights())
                        m = mm(bank[32 * j:32 * j + 2, :], SC[:, 4 * half + k, :], w[j][:, k, :],
                               start=half == 0 and k == 0, stop=half == 1 and k == 3)
                        if k == 3 and (half == 0 or j < 2):
                            m.then_inc(unit_free, 1)
                        elif k < 3:
                            frees(m)
                m.then_inc(lin_ready, 1)
                at["owed"] += 1

            def ada_turned(layer, rows):
                for r in range(2):
                    pe.wait_ge(lin_taken, turn["ada", layer, r] + 1)
                bank = lin_bank(("mod", layer))
                for j in range(3):
                    if j:
                        pe.wait_ge(rows_turned, 2 * layer + j)
                    q = slice(32 * j, 32 * j + 2)
                    for r in range(2):
                        for c in range(4):
                            t = 12 * r + 4 * j + c
                            m = tr(bank[:, 2 * t:2 * t + 2], rows[q, r, c * P:(c + 1) * P], t0("ident")[q, 32 * j:32 * j + 2])
                    if j < 2:
                        m.then_inc(rows_turned, 1)
                m.then_inc(lin_ready, 1)

            def rotate(key, src, n_done):
                pe.wait_ge(lin_taken, n_done + 1)
                mm(aux_bank(("rot", key))[:, 0:SEQ], cb[:, 0:P], src, start=True, stop=True).then_inc(aux_ready, 1)

            def turn_tile(key, n_done, v, n):
                pe.wait_ge(lin_taken, n_done + 1)
                bank = aux_bank(("turn", key))
                for j in range(n):
                    m = tr(bank[:, j * P:(j + 1) * P], SQ[:, v % 2, j * P:(j + 1) * P], t0("ident"))
                m.then_inc(aux_ready, 1)

            def attention(name, between):
                items = STAGES[name]
                for i in range(len(items) + 3):
                    if i < len(items):
                        it, s = items[i], scored_first[name] + i
                        if s >= 2:
                            pe.wait_ge(scores_taken, s - 1)
                        a = 0
                        for q, k in zip(it["qs"], it["ks"]):
                            m = mm(sc[:, s % 2, a:a + k.shape[-1]], q, k, start=True, stop=True, skip_group_check=True)
                            a += k.shape[-1]
                        m.then_inc(scores_ready, 1)
                    if 2 <= i < len(items) + 2:
                        it, g = items[i - 2], first[name] + i - 2
                        pe.wait_ge(probs_scaled, g + 1)
                        nk = it["w"] // P
                        for j in range(nk):
                            if j % 4 == 0:
                                bank = lin_bank()
                            m = tr(bank[:, j % 4 * P:(j % 4 + 1) * P], S[:, g % 3, 1 + j * P:1 + (j + 1) * P], t0("ident"))
                            if j % 4 == 3 or j == nk - 1:
                                m.then_inc(lin_ready, 1)
                        T_LAST[g] = at["lin"] - 1
                    if i >= 4 and i % 2 == 0:
                        pair, g = items[i - 4:i - 2], first[name] + i - 4
                        pe.wait_ge(lin_taken, T_LAST[g + 1] + 1)
                        V_TURN[g] = V_TURN[g + 1] = at["aux"]
                        bank = aux_bank()
                        nk = len(pair[0]["vs"])
                        turns = [(x, j) for j in range(nk) for x in range(2)]
                        for x, j in turns if pair[0]["bank"][0] != pair[1]["bank"][0] else sorted(turns):
                            m = mm(bank[pair[x]["bank"]], pair[x]["vs"][j], PT[:, (g + x) % 3, j * P:(j + 1) * P],
                                   start=j == 0, stop=j == nk - 1)
                        m.then_inc(aux_ready, 1)
                    between(i)

            def attended(name):
                pe.wait_ge(aux_taken, V_TURN[first[name] + len(STAGES[name]) - 1] + 1)

            pe.wait_ge(silu_c, 1)
            ada_rows(0, 0)
            pe.wait_ge(c0_in_s, 16)
            mean_square("l0", 2)
            ada_rows(0, 1)
            ada_turned(0, S[:, :, 1:513])
            for layer in range(DEPTH):
                L = f"l{layer}"
                ns = 2 if layer == 0 else 1
                later, v = None, 0
                for t in FIRST1:
                    both = layer == 0 or t in (KK, VV)
                    n = 512 if both else 256
                    bank = lin_bank((L, t))
                    product(bank[:, 0:n], (lambda k: H[:, 0:2, k, :]) if both else (lambda k: H[:, 0, k, :]),
                            (lambda k: pe.wait_ge(shifted[L], k + 1 + (k + 1) * (1 - layer))) if t == 0 else
                            (lambda k: pe.wait_ge(shifted[L], KT + k + 1)) if layer == 1 and t == KK else None).then_inc(lin_ready, 1)
                    if later:
                        later()
                        later = None
                    if layer == 0 and t == KK:
                        pe.wait_ge(consts_in, 3 * 16)
                    if t == KK or QQ <= t < FU:
                        later = lambda t=t: rotate((L, t), P1[:, t, 0, :], turn[L, t])
                    elif t == VV or FU <= t < GA:
                        later = lambda t=t, v=v: turn_tile((L, t), turn[L, t], v, 4 if t == VV else ns * TT)
                        v += 1
                n = ns * SEQ
                pe.wait_ge(conv_done, layer + 1)
                bank = aux_bank((L, "mean"))
                for t in range(2):
                    m = mm(bank[:, 0:n], t0("ones_c"), CV[:, t, 0:ns, :], start=t == 0, stop=t == 1)
                m.then_inc(aux_ready, 1)
                pe.wait_ge(aux_taken, turn["turn", (L, FU + 1)] + 1)
                for s in range(ns):
                    for f in range(2):
                        bank = aux_bank((L, "dft", s, f))
                        for t in range(TT):
                            m = mm(bank[:, :], FT[:, s * TT + t, f * P:(f + 1) * P], t1(f"dft{t}"), start=t == 0, stop=t == 1)
                        m.then_inc(aux_ready, 1)
                pe.wait_ge(conv_sq, layer + 1)
                bank = lin_bank((L, "var"))
                for t in range(2):
                    m = mm(bank[:, 0:n], t0("ones_c"), SQ[:, t, 0:n], start=t == 0, stop=t == 1)
                m.then_inc(lin_ready, 1)
                for f in range(2):
                    pe.wait_ge(aux_taken, turn[L, "dft", ns - 1, f] + 1)
                    bank = aux_bank((L, "mix", f))
                    mm(bank[:, 0:n], t1("bc"), CS[:, f, 0:ns, 0:256], start=True, stop=False)
                    mm(bank[:, 0:n], t1("bs"), CS[:, f, 0:ns, 256:512], start=False, stop=True).then_inc(aux_ready, 1)
                pe.wait_ge(aux_taken, turn[L, "mix", 1] + 1)
                for t in range(2):
                    bank = aux_bank((L, "four", t))
                    for f in range(2):
                        m = mm(bank[:, 0:n], wfour[:, layer, f, t * P:(t + 1) * P], FF[:, f, 0:ns, :], start=f == 0, stop=f == 1)
                    m.then_inc(aux_ready, 1)
                pe.wait_ge(roped, 5 * (layer + 1))
                attention(L, lambda i: fill(layer, i))
                projected_out((L, "out"), lambda k: YB[:, k, 0:ns, :], n, lambda n: pe.wait_ge(gated, KT * layer + n + 1),
                              MIX_ORDER, (lambda: mean_square("mem", 1)) if layer == 1 else lambda: None)
                mean_square("l1" if layer == 0 else "fin1", 2 - layer)

            def memory(t):
                bank = lin_bank(("in2", t))
                product(bank[:, 0:SEQ], lambda k: H[:, 1, k, :],
                        (lambda k: pe.wait_ge(normed["mem"], k + 1)) if t == MK else None).then_inc(lin_ready, 1)

            memory(MK)
            memory(MK + 1)
            memory(MK + 2)
            mean_square("mix", 1)
            memory(MK + 3)

            later, v, ropes = None, 0, 5 * DEPTH
            for t in [MV, MV + 1, MV + 2, MV + 3] + list(range(IN2)):
                if t >= MV:
                    memory(t)
                else:
                    bank = lin_bank(("in2", t))
                    product(bank[:, 0:SEQ], lambda k: H[:, 0, k, :],
                            (lambda k: pe.wait_ge(normed["mix"], k + 1)) if t == 0 else None).then_inc(lin_ready, 1)
                if later:
                    later()
                    later = None
                if t == 0:
                    pe.wait_ge(c2_in_s, 16)
                if t == AV or BV <= t < MQ or t >= MV:
                    later = lambda t=t, v=v: turn_tile(("in2", t), turn["in2", t], v, TT)
                    v += 1
                elif t < MQ:
                    later = lambda t=t: rotate(("in2", t), PR[:, AT[t], :], turn["in2", t])
                    ropes += 1
                if t == BQ:
                    bank = aux_bank("iw")
                    for tt in range(TT):
                        for k in range(KT):
                            m = mm(bank[:, 4 * tt:4 * tt + 4], H[:, 0, k, tt * P:(tt + 1) * P], wsmall[:, k, 20:24],
                                   start=k == 0, stop=k == KT - 1)
                    m.then_inc(aux_ready, 1)
                if t == BQ + 2:
                    pe.wait_ge(roped, 5 * DEPTH + 8)
                    for tt in range(TT):
                        s, w = IDX_TURN + tt, P * (tt + 1)
                        pe.wait_ge(scores_taken, s - 1)
                        for h in range(4):
                            r = slice(h % 2 * HD, h % 2 * HD + HD)
                            a = h % 2 * 512 + h // 2 * w
                            m = mm(sc[:, s % 2, a:a + w], PR[r, AT[IQ] + h // 2, tt * P:(tt + 1) * P],
                                   PR[r, AT[IK], 0:w], start=True, stop=True, skip_group_check=True)
                        m.then_inc(scores_ready, 1)
            pe.wait_ge(roped, ropes)
            pe.wait_ge(aux_taken, turn["turn", ("in2", MQ - 1)] + 1)
            pe.wait_ge(idx_mask, 1)

            def gate(t, b):
                bank = lin_bank(("gate", t, b))
                product(bank[:, 0:SEQ], lambda k: H[:, 0, k, :]).then_inc(lin_ready, 1)

            attention("abm", lambda i: gate(*divmod(GATE_STEPS.index(i), 3)) if i in GATE_STEPS else None)
            for mp in range(4):
                for t in (2 * mp, 2 * mp + 1) if mp else ():
                    for b in range(3):
                        gate(t, b)
                if mp == 0:
                    attended("abm")
                for b in range(3):
                    w = block_of_weights()
                    for i in range(2):
                        bank = aux_bank(("branch", 2 * mp + i, b))
                        for k in range(4):
                            m = mm(bank[:, 0:SEQ], w[:, 4 * i + k, :], Y[:, 4 * b + k, :], start=k == 0, stop=k == 3)
                            if k < 3:
                                frees(m)
                        m.then_inc(aux_ready, 1)
            projected_out(("out2",), lambda k: H[:, 1, k, :], SEQ, lambda n: pe.wait_ge(merged, n + 1))
            mean_square("ffn", 1)
            at["owed"] = 1
            bank = aux_bank("logits")
            for k in range(KT):
                pe.wait_ge(normed["ffn"], k + 1)
                m = mm(bank[0:20, 0:SEQ], wsmall[:, k, 0:20], H[:, 0, k, :], start=k == 0, stop=k == KT - 1)
                if k == 0:
                    frees(m)
            m.then_inc(aux_ready, 1)
            pe.wait_ge(aux_taken, turn["logits"] + 1)
            bank = aux_bank("route")
            for tt in range(TT):
                m = tr(bank[:, 20 * tt:20 * tt + 20], RT[0:20, 0, tt * P:(tt + 1) * P], t0("ident")[0:20, 0:20])
            m.then_inc(aux_ready, 1)
            for tt in range(TT):
                for half in range(2):
                    bank = lin_bank()
                    for k in range(4):
                        m = tr(bank[:, k * P:(k + 1) * P], H[:, 0, 4 * half + k, tt * P:(tt + 1) * P], t0("ident"))
                    m.then_inc(lin_ready, 1)
            pe.wait_ge(places_from, 1)
            bank = aux_bank("places")
            one, before = t0("tri")[:, P:2 * P], t0("tri")[:, 0:P]
            mm(bank[:, 0:16], before, MK1[:, 0, :], start=True, stop=True)
            mm(bank[:, 16:32], before, MK1[:, 1, :], start=True, stop=False)
            mm(bank[:, 16:32], one, MK1[:, 0, :], start=False, stop=True)
            mm(bank[:, 32:48], one, MK1[:, 0, :], start=True, stop=False)
            mm(bank[:, 32:48], one, MK1[:, 1, :], start=False, stop=True).then_inc(aux_ready, 1)

            def gather(halves=(0, 1)):
                for half in halves:
                    for k in range(4):
                        for tt in range(TT):
                            a = 4 * half + k
                            m = mm(sc[:, 0, a * P:(a + 1) * P], TK[:, tt, a * P:(a + 1) * P], SEL[:, tt, :],
                                   start=tt == 0, stop=tt == TT - 1)
                    m.then_inc(e_gathered, 1)

            def scatter(i):
                pe.wait_ge(e_y_lo, i + 1)
                pe.wait_ge(e_y_hi, i + 1)
                pe.wait_ge(e_swt_in, i + 1)
                for q in range(4):
                    if q >= 2:
                        pe.wait_ge(e_added, 4 * i + q - 1)
                    for b in range(2):
                        a = 2 * q + b
                        m = mm(sc[:, 1, q % 2 * 512 + b * SEQ:q % 2 * 512 + (b + 1) * SEQ], YS[:, a * P:(a + 1) * P], SWT,
                               start=True, stop=True)
                    m.then_inc(e_out, 1)

            pe.wait_ge(e_sel, 1)
            gather()
            pe.wait_ge(aux_taken, at["aux"])
            pe.wait_ge(lin_taken, at["lin"])
            assert at["owed"] == 0

            def experts(i):
                ringed = RINGED[i] if isinstance(i, int) else RINGED[2]

                def unit(j):
                    if j >= ringed:
                        if isinstance(i, int):
                            n, rounds = j - ringed + SLOTS * i, 1
                        else:
                            n, rounds = j - ringed, i
                        pe.wait_ge(aside_in[n // 2], rounds * 2 * 16)
                        return ASIDE[n].rearrange("p (k n) -> p k n", n=512)
                    slot = (BASE + j) % SLOTS
                    rounds = (BASE + j % SLOTS) // SLOTS + 1 + i
                    if isinstance(i, int):
                        rounds += j // SLOTS
                    elif j < RINGED[1] - SLOTS:
                        rounds += 1
                    pe.wait_ge(unit_in[slot], 16 * rounds)
                    return ring[:, slot, :, :].rearrange("p b (k n) -> p (b k) n", n=512)

                def both(bank, left, n_k, j0, done):
                    for half in range(n_k // 4):
                        w = [unit(j0 + 2 * half + x) for x in range(2)]
                        for k in range(4):
                            for x in range(2):
                                c = slice(x * CAP, (x + 1) * CAP)
                                last = 4 * half + k == n_k - 1
                                m = mm(bank[c, :], left[:, 4 * half + k, c], w[x][:, k, :], start=half + k == 0, stop=last)
                                if k == 3 and not (last and x == 1):
                                    m.then_inc(unit_free, 1)
                                elif k < 3:
                                    frees(m)
                    at["owed"] += 1
                    m.then_inc(done, 1)

                for half in range(2):
                    pe.wait_ge(e_te_in, 2 * i + half + 1)
                both(lin[0], TE, KT, 0, e_first)
                scatter(i)
                both(lin[1], TE, KT, 4, e_third)
                pe.wait_ge(e_sel, i + 2)
                gather([0])
                pe.wait_ge(e_hidden, i + 1)
                for k in range(4):
                    m = tr(aux[0][:, k * P:(k + 1) * P], HS[:, k * P:(k + 1) * P], t0("ident"))
                m.then_inc(e_turned, 1)
                gather([1])
                pe.wait_ge(e_hid_in, i + 1)
                both(aux[1], HT, 4, 8, e_y)
                both(aux[0], HT, 4, 10, e_y)
                pe.wait_ge(e_sw, i + 1)
                pe.wait_ge(e_added, 4 * i + 4)
                for tt in range(TT):
                    m = tr(sc[:, 1, 512 + tt * P:512 + (tt + 1) * P], SW[:, tt, :], t0("ident"))
                    if tt == 0:
                        frees(m)
                m.then_inc(e_swt, 1)
                assert at["owed"] == 0

            experts(0)
            experts(1)
            pe.wait_ge(pairs_in, 1)
            n_pairs = pe.value_load(NP[0:1, 0:1], min_val=PAIRS, max_val=PAIRS * PASSES)
            with pe.Fori(2, n_pairs) as i:
                experts(i)
            scatter(n_pairs)
            bank = lin[0]
            turn["fin2"] = at["lin"]
            pe.wait_ge(sq_added, (KT - 1) * (at["sq"] + 1))
            mm(bank[:, 0:SEQ], t0("ones_d"), SA[:, 0:SEQ], start=True, stop=True).then_inc(lin_ready, 1)

        @block.sync
        def _(sp):
            def load(u, slot):
                src = w_stream[u] if isinstance(u, int) else w_stream[bass.ds(u, 1)].rearrange("u p b n -> (u p) b n")
                sp.dma_start(ring[:, slot, :, :], src).then_inc(unit_in[slot], 16)

            head = BASE + SLOTS
            for slot in range(SLOTS):
                load(slot, slot)
            sp.dma_start(X[:, :, :, :], x_in).then_inc(x_in_s, 16)
            with sp.Fori(1, head // SLOTS) as r:
                for slot in range(SLOTS):
                    sp.wait_ge(unit_free, SLOTS * r + slot - SLOTS + 1)
                    load(SLOTS * r + slot, slot)
            def load_expert(i, j, n=None):
                u = BASE + PAIR_UNITS * i + j
                if n is None:
                    load(u, (BASE + j) % SLOTS)
                else:
                    src = w_stream[u] if isinstance(u, int) else w_stream[bass.ds(u, 1)].rearrange("u p b n -> (u p) b n")
                    sp.dma_start(ASIDE[n].rearrange("p (b n) -> p b n", b=UNIT), src).then_inc(aside_in[n // 2], 16)

            def used(i, j):
                sp.wait_ge(unit_free, BASE + PAIR_UNITS * i + j + 1)

            sp.wait_ge(aux_ready, turn["branch", KT - 1, 2] + 1)
            for n in (2, 3):
                load_expert(0, SLOTS + n, n)
            for u in range(head // SLOTS * SLOTS, head):
                sp.wait_ge(unit_free, u - SLOTS + 1)
                load(u, u % SLOTS)
            sp.wait_ge(aux_ready, turn["out2", KT - 1] + 1)
            load_expert(1, RINGED[1] + 3, SLOTS + 3)
            for j in range(SLOTS):
                used(0, j)
                load_expert(1, j)
            for j in (6, 7):
                used(0, j)
                load_expert(2, j, j - SLOTS)
            for j in (6, 7):
                used(1, j - SLOTS)
                load_expert(1, j)
            for j in range(8, PAIR_UNITS):
                used(0, j)
                load_expert(2, j, j - SLOTS)
            for j in range(SLOTS):
                used(1, j + SLOTS if j < 2 else j)
                load_expert(2, j)

            def load_pair(i, source):
                for j in range(PAIR_UNITS):
                    used(i - 1, j)
                    load_expert(source, j, j - SLOTS if j >= SLOTS else None)

            with sp.Fori(3, PAIRS) as i:
                load_pair(i, i)
            sp.wait_ge(pairs_in, 1)
            n_pairs = sp.value_load(NP[0:1, 0:1], min_val=PAIRS, max_val=PAIRS * PASSES)
            with sp.If(n_pairs > PAIRS):
                with sp.Fori(PAIRS, n_pairs) as i:
                    load_pair(i, i % PAIRS)
            for half in (slice(0, 4), slice(4, KT)):
                sp.wait_ge(normed["fin2"], half.stop)
                sp.dma_start(out[:, half, :], H[:, 0, half, :]).then_inc(out_s, 16)
            sp.wait_ge(out_s, 2 * 16)

        @block.scalar
        def _(act):
            fn = nc.scalar.activation
            at = {"lin": 0, "sq": 0}

            def take():
                n = at["lin"]
                at["lin"] += 1
                act.wait_ge(lin_ready, n + 1)
                return lin[n % 2]

            def warm_up(f):
                fn(warm[:, :], col("eps"), f)

            def squares(name, src, ns, ready, between={}):
                warm_up(ACT.Sqrt)
                for k in range(KT):
                    ready(k)
                    if k in between:
                        between[k]()
                    if k >= 2:
                        act.wait_ge(sq_added, (KT - 1) * at["sq"] + max(1, k - 2))
                    fn(SQ[:, k % 2, 0:ns * SEQ], src(k), ACT.Square).then_inc(sq_ready, 1)
                if KT in between:
                    between[KT]()
                at["sq"] += 1
                fn(RS[:, 0:ns * SEQ], take()[:, 0:ns * SEQ], ACT.Sqrt, bias=col("eps")).then_inc(lin_taken, 1)

            def attention(name, between):
                items = STAGES[name]
                sinks = sum(x["sink"] is not None for n_, its in STAGES.items() for x in its if first[n_] < first[name])
                for i in range(len(items) + 2):
                    if i >= 2:
                        it, g = items[i - 2], first[name] + i - 2
                        if g >= 3:
                            act.wait_ge(aux_ready, V_TURN[g - 3] + 1)
                        for a in range(0, it["w"], 512):
                            b = min(a + 512, it["w"])
                            fn(PT[:, g % 3, a:b], take()[:, 0:b - a], ACT.Copy).then_inc(lin_taken, 1)
                    if i < len(items):
                        it, g = items[i], first[name] + i
                        act.wait_ge(bias_ready, g + 1)
                        lo = 1
                        if it["sink"] is not None:
                            sinks += 1
                            act.wait_ge(sink_in, sinks)
                            lo = 0
                        p = S[:, g % 3, lo:1 + it["w"]]
                        fn(p, p, ACT.Exp, bias=ST[:, g % 4, 1:2], scale=it["scale"],
                           accum_out=ST[:, g % 4, 2:3]).then_inc(probs_ready, 1)
                    between(i)

            def fill(layer, i):
                t, k = divmod((i + 1) * PER_STEP[layer], KT)
                if k == 0 and t <= GATES:
                    act.wait_ge(fill_ready, GATES * layer + t)
                    fn(P1[:, GA + t - 1, 0:2 - layer, :], sc[:, (t - 1) % 2, 512:512 + (2 - layer) * SEQ],
                       ACT.Copy).then_inc(fill_taken, 1)
                if layer == 0 and i in ADA_STEPS:
                    ada_rows(SQ, ADA_STEPS.index(i))
                if layer == 0 and i == ADA_STEPS[1] + 3:
                    ada_turned(1)

            act.dma_start(cols[:, :], cols_in).then_inc(cols_in_s, 16)
            act.dma_start(c0[:, :], c0_in).then_inc(c0_in_s, 16)
            act.wait_ge(cols_in_s, 16)
            fn(SC.rearrange("p k s -> p (k s)"), col("c", 0, 16), ACT.Silu).then_inc(silu_c, 1)

            def ada_rows(rows, r):
                bank = take()
                for j in range(3):
                    q = slice(32 * j, 32 * j + 2)
                    m = fn(rows[q, r, 0:512], bank[q, :], ACT.Copy)
                m.then_inc(lin_taken, 1)

            def ada_turned(layer):
                fn(MOD[:, layer, :, :].rearrange("p t s -> p (t s)"), take()[:, 0:2 * ADA], ACT.Copy).then_inc(lin_taken, 1)

            for layer in range(DEPTH):
                L = f"l{layer}"
                ns = 2 if layer == 0 else 1
                last = (lambda k: None) if layer == 0 else (lambda k: act.wait_ge(aux_taken, turn["l0", "out", k] + 1))
                if layer == 0:
                    ada_rows(S[:, :, 1:513], 0)
                    act.wait_ge(x_in_s, 16)
                squares(L, lambda k: X[:, 0:2, k, :], 2, last)
                if layer == 0:
                    ada_rows(S[:, :, 1:513], 1)
                    ada_turned(0)
                    act.dma_start(cb[:, :], c1_in).then_inc(consts_in, 16)
                    act.dma_start(wfour[:, :, :, :], wfour_in).then_inc(consts_in, 16)
                    act.dma_start(wsmall[:, :, :], wsmall_in).then_inc(consts_in, 16)
                act.wait_ge(gains_ready, layer + 1)
                for i, (k, s) in enumerate((k, s) for streams in NORM_ORDER[layer] for k in range(KT) for s in streams):
                    act.wait_ge(normed[L], i + 1)
                    fn(H[:, s, k, :], H[:, s, k, :], ACT.Identity, bias=MOD[:, layer, k, s:s + 1],
                       scale=GS[:, k, s:s + 1]).then_inc(shifted[L], 1)
                if layer == 1:
                    act.dma_start(X[:, 1, :, :], mem_in).then_inc(mem_in_s, 16)
                v = 0
                for t in FIRST1:
                    n = 2 if layer == 0 or t in (KK, VV) else 1
                    bank = take()[:, 0:n * SEQ]
                    if t == VV or FU <= t < GA:
                        if v >= 2:
                            act.wait_ge(aux_ready, turn["turn", (L, FU + v - 3 if v > 2 else VV)] + 1)
                        fn(SQ[:, v % 2, 0:n * SEQ], bank, ACT.Copy).then_inc(lin_taken, 1)
                        v += 1
                    else:
                        f = ACT.Sigmoid if t < CA else ACT.Copy
                        fn(P1[:, t, 0:n, :], bank, f).then_inc(lin_taken, 1)
                n = ns * SEQ
                warm_up(ACT.Sqrt)
                fn(RS[:, 0:n], take()[:, 0:n], ACT.Sqrt, bias=col("eps")).then_inc(lin_taken, 1)
                act.wait_ge(conv_norm, layer + 1)
                for t in range(2):
                    v_ = CV[:, t, 0:ns, :]
                    fn(v_, v_, ACT.Silu, bias=col(f"ln_b{layer}", t), scale=col(f"ln_g{layer}", t)).then_inc(conv_act, 1)
                attention(L, lambda i: fill(layer, i))
                act.wait_ge(fill_taken, GATES * (layer + 1))
                for k in MIX_ORDER:
                    g = P1[:, GA + k, 0:ns, :]
                    fn(g, g, ACT.Silu).then_inc(gates_act, 1)
            squares("mem", lambda k: X[:, 1, k, :], 1, lambda k: act.wait_ge(mem_in_s, 16))

            def memory_keys(n):
                for _ in range(n):
                    fn(PR[:, AT[next(keys)], :], take()[:, 0:SEQ], ACT.Copy).then_inc(lin_taken, 1)

            keys = iter(range(MK, MV))
            squares("fin1", lambda k: X[:, 0, k, :], 1, lambda k: act.wait_ge(aux_taken, turn["l1", "out", k] + 1))
            act.dma_start(cb[:, 0:N_C2], c2_in).then_inc(c2_in_s, 16)
            squares("mix", lambda k: X[:, 0, k, :], 1, lambda k: act.wait_ge(normed["fin1"], k + 1),
                    {2: lambda: memory_keys(1), KT: lambda: memory_keys(2)})
            memory_keys(1)
            v = 0
            turned = list(range(MV, MV + 4)) + [AV] + list(range(BV, MQ))
            for t in list(range(MV, MV + 4)) + list(range(IN2)):
                bank = take()[:, 0:SEQ]
                if t in turned:
                    if v >= 2:
                        act.wait_ge(aux_ready, turn["turn", ("in2", turned[v - 2])] + 1)
                    fn(SQ[:, v % 2, 0:SEQ], bank, ACT.Copy).then_inc(lin_taken, 1)
                    v += 1
                else:
                    fn(PR[:, AT[t], :], bank, ACT.Copy).then_inc(lin_taken, 1)
            attention("abm", lambda i: fn(GT(*divmod(GATE_STEPS.index(i), 3)), take()[:, 0:SEQ], ACT.Copy).then_inc(lin_taken, 1)
                      if i in GATE_STEPS else None)
            act.wait_ge(aux_ready, V_TURN[first["abm"] + len(STAGES["abm"]) - 1] + 1)
            for n in (0, 1, 4, 5, 6, 7, 8):
                u = BASE + SLOTS + n if n < SLOTS else BASE + PAIR_UNITS + RINGED[1] + n - SLOTS
                act.dma_start(ASIDE[n], w_stream[u].rearrange("p b n -> p (b n)")).then_inc(aside_in[n // 2], 16)
            act.wait_ge(lin_taken, turn["gate", 1, 2] + 1)
            for t in range(KT):
                for b in range(3):
                    g = GT(t, b)
                    if t < 2:
                        fn(g, g, ACT.Sigmoid, bias=col("b_gate", b * KT + t)).then_inc(gates_in, 1)
                    else:
                        fn(g, take()[:, 0:SEQ], ACT.Sigmoid, bias=col("b_gate", b * KT + t)).then_inc(lin_taken, 1)
            squares("ffn", lambda k: X[:, 0, k, :], 1, lambda k: act.wait_ge(aux_taken, turn["out2", k] + 1))
            warm_up(ACT.Exp)
            for tt in range(TT):
                for half in range(2):
                    fn(TK[:, tt, 512 * half:512 * half + 512], take()[:, :], ACT.Copy).then_inc(lin_taken, 1)
            act.wait_ge(route_a, 1)
            fn(RF["e"], RF["d"], ACT.Exp).then_inc(route_b, 1)
            act.wait_ge(pairs_in, 1)
            n_pairs = act.value_load(NP[0:1, 0:1], min_val=PAIRS, max_val=PAIRS * PASSES)

            def gathered(n, halves=(0, 1)):
                for half in halves:
                    act.wait_ge(e_gathered, 2 * n + half + 1)
                    fn(TE[:, 4 * half:4 * half + 4, :].rearrange("p k n -> p (k n)"), sc[:, 0, half * 512:(half + 1) * 512],
                       ACT.Copy).then_inc(e_te_in, 1)

            gathered(0)
            with act.Fori(0, n_pairs) as i:
                act.wait_ge(e_first, i + 1)
                fn(SG, lin[0][:, :], ACT.Silu).then_inc(e_silu, 1)
                gathered(i + 1, [0])
                act.wait_ge(e_turned, i + 1)
                fn(HT.rearrange("p k n -> p (k n)"), aux[0][:, :], ACT.Copy).then_inc(e_hid_in, 1)
                gathered(i + 1, [1])
                act.wait_ge(e_y, 2 * i + 1)
                fn(YS[:, 0:512], aux[1][:, :], ACT.Copy).then_inc(e_y_lo, 1)
            for k in range(KT):
                if k % 2 == 0:
                    act.wait_ge(e_added, 4 * n_pairs + k // 2 + 1)
                if k >= 2:
                    act.wait_ge(sq_added, (KT - 1) * at["sq"] + max(1, k - 2))
                fn(SQ[:, k % 2, 0:SEQ], X[:, 0, k, :], ACT.Square).then_inc(sq_ready, 1)
            act.wait_ge(lin_ready, at["lin"] + 1)
            fn(RS[:, 0:SEQ], lin[0][:, 0:SEQ], ACT.Sqrt, bias=col("eps")).then_inc(lin_taken, 1)

        @block.gpsimd
        def _(pool):
            nc.gpsimd.memset(U[:, :, :, 0:PAD], 0.0)
            nc.gpsimd.memset(U[:, :, :, PAD + SEQ:], 0.0).then_inc(pads_ready, 1)
            pool.wait_ge(sinks_ready, 1)
            n = 0
            for name in ("l0", "l1"):
                for i, it in enumerate(STAGES[name]):
                    g = first[name] + i
                    if g >= 3:
                        pool.wait_ge(probs_ready, g - 2)
                    nc.gpsimd.tensor_copy(S[:, g % 3, 0:1], SK[:, it["sink"]:it["sink"] + 1]).then_inc(sink_in, 1)

        @block.vector
        def _(dve):
            v = nc.vector
            at = {"aux": 0, "step": 0, "sq": 0}

            def step(ins):
                at["step"] += 1
                ins.then_inc(dve_step, 1)
                return at["step"]

            def after(n):
                dve.wait_ge(dve_step, n)

            def take(key=None):
                n = at["aux"]
                assert key is None or turn[key] == n, (key, turn[key], n)
                at["aux"] += 1
                dve.wait_ge(aux_ready, n + 1)
                return aux[n % 2]

            def add_squares(ks, ns):
                for k in ks:
                    if k < 1:
                        continue
                    n = (KT - 1) * at["sq"] + k
                    dve.wait_ge(sq_ready, KT * at["sq"] + k + 1)
                    if k > 1:
                        dve.wait_ge(sq_added, n - 1)
                    c = slice(0, ns * SEQ)
                    v.tensor_tensor(SA[:, c], SA[:, c] if k > 1 else SQ[:, 0, c], SQ[:, k % 2, c], ALU.add).then_inc(sq_added, 1)
                    if k == KT - 1:
                        at["sq"] += 1

            def norm(name, src, dst, gain, each=lambda k: None):
                dve.wait_ge(lin_taken, turn[name] + 1)
                after(step(v.reciprocal(RI[:, 0:SEQ], RS[:, 0:SEQ])))
                for k in range(KT):
                    v.scalar_tensor_tensor(out=dst[:, k, :], in0=src[:, k, :], scalar=col(gain, k), in1=RI[:, 0:SEQ],
                                           op0=ALU.mult, op1=ALU.mult).then_inc(normed[name], 1)
                    each(k)
                dve.wait_ge(normed[name], KT)

            def norm_both(layer):
                L = f"l{layer}"
                dve.wait_ge(lin_taken, turn[L] + 1)
                for streams in NORM_ORDER[layer]:
                    c = slice(streams[0] * SEQ, (streams[-1] + 1) * SEQ)
                    after(step(v.reciprocal(RI[:, c], RS[:, c])))
                    for k in range(KT):
                        for s in streams:
                            v.tensor_tensor(H[:, s, k, :], X[:, s, k, :], RI[:, s * SEQ:(s + 1) * SEQ],
                                            ALU.mult).then_inc(normed[L], 1)
                dve.wait_ge(normed[L], 2 * KT)

            def modulation(layer):
                dve.wait_ge(lin_taken, turn["mod", layer] + 1)
                for s in range(2):
                    n = step(v.tensor_tensor(MOD[:, layer, :, s], MOD[:, layer, :, s], col(f"b_ada{layer}", 0, ADA), ALU.add))
                return n

            def gains(layer, n):
                after(n)
                for s in range(2):
                    n = step(v.scalar_tensor_tensor(out=GS[:, :, s], in0=MOD[:, layer, KT:2 * KT, s], scalar=1.0,
                                                    in1=col(f"norm_g{layer}", 0, KT), op0=ALU.add, op1=ALU.mult))
                after(n)
                v.memset(RO[:, layer:layer + 1], 0.0).then_inc(gains_ready, 1)

            ropes = [0]

            def rope(key, x, cos, sin):
                b = ropes[0] % 2
                ropes[0] += 1
                bank = take(("rot", key))
                v.tensor_tensor(RT[:, b, :], bank[:, 0:SEQ], sin, ALU.mult).then_inc(aux_taken, 1)
                n = step(v.tensor_tensor(x, x, cos, ALU.mult))
                after(n)
                v.tensor_tensor(x, x, RT[:, b, :], ALU.add).then_inc(roped, 1)

            def attention(name):
                items = STAGES[name]
                for i in range(len(items) + 4):
                    if i < len(items):
                        it, s, g = items[i], scored_first[name] + i, first[name] + i
                        if g >= 3:
                            dve.wait_ge(lin_ready, T_LAST[g - 3] + 1)
                        dve.wait_ge(scores_ready, s + 1)
                        w, st = it["w"], ST[:, g % 4, :]
                        most = SK[:, it["sink"]:it["sink"] + 1] if it["sink"] is not None else -3e38
                        v.tensor_tensor_reduce(out=S[:, g % 3, 1:1 + w], in0=sc[:, s % 2, 0:w], in1=it["mask"], scale=1.0,
                                               scalar=most, op0=ALU.add, op1=ALU.max, accum_out=st[:, 0:1]).then_inc(scores_taken, 1)
                        dve.wait_ge(scores_taken, s + 1)
                        v.tensor_scalar(st[:, 1:2], st[:, 0:1], -it["scale"], None, ALU.mult).then_inc(bias_ready, 1)
                    if 1 <= i <= len(items):
                        it, g = items[i - 1], first[name] + i - 1
                        st, p = ST[:, g % 4, :], S[:, g % 3, 1:1 + it["w"]]
                        dve.wait_ge(probs_ready, g + 1)
                        after(step(v.reciprocal(st[:, 3:4], st[:, 2:3])))
                        v.tensor_scalar(p, p, st[:, 3:4], None, ALU.mult).then_inc(probs_scaled, 1)
                    if i >= 5 and i % 2 == 1:
                        it = items[i - 5]
                        out_ = take()[:, 0:it["to"].shape[-1]]
                        v.tensor_copy(it["to"], out_).then_inc(aux_taken, 1)

            dve.wait_ge(cols_in_s, 16)
            v.tensor_scalar(SK[:, :], col("sink", 0, 16), float(HD) ** 0.5, None, ALU.mult).then_inc(sinks_ready, 1)
            for layer in range(DEPTH):
                L = f"l{layer}"
                ns = 2 if layer == 0 else 1
                n = ns * SEQ
                if layer == 0:
                    dve.wait_ge(x_in_s, 16)
                    add_squares(range(KT), 2)
                    norm_both(0)
                    gains(0, modulation(0))
                else:
                    gains(1, n_mod)
                    norm_both(1)

                dve.wait_ge(lin_taken, turn[L, CA + 1] + 1)
                dve.wait_ge(pads_ready, 1)
                last = {}
                for t in range(2):
                    last[t] = step(v.tensor_tensor(U[:, t, 0:ns, PAD:PAD + SEQ], P1[:, CA + t, 0:ns, :], P1[:, CB + t, 0:ns, :], ALU.mult))
                taps = [(k, t) for k in range(CONV_K) for t in range(2)]

                def conv(n_taps):
                    for _ in range(min(n_taps, len(taps))):
                        k, t = taps.pop(0)
                        after(last[t])
                        w, u = col(f"conv_w{layer}", t * CONV_K + k), U[:, t, 0:ns, k:k + SEQ]
                        if k == 0:
                            ins = v.tensor_scalar(CV[:, t, 0:ns, :], u, w, col(f"conv_b{layer}", t), ALU.mult, ALU.add)
                        else:
                            ins = v.scalar_tensor_tensor(out=CV[:, t, 0:ns, :], in0=u, scalar=w, in1=CV[:, t, 0:ns, :],
                                                         op0=ALU.mult, op1=ALU.add)
                        if taps:
                            last[t] = step(ins)
                        else:
                            ins.then_inc(conv_done, 1)

                for t in [KK, VV, QQ, QQ + 1, QQ + 2, QQ + 3, FU, FU + 1]:
                    conv(7)
                    if t == VV:
                        bank = take(("turn", (L, t)))
                        v.tensor_copy(VT.rearrange("p t n -> p (t n)"), bank[:, :]).then_inc(aux_taken, 1)
                    elif t >= FU:
                        bank = take(("turn", (L, t)))
                        v.tensor_copy(FT[:, 0:2 * ns, (t - FU) * P:(t - FU + 1) * P],
                                      bank[:, 0:n].rearrange("p (j n) -> p j n", n=P)).then_inc(aux_taken, 1)
                    else:
                        dve.wait_ge(lin_taken, turn[L, t] + 1)
                        rope((L, t), P1[:, t, 0, :], t1("cos"), t1("sin"))
                conv(len(taps))
                bank = take((L, "mean"))
                for t in range(2):
                    ins = v.tensor_tensor(CV[:, t, 0:ns, :], CV[:, t, 0:ns, :], bank[:, 0:n].rearrange("p (s n) -> p s n", s=ns), ALU.subtract)
                ins.then_inc(aux_taken, 1)
                dve.wait_ge(aux_taken, at["aux"])
                for t in range(2):
                    ins = v.tensor_tensor(SQ[:, t, 0:n].rearrange("p (s n) -> p s n", s=ns), CV[:, t, 0:ns, :], CV[:, t, 0:ns, :], ALU.mult)
                ins.then_inc(conv_sq, 1)
                for s in range(ns):
                    for f in range(2):
                        v.tensor_copy(CS[:, f, s, :], take((L, "dft", s, f))[:, :]).then_inc(aux_taken, 1)
                dve.wait_ge(lin_taken, turn[L, "var"] + 1)
                after(step(v.reciprocal(RI[:, 0:n], RS[:, 0:n])))
                for t in range(2):
                    ins = v.tensor_tensor(CV[:, t, 0:ns, :], CV[:, t, 0:ns, :], RI[:, 0:n].rearrange("p (s n) -> p s n", s=ns), ALU.mult)
                ins.then_inc(conv_norm, 1)
                for f in range(2):
                    v.tensor_copy(FF[:, f, 0:ns, :], take((L, "mix", f))[:, 0:n].rearrange("p (s n) -> p s n", s=ns)).then_inc(aux_taken, 1)
                for t in range(2):
                    bank = take((L, "four", t))
                    v.tensor_scalar(YB[:, 6 + t, 0:ns, :], bank[:, 0:n].rearrange("p (s n) -> p s n", s=ns),
                                    col(f"b_four{layer}", t), None, ALU.add).then_inc(aux_taken, 1)
                attention(L)
                if layer == 0:
                    n_mod = modulation(1)
                dve.wait_ge(aux_taken, at["aux"])
                for n_gate, k in enumerate(MIX_ORDER):
                    dve.wait_ge(gates_act, KT * layer + n_gate + 1)
                    if k in (4, 5):
                        dve.wait_ge(conv_act, 2 * layer + k - 3)
                    branch = CV[:, k - 4, 0:ns, :] if k in (4, 5) else YB[:, k, 0:ns, :]
                    v.tensor_tensor(YB[:, k, 0:ns, :], branch, P1[:, GA + k, 0:ns, :], ALU.mult).then_inc(gated, 1)
                if layer == 1:
                    add_squares(range(KT), 1)
                for t in range(KT):
                    bank = take((L, "out", t))
                    for s in range(ns):
                        ins = v.scalar_tensor_tensor(out=X[:, s, t, :], in0=bank[:, s * SEQ:(s + 1) * SEQ],
                                                     scalar=MOD[:, layer, 2 * KT + t, s:s + 1], in1=X[:, s, t, :],
                                                     op0=ALU.mult, op1=ALU.add)
                    ins.then_inc(aux_taken, 1)
                    add_squares([t - 1], ns)
                    if layer == 1 and t == KT // 2:
                        dve.wait_ge(lin_taken, turn["mem"] + 1)
                        after(step(v.reciprocal(RI[:, 0:SEQ], RS[:, 0:SEQ])))
                    if layer == 1 and t >= KT // 2:
                        for k in (2 * t - KT, 2 * t - KT + 1):
                            v.scalar_tensor_tensor(out=H[:, 1, k, :], in0=X[:, 1, k, :], scalar=col("g_mem", k), in1=RI[:, 0:SEQ],
                                                   op0=ALU.mult, op1=ALU.mult).then_inc(normed["mem"], 1)

                add_squares([KT - 1], ns)

            dve.wait_ge(aux_taken, at["aux"])
            dve.wait_ge(normed["mem"], KT)
            norm("fin1", X[:, 0], X[:, 0], "final_g", lambda k: add_squares([k - 2], 1))
            add_squares([KT - 2, KT - 1], 1)
            norm("mix", X[:, 0], H[:, 0], "g_mix")

            for t in list(range(MV, MV + 4)) + list(range(IN2)):
                key = ("in2", t)
                if t == AV:
                    v.tensor_copy(AVT[:, :, :], take(("turn", key))[:, 0:SEQ].rearrange("p (t n) -> p t n", t=TT)).then_inc(aux_taken, 1)
                elif BV <= t < MQ:
                    v.tensor_copy(BVT[:, :, (t - BV) * P:(t - BV + 1) * P],
                                  take(("turn", key))[:, 0:SEQ].rearrange("p (t n) -> p t n", t=TT)).then_inc(aux_taken, 1)
                elif t >= MV:
                    v.tensor_copy(MVT[:, :, (t - MV) * P:(t - MV + 1) * P],
                                  take(("turn", key))[:, 0:SEQ].rearrange("p (t n) -> p t n", t=TT)).then_inc(aux_taken, 1)
                elif t < MQ:
                    if t == 0:
                        dve.wait_ge(c2_in_s, 16)
                    dve.wait_ge(lin_taken, turn[key] + 1)
                    rope(key, PR[:, AT[t], :], t2("cos"), t2("sin"))
                if t == BQ - 1:
                    v.tensor_copy(IW[:, :, 0:4], take("iw")[:, 0:8].rearrange("p (t n) -> p t n", t=TT)).then_inc(aux_taken, 1)
                    dve.wait_ge(aux_taken, at["aux"])
                if t == BQ + 1:
                    rounds = []
                    for tt in range(TT):
                        s, w = IDX_TURN + tt, P * (tt + 1)
                        dve.wait_ge(scores_ready, s + 1)
                        n = []
                        for h in range(4):
                            a = h % 2 * 512 + h // 2 * w
                            ins = v.tensor_scalar(RL[:, h, 0:w], sc[:, s % 2, a:a + w], 0.0, IW[:, tt, h:h + 1], ALU.max, ALU.mult)
                            n = step(ins) if h < 3 else None
                        ins.then_inc(scores_taken, 1)
                        dve.wait_ge(scores_taken, s + 1)
                        x = DS[:, tt, 0:w]
                        after(step(v.tensor_tensor(x, RL[:, 0, 0:w], RL[:, 1, 0:w], ALU.add)))
                        after(step(v.tensor_tensor(x, x, RL[:, 2, 0:w], ALU.add)))
                        after(step(v.tensor_tensor(x, x, RL[:, 3, 0:w], ALU.add)))
                        after(step(v.tensor_tensor(x, x, t2(f"causal{tt}"), ALU.add)))
                if BQ + 1 <= t < BQ + 1 + TOPK // 8:
                    for tt in range(TT):
                        x = DS[:, tt, 0:P * (tt + 1)]
                        after(step(v.max(M8[:, tt, :], x)))
                        after(step(v.match_replace(x, M8[:, tt, :], x, GONE)))
                if t == BQ + 1 + TOPK // 8:
                    for tt in range(TT):
                        w = P * (tt + 1)
                        after(step(v.tensor_scalar(MA[:, tt, 0:w], DS[:, tt, 0:w], GONE, NEG, ALU.not_equal, ALU.mult)))
                        ins = v.tensor_tensor(MA[:, tt, 0:w], MA[:, tt, 0:w], t2(f"causal{tt}"), ALU.add)
                        if tt == 0:
                            step(ins)
                    ins.then_inc(idx_mask, 1)
                    dve.wait_ge(idx_mask, 1)

            attention("abm")
            for mp in range(4):
                for b in range(3):
                    for t in (2 * mp, 2 * mp + 1):
                        if mp:
                            dve.wait_ge(lin_taken, turn["gate", t, b] + 1)
                        else:
                            dve.wait_ge(gates_in, 3 * t + b + 1)
                        g = GT(t, b)
                        v.tensor_tensor(g, take(("branch", t, b))[:, 0:SEQ], g, ALU.mult).then_inc(aux_taken, 1)
                dve.wait_ge(aux_taken, at["aux"])
                for t in (2 * mp, 2 * mp + 1):
                    n = step(v.tensor_tensor(GT(t, 0), GT(t, 0), GT(t, 1), ALU.add))
                after(n)
                for t in (2 * mp, 2 * mp + 1):
                    v.tensor_tensor(H[:, 1, t, :], GT(t, 0), GT(t, 2), ALU.add).then_inc(merged, 1)
            def link(ins):
                after(step(ins))

            step(v.memset(PX[:, :, :], -1.0))
            link(v.memset(CX[:, :, :], 0.0))
            v.memset(SWT, 0.0).then_inc(e_swt_in, 1)
            v.memset(YS[:, 0:512], 0.0).then_inc(e_y_lo, 1)
            v.memset(YS[:, 512:1024], 0.0).then_inc(e_y_hi, 1)
            for t in range(KT):
                v.tensor_tensor(X[:, 0, t, :], take(("out2", t))[:, 0:SEQ], X[:, 0, t, :], ALU.add).then_inc(aux_taken, 1)
                add_squares([t - 1], 1)
            add_squares([KT - 1], 1)
            dve.wait_ge(aux_taken, at["aux"])
            norm("ffn", X[:, 0], H[:, 0], "g_ffn")

            v.tensor_copy(RT[0:20, 0, :], take("logits")[0:20, 0:SEQ]).then_inc(aux_taken, 1)

            v.tensor_tensor(RF["logits"], take("route")[:, 0:40].rearrange("p (t n) -> p t n", t=TT),
                            col("b_route", 0, 40).rearrange("p (t n) -> p t n", t=TT), ALU.add).then_inc(aux_taken, 1)
            dve.wait_ge(aux_taken, at["aux"])
            four = [P, TT, 4]

            def first_max(out_, x, top):
                link(v.tensor_reduce(top, x, AX.X, ALU.max))
                link(v.tensor_tensor(RF["is_max"], x, top.broadcast_to(four), ALU.is_ge))
                flat = "p t n -> p (t n)"
                link(v.tensor_tensor_scan(RF["count"].rearrange(flat), t0("restart"), RF["is_max"].rearrange(flat), 0.0,
                                          ALU.mult, ALU.add))
                link(v.scalar_tensor_tensor(out=out_, in0=RF["count"], scalar=1.0, in1=RF["is_max"], op0=ALU.is_le, op1=ALU.mult))

            groups = RF["logits"][:, :, 0:4]
            subs = RF["logits"][:, :, 4:20].rearrange("p t (g e) -> p t g e", g=4)
            first_max(RF["group"], groups, RF["top_g"])
            step(v.tensor_tensor(RF["d"][:, :, 0:4], groups, RF["top_g"].broadcast_to(four), ALU.subtract))
            link(v.tensor_tensor(RF["of_group"], subs, RF["group"].rearrange("p t (g o) -> p t g o", o=1).broadcast_to([P, TT, 4, 4]),
                                 ALU.mult))
            link(v.tensor_reduce(RF["sub"], RF["of_group"].rearrange("p t g e -> p t e g"), AX.X, ALU.add))
            first_max(RF["first"], RF["sub"], RF["top_1"])
            link(v.scalar_tensor_tensor(out=RF["rest"], in0=RF["first"], scalar=NEG, in1=RF["sub"], op0=ALU.mult, op1=ALU.add))
            first_max(RF["second"], RF["rest"], RF["top_2"])
            v.tensor_tensor(RF["d"][:, :, 4:5], RF["top_2"], RF["top_1"], ALU.subtract).then_inc(route_a, 1)
            dve.wait_ge(route_b, 1)
            e2 = RF["e"][:, :, 4:5]
            link(v.tensor_reduce(RF["sum"], RF["e"][:, :, 0:4], AX.X, ALU.add))
            link(v.scalar_tensor_tensor(out=RF["sum"], in0=e2, scalar=1.0, in1=RF["sum"], op0=ALU.add, op1=ALU.mult))
            link(v.reciprocal(RF["w1"], RF["sum"]))
            step(v.tensor_tensor(RF["first"], RF["first"], RF["w1"].broadcast_to(four), ALU.mult))
            link(v.tensor_tensor(RF["w2"], RF["w1"], e2, ALU.mult))
            link(v.tensor_tensor(RF["second"], RF["second"], RF["w2"].broadcast_to(four), ALU.mult))
            link(v.tensor_tensor(RF["first"], RF["first"], RF["second"], ALU.add))
            link(v.tensor_tensor(CM.rearrange("p t (g e) -> p t g e", g=4),
                                 RF["group"].rearrange("p t (g o) -> p t g o", o=1).broadcast_to([P, TT, 4, 4]),
                                 RF["first"].rearrange("p t (o e) -> p t o e", o=1).broadcast_to([P, TT, 4, 4]), ALU.mult))

            v.tensor_scalar(MK1.rearrange("p t n -> p (t n)"), CM.rearrange("p t n -> p (t n)"), 0.0, None,
                            ALU.is_gt).then_inc(places_from, 1)
            bank = take("places")
            dve.wait_ge(places_from, 1)
            step(v.tensor_reduce(CN[:, 0:1], bank[:, 32:48], AX.X, ALU.max))
            v.scalar_tensor_tensor(out=RF["place"], in0=bank[:, 0:32].rearrange("p (t n) -> p t n", t=TT), scalar=1.0,
                                   in1=MK1, op0=ALU.add, op1=ALU.mult).then_inc(aux_taken, 1)
            dve.wait_ge(aux_taken, at["aux"])

            def places(n):
                c = slice(N_EXP * n, N_EXP * (n + 1))
                step(v.tensor_scalar(PX[:, :, c], RF["place"], float(-1 - CAP * n), None, ALU.add))
                link(v.tensor_copy(CX[:, :, c], CM[:, :, :]))

            def slots(dst, n, weight, done):
                for tt in range(TT):
                    for x in range(2):
                        w = CX[:, tt, bass.ds(2 * n + x, 1)] if weight else None
                        ins = v.tensor_scalar(dst[:, tt, x * CAP:(x + 1) * CAP], t0("iota"), PX[:, tt, bass.ds(2 * n + x, 1)], w,
                                              ALU.is_equal, *([ALU.mult] if weight else []))
                ins.then_inc(done, 1)

            places(0)
            slots(SEL, 0, False, e_sel)
            link(v.tensor_scalar(CN[:, 1:PASSES], t0("caps"), CN[:, 0:1], float(PAIRS), ALU.is_lt, ALU.mult))
            link(v.tensor_reduce(CN[:, 4:5], CN[:, 1:PASSES], AX.X, ALU.add))
            v.tensor_scalar(NP[:, :], CN[:, 4:5], float(PAIRS), None, ALU.add).then_inc(pairs_in, 1)
            for n in range(1, PASSES):
                places(n)
            dve.wait_ge(pairs_in, 1)
            n_pairs = dve.value_load(NP[0:1, 0:1], min_val=PAIRS, max_val=PAIRS * PASSES)

            def add_outputs(n, each=lambda q: None):
                for q in range(4):
                    dve.wait_ge(e_out, 4 * n + q + 1)
                    x = X[:, 0, 2 * q:2 * q + 2, :].rearrange("p k n -> p (k n)")
                    v.tensor_tensor(x, sc[:, 1, q % 2 * 512:q % 2 * 512 + 512], x, ALU.add).then_inc(e_added, 1)
                    each(q)

            with dve.Fori(0, n_pairs) as i:
                dve.wait_ge(e_gathered, 2 * i + 2)
                slots(SEL, i + 1, False, e_sel)
                slots(SW, i, True, e_sw)
                add_outputs(i)
                dve.wait_ge(e_silu, i + 1)
                dve.wait_ge(e_third, i + 1)
                v.tensor_tensor(HS, lin[1][:, :], SG, ALU.mult).then_inc(e_hidden, 1)
                dve.wait_ge(e_y, 2 * i + 2)
                v.tensor_copy(YS[:, 512:1024], aux[0][:, :]).then_inc(e_y_hi, 1)
                dve.wait_ge(e_swt, i + 1)
                v.tensor_copy(SWT, sc[:, 1, 512:512 + SEQ]).then_inc(e_swt_in, 1)
                dve.wait_ge(e_added, 4 * i + 4)
            add_outputs(n_pairs, lambda q: add_squares([2 * q - 2, 2 * q - 1], 1))
            add_squares([KT - 2, KT - 1], 1)
            dve.wait_ge(e_added, 4 * n_pairs + 4)
            norm("fin2", X[:, 0], H[:, 0], "g_final")


def tiles_of(w, n):
    return w.reshape(KT, P, n, P).transpose(2, 1, 0, 3).reshape(n, P, KT * P)


def rows_of(w):
    return w.reshape(4, P, 512).transpose(1, 0, 2).reshape(P, 4 * 512)


def ada_of(w):
    return np.stack([rows_of(w[h * 512:(h + 1) * 512, (3 * r + j) * 512:(3 * r + j + 1) * 512])
                     for r in range(2) for h in range(2) for j in range(3)])


def pairs_of(w):
    n = w.shape[1] // 256
    return w.reshape(4, P, n, 2, P).transpose(2, 1, 3, 0, 4).reshape(n, P, KT * P)


def per_feature(v):
    return v.reshape(-1, P).T


def kernel(**inputs):
    import concourse.bacc as bacc
    from concourse.bass_utils import run_bass_kernel_spmd

    a = {k: np.asarray(v) for k, v in inputs.items()}
    grouped = np.concatenate([np.arange(h * HD, h * HD + HD) for t in range(4) for h in (t, t + 4)])
    o = np.cumsum([0, 512, 128, 128, 512, 256, 256, 256, 256, 256])
    q, k, v, ga, ca, cbb, gc, fu, gf = (np.arange(o[i], o[i + 1]) for i in range(9))
    in1 = np.concatenate([cbb, ca, k, v, q[grouped], fu, ga[grouped], gc, gf])
    of_heads = np.concatenate([grouped, np.arange(512, D)])
    o = np.cumsum([0, 512, 128, 128, 256, 64, 4, 1536, 1536, 1536, 512])
    aq, ak, av, iq, ik, iw, bq, bk, bv, mq = (np.arange(o[i], o[i + 1]) for i in range(10))
    in2 = np.concatenate([aq[grouped], ak, av, iq, ik, ik, bq, bk, bv, mq])
    def units(*blocks):
        b = np.concatenate(blocks)
        return b.reshape(len(b) // UNIT, UNIT, P, KT * P).transpose(0, 2, 1, 3).reshape(-1, P, UNIT * KT * P)

    order1 = FIRST1 + list(range(GA, GF))
    w_in_0, w_in_1 = (tiles_of(a["w_in"][l][:, in1], IN1)[order1] for l in range(DEPTH))
    ada_1 = ada_of(a["w_ada"][1])
    cuts = [len(FIRST1) + (i + 1) * PER_STEP[0] // KT for i in ADA_STEPS]
    head = [ada_of(a["w_ada"][0]), units(w_in_0[:cuts[0]]), ada_1[:6], units(w_in_0[cuts[0]:cuts[1]]), ada_1[6:],
            units(w_in_0[cuts[1]:])]
    stream = [tiles_of(a["w_out"][0][of_heads], KT), w_in_1, tiles_of(a["w_out"][1][of_heads], KT),
              tiles_of(a["w_mem_kv_2"][0], 8), tiles_of(a["w_in_2"][0][:, in2], IN2)]
    gates = tiles_of(a["w_gate_2"][0], ADA)
    branches = [pairs_of(a["w_branch_2"][0, b][grouped] if b == 0 else a["w_branch_2"][0, b]) for b in range(3)]
    for mp in range(4):
        stream += [gates[b * KT + t][None] for t in (2 * mp, 2 * mp + 1) for b in range(3)]
        stream += [branches[b][mp][None] for b in range(3)]
    stream.append(tiles_of(a["w_out_2"][0], KT))
    stream.append(np.zeros((PADDED - N_HEAD_BLOCKS, P, KT * P), np.float32))
    tail = []
    for e in range(0, N_EXP, 2):
        for w in (a["w1_2"][0], a["w3_2"][0]):
            tail += [rows_of(w[e + x, h * 512:(h + 1) * 512]) for h in range(2) for x in range(2)]
        tail += [rows_of(a["w2_2"][0, e + x][:, n * 512:(n + 1) * 512]) for n in range(2) for x in range(2)]
    w_stream = np.concatenate(head + [units(*stream), np.stack(tail)]).reshape(N_UNITS, P, UNIT, KT * P)

    cols = np.zeros((P, N_COL), np.float32)

    def put(name, x):
        cols[:, slice(*COL[name])] = x

    put("c", np.stack([per_feature(a["c"][0]), per_feature(a["c_ctx"])], 2).reshape(P, 16))
    for name in ("final_g",):
        put(name, per_feature(a[name]))
    for name, key in (("g_mix", "g_mix_2"), ("g_mem", "g_mem_2"), ("g_ffn", "g_ffn_2"), ("b_gate", "b_gate_2")):
        put(name, per_feature(a[key][0]))
    put("g_final", per_feature(a["g_final_2"]))
    for l in range(DEPTH):
        put(f"b_ada{l}", per_feature(a["b_ada"][l]))
        put(f"norm_g{l}", per_feature(a["norm_g"][l]))
        put(f"conv_w{l}", a["conv_w"][l].T.reshape(2, P, CONV_K).transpose(1, 0, 2).reshape(P, 2 * CONV_K))
        put(f"conv_b{l}", per_feature(a["conv_b"][l]))
        put(f"ln_g{l}", per_feature(a["conv_ln_g"][l]))
        put(f"ln_b{l}", per_feature(a["conv_ln_b"][l]))
        put(f"b_four{l}", per_feature(a["b_four"][l]))
    put("sink", np.broadcast_to(a["attn_sink"].reshape(1, 16), (P, 16)))
    b_route = np.concatenate([a["b_group_2"][0], a["b_sub_2"][0].reshape(16)])
    put("b_route", np.broadcast_to(np.tile(b_route, 2)[None], (P, 40)))
    put("eps", np.full((P, 1), EPS, np.float32))
    x_in = np.stack([a["x"][0], a["ctx"][0]]).transpose(2, 0, 1).reshape(KT, P, 2, SEQ).transpose(1, 2, 0, 3)
    mem_in = a["mem_2"][0].T.reshape(KT, P, SEQ).transpose(1, 0, 2)
    wfour = a["w_four"].reshape(DEPTH, 2, P, 256).transpose(2, 0, 1, 3)
    small = np.concatenate([a["w_group_2"][0], a["w_sub_2"][0].transpose(1, 0, 2).reshape(D, 16), a["w_in_2"][0][:, iw]], 1)
    small = small.reshape(KT, P, 24).transpose(1, 0, 2)
    c0, c1, c2 = constants()

    nc = bacc.Bacc("TRN2", target_bir_lowering=False, num_devices=1)
    arrays, args = {}, []
    for name, x in (("w_stream", w_stream), ("x_in", x_in), ("mem_in", mem_in), ("cols_in", cols), ("wfour_in", wfour),
                    ("wsmall_in", small), ("c0_in", c0), ("c1_in", c1), ("c2_in", c2)):
        arrays[name] = np.ascontiguousarray(x)
        args.append(nc.dram_tensor(name, x.shape, F32, kind="ExternalInput").ap())
    args.append(nc.dram_tensor("out", (P, KT, SEQ), F32, kind="ExternalOutput").ap())
    build(nc, *args)
    r = run_bass_kernel_spmd(nc, [arrays], core_ids=[0])
    y = r.results[0]["out"]
    return y.transpose(2, 1, 0).reshape(1, SEQ, D)
```
